# Optimizing a Trainium2 kernel written in Bass

```python
import math
import jax
import jax.numpy as jnp
from jax import lax
import numpy as np

D_MODEL = 1024
BATCH = 1
SEQ = 256
DEPTH = 2

HEAD_DIM = 64
ROPE_THETA = 10000.0
Q_BLOCK = 128
NSA_HEADS = 8
NSA_KV_HEADS = 2
NSA_GROUP = NSA_HEADS // NSA_KV_HEADS
CMP_BLOCK = 32
CMP_STRIDE = 16
SEL_BLOCK = 64
SEL_TOPK = 8
WINDOW = 256
FOX_HEADS = 8
GDN_HEADS = 8
GDN_HEAD_DIM = 128
GDN_WIDTH = GDN_HEADS * GDN_HEAD_DIM
CONV_WIDTH = 4
GDN_CHUNK = 64
N_GROUPS = 4
EXPERTS_PER_GROUP = 4
N_EXPERTS = N_GROUPS * EXPERTS_PER_GROUP
EXPERT_TOPK = 2
EXPERT_FF = 256

NORM_EPS = 1e-6
NEG_INF = -1e30
FORCE_SCORE = 1e9

NSA_Q_W = NSA_HEADS * HEAD_DIM
NSA_KV_W = NSA_KV_HEADS * HEAD_DIM
NSA_GATE_W = 3 * NSA_HEADS
FOX_W = FOX_HEADS * HEAD_DIM
EVEN_IN_W = NSA_Q_W + 6 * NSA_KV_W + NSA_GATE_W + 3 * FOX_W + FOX_HEADS
EVEN_MIX_W = NSA_Q_W + FOX_W
ODD_IN_W = 4 * GDN_WIDTH + 2 * GDN_HEADS

kernel_name = "hybrid_nsa_fox_gdn_hmoe"

def rms_norm(x, gain):
    xf = x.astype(jnp.float32)
    y = xf * lax.rsqrt(jnp.mean(xf * xf, axis=-1, keepdims=True) + NORM_EPS)
    return (y * gain.astype(jnp.float32)).astype(x.dtype)

def l2_norm(x):
    xf = x.astype(jnp.float32)
    return xf * lax.rsqrt(jnp.sum(xf * xf, axis=-1, keepdims=True) + NORM_EPS)

def rope(x, pos):
    half = x.shape[-1] // 2
    inv_freq = ROPE_THETA ** (-jnp.arange(half, dtype=jnp.float32) / half)
    ang = pos.astype(jnp.float32)[:, None] * inv_freq
    cos = jnp.cos(ang)[:, None, :]
    sin = jnp.sin(ang)[:, None, :]
    xf = x.astype(jnp.float32)
    x1, x2 = xf[..., :half], xf[..., half:]
    return jnp.concatenate([x1 * cos - x2 * sin, x2 * cos + x1 * sin], axis=-1).astype(x.dtype)

def compress_blocks(blk, pe, w1, w2):
    h = blk + pe[None, None, :, None, :]
    h = jnp.einsum('bnlhd,lde->bnhe', h, w1)
    return jnp.einsum('bnhe,ef->bnhf', jax.nn.gelu(h), w2)

def nsa_attention(q, kc_raw, vc_raw, ks, vs, kw, vw, gates, cmp_pe, cmp_w1, cmp_w2, k_gains):
    B, T = q.shape[0], q.shape[1]
    f32 = jnp.float32
    scale = HEAD_DIM ** -0.5
    pos = jnp.arange(T)
    n_q = T // Q_BLOCK
    q_g = q.reshape(B, T, NSA_KV_HEADS, NSA_GROUP, HEAD_DIM)

    n_cmp = (T - CMP_BLOCK) // CMP_STRIDE + 1
    cmp_idx = np.arange(n_cmp)[:, None] * CMP_STRIDE + np.arange(CMP_BLOCK)[None, :]
    cmp_end = cmp_idx[:, -1]
    kc = compress_blocks(kc_raw[:, cmp_idx], cmp_pe[0], cmp_w1[0], cmp_w2[0])
    vc = compress_blocks(vc_raw[:, cmp_idx], cmp_pe[1], cmp_w1[1], cmp_w2[1])
    kc = rope(rms_norm(kc, k_gains[0]), jnp.asarray(cmp_end))
    s_c = jnp.einsum('bthgd,bnhd->bhgtn', q_g, kc).astype(f32) * scale
    valid_c = jnp.asarray(cmp_end[None, :] <= np.arange(T)[:, None])
    p_c = jax.nn.softmax(jnp.where(valid_c, s_c, NEG_INF), axis=-1) * valid_c.astype(f32)
    o_cmp = jnp.einsum('bhgtn,bnhd->bthgd', p_c.astype(vc.dtype), vc)

    n_sel = T // SEL_BLOCK
    k_top = min(SEL_TOPK, n_sel)
    cs = np.arange(n_cmp)[:, None] * CMP_STRIDE
    ss = np.arange(n_sel)[None, :] * SEL_BLOCK
    overlap = np.clip(np.minimum(cs + CMP_BLOCK, ss + SEL_BLOCK) - np.maximum(cs, ss), 0, None)
    overlap = jnp.asarray((overlap / CMP_BLOCK).astype(np.float32))
    imp = jnp.einsum('bhgtn,nj->bhtj', p_c, overlap)
    blk = np.arange(n_sel)[None, :]
    cur = (np.arange(T) // SEL_BLOCK)[:, None]
    forced = jnp.asarray((blk == 0) | (blk == cur) | (blk == cur - 1))
    future = jnp.asarray(blk * SEL_BLOCK > np.arange(T)[:, None])
    imp = jnp.where(forced, FORCE_SCORE, jnp.where(future, NEG_INF, imp))
    _, sel_idx = lax.top_k(imp, k_top)

    ks_blk = rope(rms_norm(ks, k_gains[1]), pos).reshape(B, n_sel, SEL_BLOCK, NSA_KV_HEADS, HEAD_DIM).transpose(0, 3, 1, 2, 4)
    vs_blk = vs.reshape(B, n_sel, SEL_BLOCK, NSA_KV_HEADS, HEAD_DIM).transpose(0, 3, 1, 2, 4)
    q_chunks = q_g.reshape(B, n_q, Q_BLOCK, NSA_KV_HEADS, NSA_GROUP, HEAD_DIM).swapaxes(0, 1)
    idx_chunks = sel_idx.reshape(B, NSA_KV_HEADS, n_q, Q_BLOCK, k_top).transpose(2, 0, 1, 3, 4)
    pos_chunks = pos.reshape(n_q, Q_BLOCK)
    b_ix = jnp.arange(B)[:, None, None, None]
    h_ix = jnp.arange(NSA_KV_HEADS)[None, :, None, None]

    def sel_block(args):
        q_c, idx_c, t_c = args
        k_g = ks_blk[b_ix, h_ix, idx_c]
        v_g = vs_blk[b_ix, h_ix, idx_c]
        s = jnp.einsum('bqhgd,bhqnld->bhgqnl', q_c, k_g).astype(f32) * scale
        key_pos = idx_c[..., None] * SEL_BLOCK + jnp.arange(SEL_BLOCK)
        valid = (key_pos <= t_c[None, None, :, None, None])[:, :, None]
        s = jnp.where(valid, s, NEG_INF).reshape(B, NSA_KV_HEADS, NSA_GROUP, Q_BLOCK, k_top * SEL_BLOCK)
        p = jax.nn.softmax(s, axis=-1).reshape(B, NSA_KV_HEADS, NSA_GROUP, Q_BLOCK, k_top, SEL_BLOCK)
        return jnp.einsum('bhgqnl,bhqnld->bqhgd', p.astype(v_g.dtype), v_g)

    o_slc = lax.map(sel_block, (q_chunks, idx_chunks, pos_chunks))
    o_slc = o_slc.swapaxes(0, 1).reshape(B, T, NSA_KV_HEADS, NSA_GROUP, HEAD_DIM)

    kw = rope(rms_norm(kw, k_gains[2]), pos)
    kpad = jnp.pad(kw, ((0, 0), (WINDOW, 0), (0, 0), (0, 0)))
    vpad = jnp.pad(vw, ((0, 0), (WINDOW, 0), (0, 0), (0, 0)))
    band_idx = np.arange(n_q)[:, None] * Q_BLOCK + np.arange(Q_BLOCK + WINDOW)[None, :]
    kb = kpad[:, band_idx]
    vb = vpad[:, band_idx]
    key_pos = (band_idx - WINDOW)[:, None, :]
    qry_pos = (np.arange(n_q)[:, None] * Q_BLOCK + np.arange(Q_BLOCK)[None, :])[:, :, None]
    valid_w = jnp.asarray((key_pos <= qry_pos) & (key_pos > qry_pos - WINDOW) & (key_pos >= 0))
    qb = q_g.reshape(B, n_q, Q_BLOCK, NSA_KV_HEADS, NSA_GROUP, HEAD_DIM)
    s_w = jnp.einsum('bcqhgd,bckhd->bhgcqk', qb, kb).astype(f32) * scale
    p_w = jax.nn.softmax(jnp.where(valid_w, s_w, NEG_INF), axis=-1)
    o_win = jnp.einsum('bhgcqk,bckhd->bcqhgd', p_w.astype(vb.dtype), vb).reshape(B, T, NSA_KV_HEADS, NSA_GROUP, HEAD_DIM)

    g = gates.reshape(B, T, NSA_KV_HEADS, NSA_GROUP, 3).astype(f32)
    o = g[..., 0:1] * o_cmp.astype(f32) + g[..., 1:2] * o_slc.astype(f32) + g[..., 2:3] * o_win.astype(f32)
    return o.reshape(B, T, NSA_Q_W)

def forgetting_attention(q, k, v, log_f):
    B, T = q.shape[0], q.shape[1]
    f32 = jnp.float32
    scale = HEAD_DIM ** -0.5
    cum = jnp.cumsum(log_f, axis=1).transpose(0, 2, 1)
    outs = []
    for i in range(T // Q_BLOCK):
        lo, hi = i * Q_BLOCK, (i + 1) * Q_BLOCK
        s = jnp.einsum('bqhd,bkhd->bhqk', q[:, lo:hi], k[:, :hi]).astype(f32) * scale
        s = s + cum[:, :, lo:hi, None] - cum[:, :, None, :hi]
        causal = jnp.asarray(np.arange(lo, hi)[:, None] >= np.arange(hi)[None, :])
        p = jax.nn.softmax(jnp.where(causal, s, NEG_INF), axis=-1)
        outs.append(jnp.einsum('bhqk,bkhd->bqhd', p.astype(v.dtype), v[:, :hi]))
    return jnp.concatenate(outs, axis=1).reshape(B, T, FOX_W)

def even_mixer(h, w_in, b_gate, b_forget, cmp_pe, cmp_w1, cmp_w2, nsa_gain, fox_gain, w_out):
    B, T, _ = h.shape
    pos = jnp.arange(T)
    proj = h @ w_in
    widths = [NSA_Q_W] + [NSA_KV_W] * 6 + [NSA_GATE_W, FOX_W, FOX_W, FOX_W]
    offs = [int(o) for o in np.cumsum(widths)]
    q_n, kc, vc, ks, vs, kw, vw, gate_l, q_f, k_f, v_f, f_l = jnp.split(proj, offs, axis=-1)
    heads = lambda t, n: t.reshape(B, T, n, -1)
    q_a = rope(rms_norm(heads(q_n, NSA_HEADS), nsa_gain[0]), pos)
    gates = jax.nn.sigmoid((gate_l + b_gate).astype(jnp.float32)).reshape(B, T, NSA_HEADS, 3)
    o_a = nsa_attention(q_a, heads(kc, NSA_KV_HEADS), heads(vc, NSA_KV_HEADS), heads(ks, NSA_KV_HEADS),
                        heads(vs, NSA_KV_HEADS), heads(kw, NSA_KV_HEADS), heads(vw, NSA_KV_HEADS),
                        gates, cmp_pe, cmp_w1, cmp_w2, nsa_gain[1:])
    q_b = rms_norm(heads(q_f, FOX_HEADS), fox_gain[0])
    k_b = rms_norm(heads(k_f, FOX_HEADS), fox_gain[1])
    log_f = jax.nn.log_sigmoid((f_l + b_forget).astype(jnp.float32))
    o_b = forgetting_attention(q_b, k_b, heads(v_f, FOX_HEADS), log_f)
    o = jnp.concatenate([o_a.astype(h.dtype), o_b.astype(h.dtype)], axis=-1)
    return (o @ w_out).astype(h.dtype)

def causal_depthwise_conv(x, w):
    xp = jnp.pad(x, ((0, 0), (CONV_WIDTH - 1, 0), (0, 0)))
    return lax.conv_general_dilated(xp, w.astype(x.dtype)[:, None, :], (1,), 'VALID',
                                    dimension_numbers=('NWC', 'WIO', 'NWC'), feature_group_count=x.shape[-1])

def gated_delta_chunked(q, k, v, g, beta):
    B, T, H, dk = q.shape
    dv = v.shape[-1]
    C = GDN_CHUNK
    N = T // C
    f32 = jnp.float32
    to_chunks = lambda t: jnp.moveaxis(t.astype(f32).reshape(B, N, C, H, *t.shape[3:]), 3, 1)
    q = to_chunks(q) * (dk ** -0.5)
    k = to_chunks(k)
    v = to_chunks(v)
    beta = to_chunks(beta)
    g = jnp.cumsum(to_chunks(g), axis=-1)
    k_beta = k * beta[..., None]
    v_beta = v * beta[..., None]
    tril = jnp.tril(jnp.ones((C, C), bool))
    strict = jnp.tril(jnp.ones((C, C), bool), -1)
    diff = g[..., :, None] - g[..., None, :]
    decay = jnp.where(tril, jnp.exp(jnp.where(tril, diff, 0.0)), 0.0)
    L = jnp.where(strict, jnp.einsum('bhncd,bhnsd->bhncs', k_beta, k) * decay, 0.0)
    eye = jnp.eye(C, dtype=f32)
    t_inv = lax.linalg.triangular_solve(eye + L, jnp.broadcast_to(eye, L.shape), left_side=True, lower=True)
    u = t_inv @ v_beta
    w = t_inv @ (k_beta * jnp.exp(g)[..., None])
    intra = jnp.where(tril, jnp.einsum('bhncd,bhnsd->bhncs', q, k) * decay, 0.0)

    def step(S, xs):
        q_i, k_i, u_i, w_i, g_i, a_i = xs
        v_new = u_i - w_i @ S
        o = (q_i * jnp.exp(g_i)[..., None]) @ S + a_i @ v_new
        k_dec = k_i * jnp.exp(g_i[..., -1:] - g_i)[..., None]
        S = S * jnp.exp(g_i[..., -1])[..., None, None] + jnp.swapaxes(k_dec, -1, -2) @ v_new
        return S, o

    xs = tuple(jnp.moveaxis(a, 2, 0) for a in (q, k, u, w, g, intra))
    S0 = jnp.zeros((B, H, dk, dv), f32)
    _, o = lax.scan(step, S0, xs)
    return jnp.moveaxis(o, 0, 2).reshape(B, H, T, dv).transpose(0, 2, 1, 3)

def odd_mixer(h, w_in, conv_w, a_log, dt_bias, norm_gain, w_out):
    B, T, _ = h.shape
    proj = h @ w_in
    qkv = jax.nn.silu(causal_depthwise_conv(proj[..., :3 * GDN_WIDTH], conv_w))
    z = proj[..., 3 * GDN_WIDTH:4 * GDN_WIDTH]
    a = proj[..., 4 * GDN_WIDTH:4 * GDN_WIDTH + GDN_HEADS].astype(jnp.float32)
    b = proj[..., 4 * GDN_WIDTH + GDN_HEADS:].astype(jnp.float32)
    heads = lambda t: t.reshape(B, T, GDN_HEADS, GDN_HEAD_DIM)
    q, k, v = jnp.split(qkv, 3, axis=-1)
    q = l2_norm(heads(q))
    k = l2_norm(heads(k))
    beta = jax.nn.sigmoid(b)
    g = -jnp.exp(a_log.astype(jnp.float32)) * jax.nn.softplus(a + dt_bias.astype(jnp.float32))
    o = gated_delta_chunked(q, k, heads(v), g, beta)
    o = rms_norm(o, norm_gain) * jax.nn.silu(heads(z).astype(jnp.float32))
    return (o.reshape(B, T, GDN_WIDTH).astype(h.dtype) @ w_out).astype(h.dtype)

def hierarchical_moe(h, w_rg, b_rg, w_re, b_re, w_ein, w_eout):
    B, T, D = h.shape
    xt = h.reshape(-1, D)
    n_tok = xt.shape[0]
    f32 = jnp.float32
    g_logits = (xt @ w_rg + b_rg).astype(f32)
    g_sel = jnp.argmax(g_logits, axis=-1)
    p_group = jnp.max(jax.nn.softmax(g_logits, axis=-1), axis=-1, keepdims=True)
    e_logits = (xt @ w_re + b_re).astype(f32).reshape(n_tok, N_GROUPS, EXPERTS_PER_GROUP)
    e_in = e_logits[jnp.arange(n_tok), g_sel]
    top_v, top_i = lax.top_k(e_in, EXPERT_TOPK)
    w_top = jax.nn.softmax(top_v, axis=-1) * p_group
    expert_id = g_sel[:, None] * EXPERTS_PER_GROUP + top_i
    gates = jnp.sum(jax.nn.one_hot(expert_id, N_EXPERTS, dtype=f32) * w_top[..., None], axis=1)
    gates = gates.astype(h.dtype)
    y = jnp.zeros((n_tok, D), h.dtype)
    for grp in range(N_GROUPS):
        sl = slice(grp * EXPERTS_PER_GROUP, (grp + 1) * EXPERTS_PER_GROUP)
        gu = jnp.einsum('nd,edf->nef', xt, w_ein[sl])
        act = jax.nn.silu(gu[..., :EXPERT_FF]) * gu[..., EXPERT_FF:] * gates[:, sl, None]
        y = y + jnp.einsum('nef,efd->nd', act, w_eout[sl]).astype(h.dtype)
    return y.reshape(B, T, D)

def setup_inputs(seed: int = 0) -> dict:
    key = jax.random.key(seed)
    ks = jax.random.split(key, 24)
    f32 = jnp.float32
    n_even = (DEPTH + 1) // 2
    n_odd = DEPTH // 2
    nrm = lambda k, shape, s: s * jax.random.normal(k, shape, f32)
    dt = jnp.exp(jax.random.uniform(ks[16], (n_odd, GDN_HEADS), f32, math.log(1e-3), math.log(1e-1)))
    return {
        "x": jax.random.normal(ks[0], (BATCH, SEQ, D_MODEL), f32),
        "norm_mix": 1.0 + nrm(ks[1], (DEPTH, D_MODEL), 0.02),
        "norm_ffn": 1.0 + nrm(ks[2], (DEPTH, D_MODEL), 0.02),
        "w_in_even": nrm(ks[3], (n_even, D_MODEL, EVEN_IN_W), D_MODEL ** -0.5),
        "b_nsa_gate": nrm(ks[4], (n_even, NSA_GATE_W), 0.1),
        "b_forget": jax.random.uniform(ks[5], (n_even, FOX_HEADS), f32, 1.0, 5.0),
        "cmp_pe": nrm(ks[6], (n_even, 2, CMP_BLOCK, HEAD_DIM), 0.02),
        "cmp_w1": nrm(ks[7], (n_even, 2, CMP_BLOCK, HEAD_DIM, HEAD_DIM), (CMP_BLOCK * HEAD_DIM) ** -0.5),
        "cmp_w2": nrm(ks[8], (n_even, 2, HEAD_DIM, HEAD_DIM), HEAD_DIM ** -0.5),
        "nsa_qk_gain": 1.0 + nrm(ks[9], (n_even, 4, HEAD_DIM), 0.02),
        "fox_qk_gain": 1.0 + nrm(ks[10], (n_even, 2, HEAD_DIM), 0.02),
        "w_out_even": nrm(ks[11], (n_even, EVEN_MIX_W, D_MODEL), EVEN_MIX_W ** -0.5),
        "w_in_odd": nrm(ks[12], (n_odd, D_MODEL, ODD_IN_W), D_MODEL ** -0.5),
        "conv_w": nrm(ks[13], (n_odd, CONV_WIDTH, 3 * GDN_WIDTH), CONV_WIDTH ** -0.5),
        "a_log": jnp.log(jax.random.uniform(ks[14], (n_odd, GDN_HEADS), f32, 1.0, 16.0)),
        "dt_bias": dt + jnp.log(-jnp.expm1(-dt)),
        "gdn_norm_gain": 1.0 + nrm(ks[15], (n_odd, GDN_HEAD_DIM), 0.02),
        "w_out_odd": nrm(ks[17], (n_odd, GDN_WIDTH, D_MODEL), GDN_WIDTH ** -0.5),
        "w_router_group": nrm(ks[18], (DEPTH, D_MODEL, N_GROUPS), D_MODEL ** -0.5),
        "b_router_group": nrm(ks[19], (DEPTH, N_GROUPS), 0.01),
        "w_router_expert": nrm(ks[20], (DEPTH, D_MODEL, N_EXPERTS), D_MODEL ** -0.5),
        "b_router_expert": nrm(ks[21], (DEPTH, N_EXPERTS), 0.01),
        "w_expert_in": nrm(ks[22], (DEPTH, N_EXPERTS, D_MODEL, 2 * EXPERT_FF), D_MODEL ** -0.5),
        "w_expert_out": nrm(ks[23], (DEPTH, N_EXPERTS, EXPERT_FF, D_MODEL), EXPERT_FF ** -0.5),
    }

def reference(x, norm_mix, norm_ffn, w_in_even, b_nsa_gate, b_forget, cmp_pe, cmp_w1, cmp_w2,
              nsa_qk_gain, fox_qk_gain, w_out_even, w_in_odd, conv_w, a_log, dt_bias, gdn_norm_gain,
              w_out_odd, w_router_group, b_router_group, w_router_expert, b_router_expert,
              w_expert_in, w_expert_out):
    for layer in range(DEPTH):
        i = layer // 2
        h = rms_norm(x, norm_mix[layer])
        if layer % 2 == 0:
            x = x + even_mixer(h, w_in_even[i], b_nsa_gate[i], b_forget[i], cmp_pe[i], cmp_w1[i], cmp_w2[i],
                               nsa_qk_gain[i], fox_qk_gain[i], w_out_even[i])
        else:
            x = x + odd_mixer(h, w_in_odd[i], conv_w[i], a_log[i], dt_bias[i], gdn_norm_gain[i], w_out_odd[i])
        h = rms_norm(x, norm_ffn[layer])
        x = x + hierarchical_moe(h, w_router_group[layer], b_router_group[layer], w_router_expert[layer],
                                 b_router_expert[layer], w_expert_in[layer], w_expert_out[layer])
    return x


_drawn_inputs = setup_inputs


def setup_inputs(seed=0):
    import zlib

    import numpy as np

    out = dict(_drawn_inputs(seed))
    spreads = {}
    factors = {'b_nsa_gate': 3.07,
     'cmp_pe': 5.384,
     'nsa_qk_gain': 3.298,
     'fox_qk_gain': 5.547,
     'gdn_norm_gain': 15.719,
     'b_router_group': 3.759,
     'b_router_expert': 22.83}
    for name, (base, spread) in spreads.items():
        noise = np.random.default_rng([zlib.crc32(name.encode()), seed]).standard_normal(out[name].shape)
        drawn = base * np.exp(spread * noise) if base else spread * noise
        out[name] = jnp.asarray(drawn.astype(out[name].dtype))
    for name, factor in factors.items():
        out[name] = (out[name] * factor).astype(out[name].dtype)
    return out
```

```python
from contextlib import ExitStack

import numpy as np

import concourse.bass as bass
from concourse import mybir

F32 = mybir.dt.float32
BF16 = mybir.dt.bfloat16
ALU = mybir.AluOpType
ACT = mybir.ActivationFunctionType
AX = mybir.AxisListType

P = 128
D = 1024
T = 256
TT = T // P
KT = D // P
HD = 64
NH = 8
NKV = 2
GROUP = NH // NKV
CMP_BLOCK, CMP_STRIDE = 32, 16
NCMP = (T - CMP_BLOCK) // CMP_STRIDE + 1
NC = 32
EVEN_IN = 2848
GATE0, FQ0, FORGET0 = 1280, 1304, 2840
GH, GD = 8, 128
CHUNK = 64
CONV = 4
NG, EPG, NE, FF = 4, 4, 16, 256
EPS = 1e-6
BIG = 1e30
SCALE = HD ** -0.5

SLOTS = 6
SLOT = 4096
MOE_STEP = 4
LEVELS = [1, 2, 4, 8, 16, 32]
LAYERS = 2


def constant_tables():
    t = np.arange(P)
    tab = {}
    tab["ident"] = np.eye(P)
    tab["ones"] = np.ones((P, P))
    tab["minus_half"] = np.full((P, 1), -0.5)
    tri = np.where(t[None, :] <= t[:, None], 0.0, -BIG)
    tab["causal"] = np.concatenate([np.zeros((P, P)), tri], 1)
    end = np.arange(NC) * CMP_STRIDE + CMP_BLOCK - 1
    tok = np.arange(T).reshape(TT, P)
    ok = (end[None, None, :] <= tok[:, :, None]) & (np.arange(NC) < NCMP)[None, None, :]
    ok = ok.transpose(1, 0, 2)
    tab["cmp_bias"] = np.where(ok, 0.0, -BIG).reshape(P, -1)
    tab["cmp_valid"] = ok.astype(np.float32).reshape(P, -1)
    half = HD // 2
    freq = (np.float32(10000.0) ** (-np.arange(half, dtype=np.float32) / half)).astype(np.float32)

    def rope(pos):
        ang = pos.astype(np.float32)[..., None] * freq
        c, s = np.cos(ang), np.sin(ang)
        return np.concatenate([c, c], -1), np.concatenate([-s, s], -1)

    c, s = rope(tok.T)
    tab["cos"], tab["sin"] = c.reshape(P, -1), s.reshape(P, -1)
    c, s = rope(np.concatenate([end[:NCMP], np.zeros(P - NCMP)]))
    tab["cmp_cos"], tab["cmp_sin"] = c, s
    tab["upto"] = (t[:, None] <= t[None, :]).astype(np.float32)
    tab["block_diag"] = np.kron(np.eye(GROUP), np.ones((NC, HD)))
    tab["rank"] = np.broadcast_to(NE - np.arange(NE), (P, NE))
    same = t[:, None] // CHUNK == t[None, :] // CHUNK
    tab["chunk_upto"] = (same & (t[:, None] <= t[None, :])).astype(np.float32)
    tab["chunk_bias"] = np.concatenate([np.where(same & (t[:, None] < t[None, :]), 0.0, -BIG),
                                        np.where(same & (t[:, None] <= t[None, :]), 0.0, -BIG)], 1)
    last = (t // CHUNK) * CHUNK + CHUNK - 1
    tab["chunk_last"] = (t[:, None] == last[None, :]).astype(np.float32)
    for lv in LEVELS:
        m = (t[:, None] // (2 * lv) == t[None, :] // (2 * lv)) & ((t[:, None] // lv) % 2 == 0) & ((t[None, :] // lv) % 2 == 1)
        tab[f"level{lv}"] = m.astype(np.float32)
    return {k: np.ascontiguousarray(v, np.float32) for k, v in tab.items()}


def table_columns():
    at, out = 0, {}
    for k, v in constant_tables().items():
        out[k] = (at, v.shape[1])
        at += v.shape[1]
    return out, at


class Chain:

    def __init__(self, eng, sem):
        self.eng, self.sem, self.n = eng, sem, 0

    def __call__(self, ins):
        ins.then_inc(self.sem, 1)
        self.n += 1
        self.eng.wait_ge(self.sem, self.n)


class Signals(dict):

    def __init__(self, nc, ctx):
        self.nc, self.ctx = nc, ctx

    def __missing__(self, name):
        self[name] = self.ctx.enter_context(self.nc.semaphore(name))
        return self[name]


def build(nc, a, out):
    cols, width = table_columns()
    ctx = ExitStack()
    with ctx:
        def sb(name, shape, dt=F32):
            return ctx.enter_context(nc.sbuf_tensor(name, shape, dt))

        S = Signals(nc, ctx)
        bank = [ctx.enter_context(nc.psum_tensor(f"bank{i}", [P, 512], F32)) for i in range(8)]

        ring = sb("ring", [P, SLOTS, SLOT])
        const = sb("const", [P, width])
        x = sb("x", [P, TT, D])
        hT = sb("hT", [P, KT, T])
        gain_rows = sb("gain_rows", [32, P])
        gainT = sb("gainT", [P, 32])
        ss = sb("ss", [P, 64])
        rstd = sb("rstd", [P, 64])
        WORK = 16448
        work = sb("work", [P, WORK])

        def table(name, rows=P):
            at, n = cols[name]
            return const[0:rows, at:at + n]

        ident, ones = table("ident"), table("ones")

        def spread(row):
            return ident[:, row:row + 1].to_broadcast([P, P])

        def cut(at, *shape):
            n = int(np.prod(shape))
            assert at + n <= WORK, (at, shape)
            v = work[:, at:at + n]
            if len(shape) > 1:
                names = "abcd"[:len(shape)]
                v = v.rearrange(f"p ({' '.join(names)}) -> p {' '.join(names)}", **dict(zip(names, shape)))
            return v, at + n

        xn, at = cut(0, TT, D)
        mixed, _ = cut(0, TT, D)
        proj, at = cut(at, TT, EVEN_IN)
        headT, at = cut(at, 16, T)
        pe_in, _ = cut(at - 16 * T, 2, 2, T)
        normed_at = at
        normed, at = cut(at, TT, 28, HD)
        kdup, at = cut(at, TT, 4, 2, HD)
        negs, at2 = cut(normed_at, 2, 384)
        probs, at2 = cut(at2, 2, 384)
        probsT, at2 = cut(at2, 2, 384)
        cumk, at2 = cut(at2, T)
        cumq, at2 = cut(at2, T)
        mix_tmp, at2 = cut(at2, 512)
        assert at2 <= at
        squares = mixed
        cmp_s, _ = cut(0, 2, TT, GROUP, NC)
        cmp_e, _ = cut(512, 2, TT, GROUP, NC)
        cmp_pT, _ = cut(1024, 512)
        silu_g, at = cut(TT * D, TT, FF)
        act, at = cut(at, TT, FF)
        actT, at = cut(at, TT, 2, P)

        HH = GH // 2
        qT, at = cut(TT * D, GH, T)
        kT, at = cut(at, GH, T)
        vb, at = cut(at, TT, GH, GD)
        zs, at = cut(at, TT, GH * GD)
        half_at = at
        LA, at = cut(half_at, HH, TT, 2, P)
        Tm, at = cut(at, HH, TT, P)
        TmT_at = at
        TmT, at = cut(at, HH, TT, P)
        X_at = at
        Xm, at = cut(at, HH, TT, P)
        level, at = cut(at, HH, TT, P)
        kbg, _ = cut(TmT_at - HH * TT * P, TT, HH, GD)
        kdec, _ = cut(X_at, TT, HH, GD)
        nwT, _ = cut(X_at + HH * TT * P, TT, HH, P)
        conv_v, _ = cut(half_at, 2, T)
        conv_sq, _ = cut(half_at + 2 * T, 2, T)
        hT_flat = hT[:].rearrange("p k t -> p (k t)")
        decay = hT_flat[:, 0:1024].rearrange("p (b t c i) -> p b t c i", b=2, t=TT, c=2)
        state = hT_flat[:, 1024:1536].rearrange("p (h d) -> p h d", h=HH)
        v_new = hT_flat[:, 1536:2048].rearrange("p (h d) -> p h d", h=HH)
        squares1 = work[:, half_at:half_at + HH * TT * GD].rearrange("p (t h d) -> p t h d", t=TT, h=HH)
        conv_rows = sb("conv_rows", [CONV * 24, P])
        convT = sb("convT", [P, CONV * 24])
        wab = sb("wab", [P, KT, 2 * GH])
        ab_bias = sb("ab_bias", [P, 2, GH])
        gdn_gain = sb("gdn_gain", [P, GD])
        ab = sb("ab", [P, 6, TT, GH])
        gd = sb("gd", [P, 12, TT, GH])
        lnss = sb("lnss", [P, 2, TT, GH])
        rowT = sb("rowT", [GH, 2, T])
        chunk_decay = sb("chunk_decay", [P, 2, TT, GH])

        pe_rows = sb("pe_rows", [CMP_BLOCK, 2, 2, HD])
        peT = sb("peT", [P, 2, CMP_BLOCK])
        w2 = sb("w2", [P, 2, P])
        hx = sb("hx", [P, 2, NC])
        hu = sb("hu", [P, 2, NC])
        hg = sb("hg", [P, 2, GROUP, NC])
        kcn = sb("kcn", [NC, 2, 2, HD])
        kct = sb("kct", [NC, 3, 2, HD])
        kcT = sb("kcT", [P, 2, NC])
        vblock = sb("vblock", [P, 2, GROUP, HD])
        head_gain = sb("head_gain", [P, 6, HD])
        bias_row = sb("bias_row", [P, 32])
        gate = sb("gate", [P, TT, 32])
        gate_tmp = sb("gate_tmp", [P, TT, 32])
        logf = sb("logf", [P, TT, NH])
        neg_max = sb("neg_max", [P, 24, TT])
        sums = sb("sums", [P, 24, TT])
        factor = sb("factor", [P, 24, TT])
        cmp_m = sb("cmp_m", [P, 2 * TT * GROUP])
        cmp_r = sb("cmp_r", [P, 2 * TT * GROUP])
        wr = sb("wr", [P, 2, KT, NG + NE])
        router_bias = sb("router_bias", [P, 2, NG + NE])
        logits = sb("logits", [P, TT, NG + NE])
        rt = sb("rt", [P, 6, TT, NE])
        rs = sb("rs", [P, 8, TT])
        gates = sb("gates", [P, TT, NE])
        zeros = table("causal")[:, 0:P].bitcast(BF16)[:, 0:P]
        finite = table("upto").bitcast(BF16)

        chunks0 = [(512, 512), (0, 512), (1024, 280), (1304, 512), (1816, 512), (2328, 512)]
        stream = [("cmp", 0), ("cmp", 1)] + [("in0", c) for c in chunks0]
        OUT0 = len(stream)
        stream += [("out0", 0), ("out0", 1)]
        MOE_USES = NE + NE // 2
        MOE = {0: len(stream)}
        IN1 = MOE[0] + MOE_USES
        stream1 = [("in1", c) for c in range(8)] + [("out1", 0), ("out1", 1)]
        OUT1 = IN1 + 8
        MOE[1] = IN1 + len(stream1)
        landed = [S[f"weights_landed{i}"] for i in range(SLOTS)]
        read = {0: ("hidden_done", 1), 1: ("hidden_done", 2)}
        for c in range(6):
            read[2 + c] = ("proj_done", TT * (c + 1))
        for l, n0 in ((0, OUT0), (1, OUT1)):
            for c in range(2):
                read[n0 + c] = ("mixed_product", 4 * l + TT * (c + 1))
        for l in range(2):
            for m in range(MOE_USES):
                pair, part = divmod(m, 3)
                read[MOE[l] + m] = (("gu_done1", l * NE + 2 * pair + part + 1) if part < 2
                                    else ("pair_done", l * NE // 2 + pair + 1))
        for c in range(8):
            read[IN1 + c] = ("qkv_done", 4 * (c + 1)) if c < 6 else ("z_done", TT * (c - 5))

        def by_k(s, n=512):
            return ring[:, s, :].rearrange("p (k n) -> p k n", k=KT)[:, :, 0:n]

        def by_f(s):
            return ring[:, s, :].rearrange("p (e f n) -> p e f n", e=2, f=2)

        def unit(u):
            b, h = divmod(u, NH)
            if b == 2:
                return b, h, 8 + h // 2, 12 + h // 2, 2328 + h * HD
            return b, h, h // 2, 4 + 2 * b + h // GROUP, (896 if b == 0 else 1152) + h // GROUP * HD

        UNITS = 3 * NH
        n_small = [0]

        ROOTS = ["mix0", "heads12", "kc", "heads16", "ffn0", "mix1", "o0", "o1", "ffn1"]

        def inverse_root(eng, name, to, of, mean):
            eng.tensor_scalar(to, of, mean, EPS, ALU.mult, ALU.add).then_inc(S["root_arg"], 1)
            eng.wait_ge(S["root_ready"], ROOTS.index(name) + 1)

        def root_pool(pool, name, to):
            pool.wait_ge(S["root_arg"], ROOTS.index(name) + 1)
            pool.tensor_tensor(to, to, table("minus_half", to.shape[0]).to_broadcast(list(to.shape)),
                               ALU.pow).then_inc(S["root_ready"], 1)

        def nth(l, f):
            return 2 * l + (f == "ffn")

        def norm_act(eng, l, f):
            if (l, f) == (0, "mix"):
                eng.wait_ge(S["x_landed"], 16)
            else:
                eng.wait_ge(S["x_added"], 2 * TT * nth(l, f))
            for t in range(TT):
                if t:
                    eng.wait_ge(S["squared"], TT * nth(l, f) + t)
                eng.activation(hT[:, 4 * t:4 * t + 4, :].rearrange("p k t -> p (k t)"), x[:, t, :], ACT.Square,
                               accum_out=ss[:, t:t + 1]).then_inc(S["squared"], 1)
            g0 = (16 if f == "ffn" else 0) + l * KT
            eng.wait_ge(S["gain_ready"], 1)
            for k in (0, 1, 4, 5):
                eng.wait_ge(S["turned"], 4 * nth(l, f) + k // 2 + 1)
                eng.activation(hT[:, k, :], bank[k // 2][:, (k % 2) * T:(k % 2 + 1) * T], ACT.Copy,
                               scale=gainT[:, g0 + k:g0 + k + 1]).then_inc(S["hT_act"], 1)

        def turn_out_act(eng, l):
            for g in (0, 2):
                eng.wait_ge(S["mixed_turned"], 4 * l + g + 1)
                eng.activation(hT[:, 2 * g:2 * g + 2, :].rearrange("p a t -> p (a t)"), bank[g][:],
                               ACT.Copy).then_inc(S["mixedT_act"], 1)

        def moe_act(eng, l):
            eng.wait_ge(S["router_arg"], 2 * l + 1)
            eng.activation(rt[:, 0, :, 0:NG], rt[:, 0, :, 0:NG], ACT.Exp).then_inc(S["router_exp"], 1)
            eng.wait_ge(S["router_arg"], 2 * l + 2)
            eng.activation(rs[:, 1, :], rs[:, 1, :], ACT.Exp).then_inc(S["router_exp"], 1)
            with eng.Fori(0, NE // MOE_STEP) as i:
                for j in range(MOE_STEP):
                    n = i * MOE_STEP + j
                    for t in range(TT):
                        eng.wait_ge(S[f"gu_done{t}"], l * NE + n + 1)
                        eng.wait_ge(S[f"act_ready{t}"], l * (NE + 1) + n + 1)
                        eng.activation(silu_g[:, t, :], bank[t][:, 0:FF], ACT.Silu).then_inc(
                            S[f"silu_ready{t}"], 1)
                        eng.wait_ge(S[f"act_turned{t}"], l * NE + n + 1)
                        eng.activation(actT[:, t, :, :].rearrange("p f t -> p (f t)"), bank[2 + t][:, 0:2 * P],
                                       ACT.Copy).then_inc(S[f"actT_ready{t}"], 1)

        def turn_in(pe, name, src):
            for g in range(4):
                for i in range(2):
                    for t in range(TT):
                        k = 2 * g + i
                        last = pe.transpose(bank[g][:, i * T + t * P:i * T + (t + 1) * P],
                                            src[:, t, k * P:(k + 1) * P], ident)
                last.then_inc(S[name], 1)

        def norm_pe(pe, l, f):
            pe.wait_ge(S["scaled"], TT * (nth(l, f) + 1))
            turn_in(pe, "turned", xn)
            pe.wait_ge(S["hT_act"], 4 * (nth(l, f) + 1))
            pe.wait_ge(S["hT_dve"], 4 * (nth(l, f) + 1))

        def out_product(pe, src, n0, l):
            pe.wait_ge(S["mixed_ready"], 2 * TT * (l + 1))
            turn_in(pe, "mixed_turned", src)
            pe.wait_ge(S["mixedT_act"], 2 * (l + 1))
            pe.wait_ge(S["mixedT_dve"], 2 * (l + 1))
            for c in range(2):
                s = (n0 + c) % SLOTS
                pe.wait_ge(landed[s], 16 * ((n0 + c) // SLOTS + 1))
                for t in range(TT):
                    for k in range(KT):
                        last = pe.matmul(bank[4 + 2 * c + t][:], hT[:, k, t * P:(t + 1) * P], by_k(s)[:, k, :],
                                         start=(k == 0), stop=(k == KT - 1))
                    last.then_inc(S["mixed_product"], 1)

        def moe_pe(pe, l):
            for t in range(TT):
                for k in range(KT):
                    last = pe.matmul(bank[0][:, t * 32:t * 32 + NG + NE], hT[:, k, t * P:(t + 1) * P], wr[:, l, k, :],
                                     start=(k == 0), stop=(k == KT - 1))
            last.then_inc(S["routed"], 1)
            pe.wait_ge(S["x_added"], 2 * TT * (2 * l + 1))
            for b in range(4, 8):
                for c in range(2):
                    pe.matmul(bank[b][:, c * 256:(c + 1) * 256], zeros, finite, start=(c == 0), stop=False,
                              skip_group_check=True)
            pe.wait_ge(S["logits_read"], l + 1)
            n0 = MOE[l]

            def inputs(i, j, t, k0, k1):
                s, turn = (n0 + 3 * (j // 2) + j % 2) % SLOTS, (n0 + 3 * (j // 2) + j % 2) // SLOTS
                if k0 == 0:
                    if t == 0:
                        pe.wait_ge(landed[s], i * 16 + 16 * (turn + 1))
                    pe.wait_ge(S[f"act_ready{t}"], l * (NE + 1) + i * MOE_STEP + j + 1)
                for k in range(k0, k1):
                    last = pe.matmul(bank[t][:], hT[:, k, t * P:(t + 1) * P], by_k(s)[:, k, :],
                                     start=(k == 0), stop=(k == KT - 1))
                if k1 == KT:
                    last.then_inc(S[f"gu_done{t}"], 1)

            def turned(i, j, t):
                pe.wait_ge(S[f"act_ready{t}"], l * (NE + 1) + i * MOE_STEP + j + 2)
                for f in range(2):
                    last = pe.transpose(bank[2 + t][:, f * P:(f + 1) * P], act[:, t, f * P:(f + 1) * P], ident)
                last.then_inc(S[f"act_turned{t}"], 1)

            def outputs(i, j, t):
                m = n0 + 3 * (j // 2) + 2
                s, turn = m % SLOTS, m // SLOTS
                if j % 2 == 0 and t == 0:
                    pe.wait_ge(landed[s], i * 16 + 16 * (turn + 1))
                pe.wait_ge(S[f"actT_ready{t}"], l * NE + i * MOE_STEP + j + 1)
                for c in range(2):
                    for f in range(2):
                        last = pe.matmul(bank[4 + 2 * c + t][:], actT[:, t, f, :],
                                         by_f(s)[:, j % 2, f, c * 512:(c + 1) * 512], start=False, stop=False,
                                         skip_group_check=True)
                if t == 1 and j % 2:
                    last.then_inc(S["pair_done"], 1)

            with pe.Fori(0, NE // MOE_STEP) as i:
                for j in range(MOE_STEP):
                    inputs(i, j, 0, 0, 4)
                    if j:
                        turned(i, j - 1, 1)
                    inputs(i, j, 0, 4, KT)
                    if j:
                        outputs(i, j - 1, 1)
                    inputs(i, j, 1, 0, 4)
                    turned(i, j, 0)
                    inputs(i, j, 1, 4, KT)
                    outputs(i, j, 0)
                turned(i, MOE_STEP - 1, 1)
                outputs(i, MOE_STEP - 1, 1)
            pe.matmul(bank[7][:, 256:512], zeros, finite, start=False, stop=True,
                      skip_group_check=True).then_inc(S["experts_done"], 1)

        def norm_dve(eng, chain, l, f):
            eng.wait_ge(S["squared"], TT * (nth(l, f) + 1))
            inverse_root(eng, f"{f}{l}", rstd[:, 0:TT], ss[:, 0:TT], 1.0 / D)
            for t in range(TT):
                eng.tensor_scalar(xn[:, t, :], x[:, t, :], rstd[:, t:t + 1], None, ALU.mult).then_inc(
                    S["scaled"], 1)
            g0 = (16 if f == "ffn" else 0) + l * KT
            for k in (2, 3, 6, 7):
                eng.wait_ge(S["turned"], 4 * nth(l, f) + k // 2 + 1)
                eng.tensor_scalar(hT[:, k, :], bank[k // 2][:, (k % 2) * T:(k % 2 + 1) * T],
                                  gainT[:, g0 + k:g0 + k + 1], None, ALU.mult).then_inc(S["hT_dve"], 1)

        def turn_out_dve(eng, l):
            for g in (1, 3):
                eng.wait_ge(S["mixed_turned"], 4 * l + g + 1)
                eng.tensor_copy(hT[:, 2 * g:2 * g + 2, :].rearrange("p a t -> p (a t)"), bank[g][:]).then_inc(
                    S["mixedT_dve"], 1)

        def add_product(eng, l):
            for c in range(2):
                for t in range(TT):
                    eng.wait_ge(S["mixed_product"], 4 * l + 2 * c + t + 1)
                    eng.tensor_tensor(x[:, t, c * 512:(c + 1) * 512], x[:, t, c * 512:(c + 1) * 512],
                                      bank[4 + 2 * c + t][:], ALU.add).then_inc(S["x_added"], 1)

        def moe_dve(eng, chain, l):
            eng.wait_ge(S["routed"], l + 1)
            tt, st = eng.tensor_tensor, eng.tensor_scalar
            chain(tt(logits[:], bank[0][:, 0:64].rearrange("p (t n) -> p t n", t=TT)[:, :, 0:NG + NE],
                     router_bias[:, l, :].unsqueeze(1).to_broadcast([P, TT, NG + NE]), ALU.add))
            eng.tensor_copy(rs[:, 7, :], rstd[:, 0:TT]).then_inc(S["logits_read"], 1)
            g_log, e_log = logits[:, :, 0:NG], logits[:, :, NG:NG + NE]
            rank = table("rank")

            def wide(v, n):
                return v.unsqueeze(2).to_broadcast([P, TT, n])

            def first_max(src, top, hot, n):
                rk = rank[:, NE - n:NE].unsqueeze(1).to_broadcast([P, TT, n])
                chain(eng.tensor_reduce(top, src, AX.X, ALU.max))
                chain(tt(hot, src, wide(top, n), ALU.is_equal))
                chain(tt(hot, hot, rk, ALU.mult))
                chain(eng.tensor_reduce(rs[:, 6, :], hot, AX.X, ALU.max))
                chain(tt(hot, wide(rs[:, 6, :], n), rk, ALU.is_equal))

            g_hot = rt[:, 1, :, 0:NG]
            first_max(g_log, rs[:, 0, :], g_hot, NG)
            tt(rt[:, 0, :, 0:NG], g_log, wide(rs[:, 0, :], NG), ALU.subtract).then_inc(S["router_arg"], 1)
            masked = rt[:, 2, :, :]
            chain(st(g_hot, g_hot, 1.0, BIG, ALU.subtract, ALU.mult))
            chain(tt(masked.rearrange("p t (g e) -> p t g e", g=NG), e_log.rearrange("p t (g e) -> p t g e", g=NG),
                     g_hot.unsqueeze(3).to_broadcast([P, TT, NG, EPG]), ALU.add))
            hot1, hot2 = rt[:, 3, :, :], rt[:, 4, :, :]
            first_max(masked, rs[:, 2, :], hot1, NE)
            chain(eng.scalar_tensor_tensor(rt[:, 5, :, :], hot1, -2 * BIG, masked, ALU.mult, ALU.add))
            first_max(rt[:, 5, :, :], rs[:, 3, :], hot2, NE)
            tt(rs[:, 1, :], rs[:, 3, :], rs[:, 2, :], ALU.subtract).then_inc(S["router_arg"], 1)
            eng.wait_ge(S["router_exp"], 2 * l + 1)
            chain(eng.tensor_reduce(rs[:, 4, :], rt[:, 0, :, 0:NG], AX.X, ALU.add))
            eng.wait_ge(S["router_exp"], 2 * l + 2)
            chain(st(rs[:, 5, :], rs[:, 1, :], 1.0, None, ALU.add))
            chain(tt(rs[:, 5, :], rs[:, 5, :], rs[:, 4, :], ALU.mult))
            chain(eng.reciprocal(rs[:, 4, :], rs[:, 5, :]))
            chain(tt(rs[:, 5, :], rs[:, 4, :], rs[:, 1, :], ALU.mult))
            chain(tt(hot1, hot1, wide(rs[:, 4, :], NE), ALU.mult))
            chain(tt(hot2, hot2, wide(rs[:, 5, :], NE), ALU.mult))
            tt(gates[:], hot1, hot2, ALU.add).then_inc(S["gates_ready"], 1)
            eng.wait_ge(S["gates_ready"], l + 1)
            for t in range(TT):
                eng.tensor_copy(rs[:, 7, t:t + 1], rstd[:, t:t + 1]).then_inc(S[f"act_ready{t}"], 1)
            with eng.Fori(0, NE // MOE_STEP) as i:
                for j in range(MOE_STEP):
                    n = i * MOE_STEP + j
                    for t in range(TT):
                        eng.wait_ge(S[f"silu_ready{t}"], l * NE + n + 1)
                        if j:
                            eng.wait_ge(S[f"act_turned{t}"], l * NE + n)
                        eng.scalar_tensor_tensor(act[:, t, :], silu_g[:, t, :],
                                                 gates[:, t, bass.ds(n, 1)],
                                                 bank[t][:, FF:2 * FF], ALU.mult, ALU.mult).then_inc(
                                                     S[f"act_ready{t}"], 1)
                    if j == MOE_STEP - 1:
                        for t in range(TT):
                            eng.wait_ge(S[f"act_turned{t}"], l * NE + n + 1)
            eng.wait_ge(S["experts_done"], l + 1)
            for c in range(2):
                for t in range(TT):
                    eng.tensor_tensor(x[:, t, c * 512:(c + 1) * 512], x[:, t, c * 512:(c + 1) * 512],
                                      bank[4 + 2 * c + t][:], ALU.add).then_inc(
                                          S["x_added"], 1)

        def gdn_loads():
            return [
                (conv_rows[:], a["conv_w"][0].rearrange("j (b p) -> (j b) p", p=P)),
                (wab[:], a["w_in_odd"][0].rearrange("(k p) n -> p k n", p=P)[:, :, 4 * GH * GD:4 * GH * GD + 2 * GH]),
                (ab_bias[:, 0, :], a["dt_bias"][0].partition_broadcast(P)),
                (ab_bias[:, 1, :], a["a_log"][0].partition_broadcast(P)),
                (gdn_gain[:], a["gdn_norm_gain"][0].partition_broadcast(P)),
            ]

        def gdn_act(eng):
            eng.wait_ge(S["ab_arg"], 2)
            eng.activation(ab[:, 2:4], ab[:, 2:4], ACT.Exp, scale=-1.0).then_inc(S["ab_exp"], 1)
            eng.activation(ab_bias[:, 1, :], ab_bias[:, 1, :], ACT.Exp).then_inc(S["ab_exp"], 1)
            eng.wait_ge(S["ab_plus1"], 1)
            eng.activation(ab[:, 2:4], ab[:, 2:4], ACT.Ln).then_inc(S["ab_ln"], 1)
            eng.wait_ge(S["lnbeta_ready"], 1)
            eng.activation(gd[:, 11], gd[:, 0], ACT.Exp).then_inc(S["beta_ready"], 1)
            eng.wait_ge(S["beta_ready"], 1)
            for b in range(24):
                which, h = divmod(b, GH)
                eng.wait_ge(S["convolved"], b + 1)
                dst = (qT[:, h, :], kT[:, h, :], conv_v[:, h % 2, :])[which]
                eng.activation(dst, dst, ACT.Silu).then_inc(S["silu_qkv"], 1)
                if which < 2:
                    eng.wait_ge(S["silu_qkv"], b + 1)
                    if b >= 2:
                        eng.wait_ge(S["norms_done"], 2 * (b - 1))
                    eng.activation(conv_sq[:, b % 2, :], dst, ACT.Square).then_inc(S["qk_squared"], 1)
                if which == 2 and h >= 1:
                    v_out(eng, h - 1)
            v_out(eng, GH - 1)
            for m in range(2 * TT):
                c, t = divmod(m, TT)
                eng.wait_ge(S["z_done"], m + 1)
                eng.activation(zs[:, t, c * 512:(c + 1) * 512], bank[m][:], ACT.Silu).then_inc(S["z_ready"], 1)
            eng.wait_ge(S["norms_plus"], 1)
            eng.activation(lnss[:], lnss[:], ACT.Ln).then_inc(S["norms_ln"], 1)
            eng.wait_ge(S["scale_args"], 4)
            eng.activation(gd[:, 6:9], gd[:, 3:6], ACT.Exp).then_inc(S["scales_ready"], 1)
            eng.activation(chunk_decay[:], chunk_decay[:], ACT.Exp).then_inc(S["scales_ready"], 1)
            for hf in range(2):
                for hh in range(HH):
                    n = hf * HH + hh
                    eng.wait_ge(S["decay_arg"], TT * (n + 1))
                    d = decay[:, n % 2].rearrange("p t c i -> p (t c i)")
                    eng.activation(d, d, ACT.Exp).then_inc(S["decay_ready"], 1)
                for g in range(2):
                    eng.wait_ge(S["inv_turned"], 2 * hf + g + 1)
                    eng.activation(Tm[:, 2 * g:2 * g + 2].rearrange("p h t i -> p (h t i)"), bank[4 + g][:],
                                   ACT.Copy).then_inc(S["inv_first_out"], 1)
                for li in range(1, len(LEVELS)):
                    for g in range(2):
                        eng.wait_ge(S["inv_x"], 10 * hf + 2 * (li - 1) + g + 1)
                        eng.activation(Xm[:, 2 * g:2 * g + 2].rearrange("p h t i -> p (h t i)"), bank[4 + g][:],
                                       ACT.Copy).then_inc(S["inv_x_out"], 1)
                for t in range(TT):
                    eng.wait_ge(S["w_done"], TT * hf + t + 1)
                    eng.activation(nwT[:, t].rearrange("p h i -> p (h i)"), bank[4 + t][:], ACT.Copy,
                                   scale=-1.0).then_inc(S["w_ready"], 1)
                for c in range(4):
                    t, s_ = divmod(c, 2)
                    rows = slice(s_ * CHUNK, (s_ + 1) * CHUNK)
                    eng.wait_ge(S["v_new_done"], 4 * hf + c + 1)
                    eng.activation(v_new[rows].rearrange("p h d -> p (h d)"), bank[6 + t][rows, :],
                                   ACT.Copy).then_inc(S["v_new_ready"], 1)
                eng.wait_ge(S["o_ready"], TT * (hf + 1))
                eng.activation(squares1, mixed.rearrange("p t (h d) -> p t h d", d=GD)[:, :, hf * HH:(hf + 1) * HH, :],
                               ACT.Square).then_inc(S["o_squared"], 1)
            turn_out_act(eng, 1)

        def v_out(eng, h):
            eng.wait_ge(S["v_turned"], h + 1)
            for t in range(TT):
                eng.activation(vb[:, t, h, :], bank[5 + h % 2][:, t * P:(t + 1) * P], ACT.Copy,
                               scale=gd[:, 11, t, h:h + 1]).then_inc(S["v_ready"], 1)

        def gdn_pe(pe):
            pe.transpose(bank[6][:, 0:CONV * 24], conv_rows[:], ident[0:CONV * 24, 0:CONV * 24]).then_inc(
                S["conv_turned"], 1)
            for t in range(TT):
                for k in range(KT):
                    last = pe.matmul(bank[7][:, t * 16:(t + 1) * 16], hT[:, k, t * P:(t + 1) * P], wab[:, k, :],
                                     start=(k == 0), stop=(k == KT - 1))
            last.then_inc(S["ab_done"], 1)

            def norms(b):
                pe.wait_ge(S["qk_squared"], b + 1)
                which, h = divmod(b, GH)
                for t in range(TT):
                    at_ = (which * TT + t) * GH + h
                    pe.matmul(bank[4][:, at_:at_ + 1], conv_sq[:, b % 2, t * P:(t + 1) * P], ones[:, 0:1],
                              start=True, stop=True).then_inc(S["norms_done"], 1)

            def turn_v(h):
                pe.wait_ge(S["silu_qkv"], 16 + h + 1)
                if h >= 2:
                    pe.wait_ge(S["v_ready"], 2 * (h - 1))
                for t in range(TT):
                    last = pe.transpose(bank[5 + h % 2][:, t * P:(t + 1) * P], conv_v[:, h % 2, t * P:(t + 1) * P],
                                        ident)
                last.then_inc(S["v_turned"], 1)

            for b in range(24 + 2):
                if b < 24:
                    c, m = divmod(b, 4)
                    s_ = (IN1 + c) % SLOTS
                    if m == 0:
                        pe.wait_ge(landed[s_], 16 * ((IN1 + c) // SLOTS + 1))
                    if b >= 4:
                        pe.wait_ge(S["convolved"], b - 3)
                    for k in range(KT):
                        last = pe.matmul(bank[b % 4][:, 0:T], by_k(s_)[:, k, m * P:(m + 1) * P], hT[:, k, :],
                                         start=(k == 0), stop=(k == KT - 1))
                    last.then_inc(S["qkv_done"], 1)
                if b == 2:
                    pe.wait_ge(S["g_ready"], 1)
                    pe.matmul(bank[7][:, 64:80], table("chunk_upto"), gd[:, 1].rearrange("p t h -> p (t h)"),
                              start=True, stop=True).then_inc(S["gc_done"], 1)
                    pe.wait_ge(S["gc_ready"], 1)
                    gc = gd[:, 2].rearrange("p t h -> p (t h)")
                    pe.matmul(bank[7][:, 80:96], table("chunk_last"), gc, start=True, stop=True)
                    for s2 in range(2):
                        last = pe.matmul(bank[7][:, 96 + 16 * s2:112 + 16 * s2],
                                         spread(s2 * CHUNK + CHUNK - 1), gc, start=True, stop=True)
                    last.then_inc(S["last_done"], 1)
                if 2 <= b < 18:
                    norms(b - 2)
                if b >= 18:
                    turn_v(b - 18)
            for m in range(2 * TT):
                c, t = divmod(m, TT)
                n = IN1 + 6 + c
                if t == 0:
                    pe.wait_ge(landed[n % SLOTS], 16 * (n // SLOTS + 1))
                pe.wait_ge(S["convolved"], 24)
                for k in range(KT):
                    last = pe.matmul(bank[m][:], hT[:, k, t * P:(t + 1) * P], by_k(n % SLOTS)[:, k, :],
                                     start=(k == 0), stop=(k == KT - 1))
                last.then_inc(S["z_done"], 1)
            pe.wait_ge(S["scale_args"], 4)
            for r in range(2):
                for t in range(TT):
                    last = pe.transpose(bank[4][0:GH, r * T + t * P:r * T + (t + 1) * P], gd[:, 3 + r, t, :], ident)
            last.then_inc(S["rows_turned"], 1)
            pe.wait_ge(S["rows_ready"], 1)
            pe.wait_ge(S["z_ready"], 2 * TT)
            for hf in range(2):
                if hf:
                    pe.wait_ge(S["o_ready"], TT)
                for hh in range(HH):
                    h, n = hf * HH + hh, hf * HH + hh
                    if hh >= 2:
                        pe.wait_ge(S["decay_arg"], TT * (n - 1))
                        pe.wait_ge(S["LA_ready"], n - 1)
                    sel = spread(h)[0:GH]
                    for r in range(2):
                        last = pe.matmul(bank[hh % 2][:, r * T:(r + 1) * T], sel, rowT[:, r, :], start=True, stop=True)
                    last.then_inc(S["rows_spread"], 1)
                    for t in range(TT):
                        tok = slice(t * P, (t + 1) * P)
                        for c, other in enumerate((kT, qT)):
                            last = pe.matmul(bank[2 + hh % 2][:, (2 * t + c) * P:(2 * t + c + 1) * P], kT[:, h, tok],
                                             other[:, h, tok], start=True, stop=True)
                    last.then_inc(S["gram_done"], 1)
                for g in range(2):
                    pe.wait_ge(S["inv_T"], 12 * hf + g + 1)
                    for m in range(4):
                        hh, t = 2 * g + m // 2, m % 2
                        last = pe.transpose(bank[4 + g][:, m * P:(m + 1) * P], TmT[:, hh, t, :], ident)
                    last.then_inc(S["inv_turned"], 1)
                for li in range(1, len(LEVELS)):
                    final = li == len(LEVELS) - 1
                    pe.wait_ge(S["level_ready"], 6 * hf + li + 1)
                    for g in range(2):
                        if li == 1:
                            pe.wait_ge(S["inv_first_out"], 2 * hf + g + 1)
                        else:
                            pe.wait_ge(S["inv_T"], 12 * hf + 2 * (li - 1) + g + 1)
                        for m in range(4):
                            hh, t = 2 * g + m // 2, m % 2
                            last = pe.matmul(bank[4 + g][:, m * P:(m + 1) * P], level[:, hh, t, :], Tm[:, hh, t, :],
                                             start=True, stop=True)
                        last.then_inc(S["inv_x"], 1)
                    for g in range(2):
                        pe.wait_ge(S["inv_x_out"], 10 * hf + 2 * (li - 1) + g + 1)
                        for m in range(4):
                            hh, t = 2 * g + m // 2, m % 2
                            last = pe.matmul(bank[g][:, m * P:(m + 1) * P], Xm[:, hh, t, :], TmT[:, hh, t, :],
                                             start=True, stop=True)
                            if not final:
                                last = pe.matmul(bank[6 + g][:, m * P:(m + 1) * P], TmT[:, hh, t, :],
                                                 Xm[:, hh, t, :], start=True, stop=True)
                        last.then_inc(S["inv_y"], 1)
                for t in range(TT):
                    for hh in range(HH):
                        last = pe.transpose(bank[2 + t][:, hh * P:(hh + 1) * P],
                                            kT[:, hf * HH + hh, t * P:(t + 1) * P], ident)
                    last.then_inc(S["k_turned"], 1)
                for t in range(TT):
                    pe.wait_ge(S["k_scaled"], 2 * (TT * hf + t + 1))
                    if t == 0:
                        pe.wait_ge(S["inv_T"], 12 * (hf + 1))
                    for hh in range(HH):
                        last = pe.matmul(bank[4 + t][:, hh * P:(hh + 1) * P], kbg[:, t, hh, :], TmT[:, hh, t, :],
                                         start=True, stop=True)
                    last.then_inc(S["w_done"], 1)
                pe.wait_ge(S["w_ready"], TT * (hf + 1))
                for c in range(4):
                    t, s_ = divmod(c, 2)
                    rows = slice(s_ * CHUNK, (s_ + 1) * CHUNK)
                    tok = slice(t * P + s_ * CHUNK, t * P + (s_ + 1) * CHUNK)
                    pe.wait_ge(S["v_ready"], 2 * GH)
                    pe.wait_ge(S["state_ready"], 5 * hf + c + 1)
                    for hh in range(HH):
                        o = bank[6 + t][rows, hh * GD:(hh + 1) * GD]
                        pe.matmul(o, TmT[:, hh, t, rows], vb[:, t, hf * HH + hh, :], start=True, stop=False)
                        last = pe.matmul(o, nwT[:, t, hh, rows], state[:, hh, :], start=False, stop=True)
                    last.then_inc(S["v_new_done"], 1)
                    for hh in range(HH):
                        last = pe.matmul(bank[t][rows, hh * GD:(hh + 1) * GD], qT[:, hf * HH + hh, tok],
                                         state[:, hh, :], start=True, stop=True)
                    last.then_inc(S["q_state_done"], 1)
                    pe.wait_ge(S["v_new_ready"], 4 * hf + c + 1)
                    for hh in range(HH):
                        last = pe.matmul(bank[4 + c % 2][:, hh * GD:(hh + 1) * GD], kdec[rows, t, hh, :],
                                         v_new[rows, hh, :], start=True, stop=True)
                    last.then_inc(S["update_done"], 1)
                    for hh in range(HH):
                        last = pe.matmul(bank[2 + t][rows, hh * GD:(hh + 1) * GD], LA[rows, hh, t, 1, rows],
                                         v_new[rows, hh, :], start=True, stop=True)
                    last.then_inc(S["chunk_out"], 1)
            out_product(pe, mixed, OUT1, 1)

        def gdn_pool(pool):
            for hf in range(2):
                for li, lv in enumerate(LEVELS):
                    if li == 0:
                        pool.wait_ge(S["LA_ready"], HH * (hf + 1))
                        if hf:
                            pool.wait_ge(S["chunk_out"], 4)
                    elif li == 1:
                        pool.wait_ge(S["inv_T"], 12 * hf + 2)
                    else:
                        pool.wait_ge(S["inv_x"], 10 * hf + 2 * (li - 1))
                    mask = table(f"level{lv}").unsqueeze(1).unsqueeze(1).to_broadcast([P, HH, TT, P])
                    pool.tensor_tensor(level, LA[:, :, :, 0, :], mask, ALU.mult).then_inc(S["level_ready"], 1)
                root_pool(pool, f"o{hf}", rstd[:, 0:TT * HH])

        def gdn_dve(eng, chain):
            tt, st, stt = eng.tensor_tensor, eng.tensor_scalar, eng.scalar_tensor_tensor
            lnbeta, g_, gc, row1, row2, dec_arg = (gd[:, i] for i in range(6))
            col = gd[:, 9]
            eng.wait_ge(S["conv_turned"], 1)
            chain(eng.tensor_copy(convT[:], bank[6][:, 0:CONV * 24]))
            eng.wait_ge(S["ab_done"], 1)
            raw = bank[7][:, 0:32].rearrange("p (t c h) -> p c t h", t=TT, c=2)
            chain(tt(ab[:, 0], raw[:, 0], ab_bias[:, 0, :].unsqueeze(1).to_broadcast([P, TT, GH]), ALU.add))
            chain(eng.tensor_copy(ab[:, 1], raw[:, 1]))
            for i in range(2):
                stt(ab[:, 2 + i], ab[:, i], -1.0, ab[:, i], ALU.mult, ALU.max).then_inc(S["ab_arg"], 1)
            eng.wait_ge(S["ab_exp"], 2)
            st(ab[:, 2:4], ab[:, 2:4], 1.0, None, ALU.add).then_inc(S["ab_plus1"], 1)
            eng.wait_ge(S["ab_ln"], 1)
            stt(lnbeta, ab[:, 1], 0.0, ab[:, 3], ALU.min, ALU.subtract).then_inc(S["lnbeta_ready"], 1)
            chain(stt(g_, ab[:, 0], 0.0, ab[:, 2], ALU.max, ALU.add))
            stt(g_, g_, -1.0, ab_bias[:, 1, :].unsqueeze(1).to_broadcast([P, TT, GH]), ALU.mult,
                ALU.mult).then_inc(S["g_ready"], 1)
            for b in range(24):
                which, h = divmod(b, GH)
                dst = (qT[:, h, :], kT[:, h, :], conv_v[:, h % 2, :])[which]
                if b == 3:
                    eng.wait_ge(S["gc_done"], 1)
                    eng.tensor_copy(gc.rearrange("p t h -> p (t h)"), bank[7][:, 64:80]).then_inc(S["gc_ready"], 1)
                    eng.wait_ge(S["last_done"], 1)
                    chain(tt(gd[:, 10].rearrange("p t h -> p (t h)"), bank[7][:, 80:96],
                             gc.rearrange("p t h -> p (t h)"), ALU.subtract))
                    chain(eng.tensor_copy(chunk_decay[:].rearrange("p s t h -> p (s t h)"), bank[7][:, 96:128]))
                eng.wait_ge(S["qkv_done"], b + 1)
                if which == 2 and h >= 2:
                    eng.wait_ge(S["v_turned"], h - 1)
                src = bank[b % 4]
                chain(st(dst, src[:, 0:T], convT[:, 72 + b:73 + b], None, ALU.mult))
                for back in (1, 2, 3):
                    i = 24 * (3 - back) + b
                    ins = stt(dst[:, back:T], src[:, 0:T - back], convT[:, i:i + 1], dst[:, back:T], ALU.mult, ALU.add)
                    if back < 3:
                        chain(ins)
                    else:
                        ins.then_inc(S["convolved"], 1)
            eng.wait_ge(S["norms_done"], 2 * 2 * GH)
            st(lnss[:].rearrange("p c t h -> p (c t h)"), bank[4][:, 0:32], EPS, None, ALU.add).then_inc(
                S["norms_plus"], 1)
            eng.wait_ge(S["norms_ln"], 1)
            lq, lk = lnss[:, 0], lnss[:, 1]
            chain(st(lq, lq, -0.5, float(-0.5 * np.log(GD)), ALU.mult, ALU.add))
            chain(st(lk, lk, -0.5, None, ALU.mult))
            chain(tt(row1, gc, lnbeta, ALU.add))
            tt(row1, row1, lk, ALU.add).then_inc(S["scale_args"], 1)
            tt(row2, gc, lq, ALU.add).then_inc(S["scale_args"], 1)
            tt(dec_arg, gd[:, 10], lk, ALU.add).then_inc(S["scale_args"], 1)
            tt(col, lk, gc, ALU.subtract).then_inc(S["scale_args"], 1)
            eng.wait_ge(S["scale_args"], 4)
            eng.wait_ge(S["rows_turned"], 1)
            eng.tensor_copy(rowT[:].rearrange("p r t -> p (r t)"), bank[4][0:GH, :]).then_inc(S["rows_ready"], 1)
            eng.wait_ge(S["scales_ready"], 2)
            s_kb, s_q, s_kd = gd[:, 6], gd[:, 7], gd[:, 8]
            bias = table("chunk_bias").rearrange("p (c i) -> p c i", c=2)
            eng.wait_ge(S["z_done"], 2 * TT)
            for hf in range(2):
                heads = slice(hf * HH, (hf + 1) * HH)

                def gram(n):
                    eng.wait_ge(S["decay_ready"], n + 1)
                    eng.wait_ge(S["gram_done"], n + 1)
                    tt(LA[:, n % HH].rearrange("p t c i -> p (t c i)"), bank[2 + n % 2][:],
                       decay[:, n % 2].rearrange("p t c i -> p (t c i)"), ALU.mult).then_inc(S["LA_ready"], 1)

                for hh in range(HH):
                    n = hf * HH + hh
                    eng.wait_ge(S["rows_spread"], n + 1)
                    if hh >= 2:
                        eng.wait_ge(S["LA_ready"], n - 1)
                    for t in range(TT):
                        stt(decay[:, n % 2, t], bank[hh % 2][:].rearrange("p (c t) -> p c t", c=2)[
                            :, :, t * P:(t + 1) * P], col[:, t, n:n + 1], bias, ALU.add, ALU.add).then_inc(
                                S["decay_arg"], 1)
                    if hh >= 1:
                        gram(n - 1)
                gram(hf * HH + HH - 1)
                eng.memset(state, 0.0).then_inc(S["state_ready"], 1)
                eng.wait_ge(S["level_ready"], 6 * hf + 1)
                for g in range(2):
                    tt(TmT[:, 2 * g:2 * g + 2], ident.unsqueeze(1).unsqueeze(1).to_broadcast([P, 2, TT, P]),
                       level[:, 2 * g:2 * g + 2], ALU.subtract).then_inc(S["inv_T"], 1)
                eng.wait_ge(S["inv_first_out"], 2 * (hf + 1))
                for li in range(1, len(LEVELS)):
                    for g in range(2):
                        eng.wait_ge(S["inv_y"], 10 * hf + 2 * (li - 1) + g + 1)
                        v = TmT[:, 2 * g:2 * g + 2].rearrange("p h t i -> p (h t i)")
                        ins = tt(v, v, bank[g][:], ALU.subtract)
                        if li < len(LEVELS) - 1:
                            chain(ins)
                            v = Tm[:, 2 * g:2 * g + 2].rearrange("p h t i -> p (h t i)")
                            ins = tt(v, v, bank[6 + g][:], ALU.subtract)
                        ins.then_inc(S["inv_T"], 1)
                for t in range(TT):
                    eng.wait_ge(S["k_turned"], TT * hf + t + 1)
                    src = bank[2 + t][:].rearrange("p (h d) -> p h d", d=GD)
                    for dst, f in ((kbg, s_kb), (kdec, s_kd)):
                        tt(dst[:, t], src, f[:, t, heads].unsqueeze(2).to_broadcast([P, HH, GD]), ALU.mult).then_inc(
                            S["k_scaled"], 1)
                for c in range(4):
                    t, s_ = divmod(c, 2)
                    eng.wait_ge(S["q_state_done"], 4 * hf + c + 1)
                    chain(tt(state, state, chunk_decay[:, s_, t, heads].unsqueeze(2).to_broadcast([P, HH, GD]),
                             ALU.mult))
                    eng.wait_ge(S["update_done"], 4 * hf + c + 1)
                    tt(state.rearrange("p h d -> p (h d)"), state.rearrange("p h d -> p (h d)"), bank[4 + c % 2][:],
                       ALU.add).then_inc(S["state_ready"], 1)
                    if s_ == 1:
                        eng.wait_ge(S["chunk_out"], 4 * hf + c + 1)
                        o = mixed.rearrange("p t (h d) -> p t h d", d=GD)[:, t, heads, :]
                        chain(tt(o, bank[t][:].rearrange("p (h d) -> p h d", d=GD),
                                 s_q[:, t, heads].unsqueeze(2).to_broadcast([P, HH, GD]), ALU.mult))
                        tt(o, o, bank[2 + t][:].rearrange("p (h d) -> p h d", d=GD), ALU.add).then_inc(
                            S["o_ready"], 1)
                eng.wait_ge(S["o_squared"], hf + 1)
                chain(eng.tensor_reduce(ss[:, 0:TT * HH].rearrange("p (t h) -> p t h", t=TT), squares1, AX.X, ALU.add))
                inverse_root(eng, f"o{hf}", rstd[:, 0:TT * HH], ss[:, 0:TT * HH], 1.0 / GD)
                for t in range(TT):
                    o = mixed.rearrange("p t (h d) -> p t h d", d=GD)[:, t, heads, :]
                    chain(tt(o, o, rstd[:, t * HH:(t + 1) * HH].unsqueeze(2).to_broadcast([P, HH, GD]), ALU.mult))
                    chain(tt(o, o, gdn_gain[:].unsqueeze(1).to_broadcast([P, HH, GD]), ALU.mult))
                    tt(o, o, zs[:, t, :].rearrange("p (h d) -> p h d", d=GD)[:, heads, :], ALU.mult).then_inc(
                        S["mixed_ready"], 1)
            turn_out_dve(eng, 1)
            add_product(eng, 1)

        N_SMALL = 1 + 10 + 8 + len(gdn_loads())

        block = ctx.enter_context(nc.Block())

        @block.sync
        def _(sp):
            def load(n, kind, c):
                s = n % SLOTS
                if n >= SLOTS:
                    name, value = read[n - SLOTS]
                    sp.wait_ge(S[name], value)
                if kind == "cmp":
                    sp.wait_ge(S["slots_zeroed"], c + 1)
                    dst = ring[:, s, :].rearrange("p (l e) -> p l e", l=CMP_BLOCK)
                    src = a["cmp_w1"][0, c].rearrange("l d e -> d l e")
                    sp.dma_start(dst[0:HD, :, 0:HD], src).then_inc(S["cmp_half_landed"], 16)
                    sp.dma_start(dst[HD:P, :, HD:P], src).then_inc(landed[s], 16)
                    return
                if kind == "in0":
                    w, (c0, n_cols) = a["w_in_even"][0], c
                    if c0 == 1024:
                        sp.dma_start(by_k(s)[:, :, 280:288], w.rearrange("(k p) n -> p k n", p=P)[
                            :, :, FORGET0:FORGET0 + 8]).then_inc(S["forget_landed"], 16)
                elif kind == "out0":
                    w, c0, n_cols = a["w_out_even"][0], 512 * c, 512
                elif kind == "in1":
                    w, c0, n_cols = a["w_in_odd"][0], 512 * c, 512
                else:
                    w, c0, n_cols = a["w_out_odd"][0], 512 * c, 512
                sp.dma_start(by_k(s, n_cols), w.rearrange("(k p) n -> p k n", p=P)[
                    :, :, c0:c0 + n_cols]).then_inc(landed[s], 16)

            def load_experts(layer):
                w_in = a["w_expert_in"][layer].rearrange("e (k p) n -> e p k n", p=P)
                w_out = a["w_expert_out"][layer].rearrange("(q e) (f p) n -> q p (e f) n", p=P, e=2)

                def load_four(i):
                    for j in range(SLOTS):
                        s = (MOE[layer] + j) % SLOTS
                        pair, part = divmod(j, 3)
                        if type(i) is int:
                            name, value = read[MOE[layer] + j - SLOTS]
                            sp.wait_ge(S[name], value)
                        elif part < 2:
                            sp.wait_ge(S["gu_done1"], layer * NE + (i - 1) * MOE_STEP + 2 * pair + part + 1)
                        else:
                            sp.wait_ge(S["pair_done"], layer * NE // 2 + (i - 1) * (MOE_STEP // 2) + pair + 1)
                        if part < 2:
                            src = w_in[bass.ds(i * MOE_STEP + 2 * pair + part, 1)]
                            dst = by_k(s)
                        else:
                            src = w_out[bass.ds(i * (MOE_STEP // 2) + pair, 1)]
                            dst = by_f(s).rearrange("p e f n -> p (e f) n")
                        sp.dma_start(dst, src.rearrange("o p k n -> (o p) k n")).then_inc(landed[s], 16)

                load_four(0)
                with sp.Fori(1, NE // MOE_STEP) as i:
                    load_four(i)

            for n, (kind, c) in enumerate(stream):
                load(n, kind, c)
            load_experts(0)
            if LAYERS > 1:
                for n, (kind, c) in enumerate(stream1):
                    load(IN1 + n, kind, c)
                load_experts(1)
            sp.wait_ge(S["x_added"], 2 * TT * 2 * LAYERS)
            sp.dma_start(out[0].rearrange("(t p) d -> p t d", p=P), x[:]).then_inc(S["stored"], 16)
            sp.wait_ge(S["stored"], 16)

        @block.gpsimd
        def _(pool):
            pool.memset(w2[:], 0.0).then_inc(S["w2_zeroed"], 1)
            pool.memset(ring[:, 0, :], 0.0).then_inc(S["slots_zeroed"], 1)
            pool.memset(ring[:, 1, :], 0.0).then_inc(S["slots_zeroed"], 1)
            root_pool(pool, "mix0", rstd[:, 0:TT])
            root_pool(pool, "heads12", rstd[:, 0:TT * 12])
            root_pool(pool, "kc", rstd[0:NC, 60:62])
            root_pool(pool, "heads16", rstd[:, 0:TT * 16])
            root_pool(pool, "ffn0", rstd[:, 0:TT])
            if LAYERS > 1:
                root_pool(pool, "mix1", rstd[:, 0:TT])
                gdn_pool(pool)
                root_pool(pool, "ffn1", rstd[:, 0:TT])

        @block.scalar
        def _(eng):
            chain = Chain(eng, S["act_chain"])
            eng.dma_start(x[:], a["x"][0].rearrange("(t p) d -> p t d", p=P)).then_inc(S["x_landed"], 16)
            eng.dma_start(const[:], a["tables"]).then_inc(S["small_landed"], 16)
            small = [
                (gain_rows[0:16, :], a["norm_mix"].rearrange("l (k p) -> (l k) p", p=P)),
                (gain_rows[16:32, :], a["norm_ffn"].rearrange("l (k p) -> (l k) p", p=P)),
                (pe_rows[:, :, 0, :], a["cmp_pe"][0].rearrange("c l d -> l c d")),
                (pe_rows[:, :, 1, :], a["cmp_pe"][0].rearrange("c l d -> l c d")),
                (head_gain[:, 0:4, :].rearrange("p a d -> p (a d)"),
                 a["nsa_qk_gain"][0].rearrange("a d -> (a d)").partition_broadcast(P)),
                (head_gain[:, 4:6, :].rearrange("p a d -> p (a d)"),
                 a["fox_qk_gain"][0].rearrange("a d -> (a d)").partition_broadcast(P)),
                (bias_row[:, 0:24], a["b_nsa_gate"][0].partition_broadcast(P)),
                (bias_row[:, 24:32], a["b_forget"][0].partition_broadcast(P)),
            ]
            for half in range(2):
                h = slice(half * HD, (half + 1) * HD)
                small.append((w2[h, :, h], a["cmp_w2"][0].rearrange("c e f -> e c f")))
            for l in range(2):
                small += [
                    (wr[:, l, :, 0:NG], a["w_router_group"][l].rearrange("(k p) n -> p k n", p=P)),
                    (wr[:, l, :, NG:NG + NE], a["w_router_expert"][l].rearrange("(k p) n -> p k n", p=P)),
                    (router_bias[:, l, 0:NG], a["b_router_group"][l].partition_broadcast(P)),
                    (router_bias[:, l, NG:NG + NE], a["b_router_expert"][l].partition_broadcast(P)),
                ]
            eng.wait_ge(S["w2_zeroed"], 1)
            for dst, src in small + gdn_loads():
                eng.dma_start(dst, src).then_inc(S["small_landed"], 16)

            norm_act(eng, 0, "mix")
            for j in range(0, 12, 2):
                c0, w = chunks0[j // 2]
                eng.wait_ge(S["proj_done"], j + 1)
                if c0 == 1024:
                    eng.activation(proj[:, 0, FORGET0:FORGET0 + 8], bank[j % 4][:, 280:288], ACT.Copy).then_inc(
                        S["forget_out"], 1)
                eng.activation(proj[:, 0, c0:c0 + w], bank[j % 4][:, 0:w], ACT.Copy).then_inc(S["proj_out_act"], 1)
                if j == 4:
                    eng.wait_ge(S["proj_out_dve"], 3)
                    eng.wait_ge(S["proj_out_act"], 3)
                    for s0, d0, w in ((0, 0, 512), (768, 512, 128), (1024, 640, 128)):
                        eng.activation(squares[:, :, d0:d0 + w], proj[:, :, s0:s0 + w], ACT.Square).then_inc(
                            S["squared_nsa"], 1)
                if j == 8:
                    eng.wait_ge(S["gelu_arg"], 1)
                    eng.activation(hu[:], hu[:], ACT.Exp, scale=-2.0 * 0.7978845608028654).then_inc(S["gelu_exp"], 1)
            eng.wait_ge(S["gate_arg"], 2)
            eng.activation(gate_tmp[:], gate_tmp[:], ACT.Exp, scale=-1.0).then_inc(S["gate_exp"], 1)
            eng.wait_ge(S["gate_plus1"], 1)
            eng.activation(logf[:], gate_tmp[:, :, 24:32], ACT.Ln).then_inc(S["forget_ln"], 1)
            eng.wait_ge(S["summed_nsa"], 1)
            eng.wait_ge(S["proj_out_act"], 5)
            eng.wait_ge(S["proj_out_dve"], 5)
            eng.activation(squares[:, :, :], proj[:, :, FQ0:FQ0 + 1024], ACT.Square).then_inc(S["squared_fox"], 1)
            for g in range(0, 8, 2):
                eng.wait_ge(S["heads_turned"], g + 1)
                eng.activation(headT[:, 2 * g:2 * g + 2, :].rearrange("p a t -> p (a t)"), bank[g % 4][:],
                               ACT.Copy).then_inc(S["heads_out_act"], 1)
            eng.wait_ge(S["cmp_shifted"], 1)
            eng.activation(cmp_e, cmp_s, ACT.Exp, scale=SCALE).then_inc(S["cmp_exp"], 1)

            def turned_out(u):
                eng.wait_ge(S["probs_turned"], u + 1)
                if u >= 2:
                    eng.wait_ge(S["unit_out"], u - 1)
                eng.activation(probsT[:, u % 2, :], bank[2 + u % 2][:, 0:384], ACT.Copy).then_inc(
                    S["probsT_ready"], 1)

            for u in range(UNITS):
                eng.wait_ge(S["masked"], TT * (u + 1))
                if u >= 2:
                    eng.wait_ge(S["probs_turned"], u - 1)
                for t, (c0, c1) in enumerate(((0, P), (P, 3 * P))):
                    eng.activation(probs[:, u % 2, c0:c1], negs[:, u % 2, c0:c1], ACT.Exp,
                                   bias=neg_max[:, u, t:t + 1], scale=-1.0,
                                   accum_out=sums[:, u, t:t + 1]).then_inc(S["probs_ready"], 1)
                if u == 3:
                    eng.wait_ge(S["cmp_turned"], 1)
                    eng.activation(cmp_pT, bank[7][:], ACT.Copy).then_inc(S["cmp_pT_ready"], 1)
                if u >= 1:
                    turned_out(u - 1)
            turned_out(UNITS - 1)
            turn_out_act(eng, 0)
            norm_act(eng, 0, "ffn")
            moe_act(eng, 0)
            if LAYERS > 1:
                norm_act(eng, 1, "mix")
                gdn_act(eng)
                norm_act(eng, 1, "ffn")
                moe_act(eng, 1)

        @block.tensor
        def _(pe):
            pe.wait_ge(S["small_landed"], 16 * N_SMALL)
            pe.transpose(bank[4][:, 0:32], gain_rows[:, :], ident[0:32, 0:32])
            for c in range(2):
                last = pe.transpose(bank[4][:, 64 + 32 * c:96 + 32 * c],
                                    pe_rows[:, c, :, :].rearrange("l a d -> l (a d)"), ident[0:32, 0:32])
            last.then_inc(S["small_turned"], 1)
            norm_pe(pe, 0, "mix")

            def project_chunk(c):
                n = 2 + c
                s, w = n % SLOTS, (288 if chunks0[c][0] == 1024 else 512)
                pe.wait_ge(landed[s], 16 * (n // SLOTS + 1))
                if w == 288:
                    pe.wait_ge(S["forget_landed"], 16)
                for t in range(TT):
                    j = 2 * c + t
                    if j >= 4:
                        pe.wait_ge(S["proj_out_dve" if t else "proj_out_act"], c - 1)
                    for k in range(KT):
                        last = pe.matmul(bank[j % 4][:, 0:w], hT[:, k, t * P:(t + 1) * P], by_k(s)[:, k, 0:w],
                                         start=(k == 0), stop=(k == KT - 1))
                    last.then_inc(S["proj_done"], 1)

            for c in range(6):
                project_chunk(c)
                if c == 1:
                    pe.wait_ge(S["proj_out_act"], 1)
                    pe.wait_ge(S["proj_out_dve"], 1)
                    for kv in range(2):
                        for t in range(TT):
                            last = pe.transpose(bank[5][:, kv * T + t * P:kv * T + (t + 1) * P],
                                                proj[:, t, 512 + kv * P:640 + kv * P], ident)
                    last.then_inc(S["raw_turned"], 1)
                if c == 3:
                    pe.wait_ge(S["cmp_half_landed"], 32)
                    pe.wait_ge(S["pe_added"], 4)
                    for kv in range(2):
                        pe.wait_ge(landed[kv], 16)
                        for l in range(CMP_BLOCK):
                            half, r = divmod(l, CMP_STRIDE)
                            rhs = pe_in[:, kv, half, :].rearrange("p (n r) -> p n r", r=CMP_STRIDE)[
                                :, half:half + NCMP, r]
                            last = pe.matmul(bank[6][:, 32 * kv:32 * kv + NCMP], ring[:, kv, l * P:(l + 1) * P], rhs,
                                             start=(l == 0), stop=(l == CMP_BLOCK - 1))
                        last.then_inc(S["hidden_done"], 1)
                if c == 4:
                    pe.wait_ge(S["gelu_done"], 2)
                    pe.matmul(bank[7][0:NC, 0:P], hg[:, 0, 0, :], w2[:, 0, :], start=True, stop=True)
                    pe.matmul(bank[7][:, P:2 * P], hg[:, 1, :, :].rearrange("p g n -> p (g n)"), w2[:, 1, :],
                              start=True, stop=True).then_inc(S["cmp_kv_done"], 1)
            pe.wait_ge(S["kc_ready"], 1)
            for hk in range(NKV):
                last = pe.transpose(bank[5][:, hk * NC:(hk + 1) * NC],
                                    kcn[:, hk, :, :].rearrange("n a d -> n (a d)"), ident[0:NC, 0:NC])
            last.then_inc(S["kc_turned"], 1)
            pe.wait_ge(S["logf_ready"], 1)
            upto = table("upto")
            pe.matmul(bank[6][:, 0:8], upto, logf[:, 0, :], start=True, stop=True)
            pe.matmul(bank[6][0:NH, 256:384], logf[:, 0, :], upto, start=True, stop=True)
            pe.matmul(bank[6][0:NH, 384:512], logf[:, 0, :], ones, start=True, stop=False)
            pe.matmul(bank[6][0:NH, 384:512], logf[:, 1, :], upto, start=False, stop=True).then_inc(S["cum_done"], 1)
            for g in range(8):
                if g < 4:
                    pe.wait_ge(S["roped"], 3)
                    pe.wait_ge(S["proj_out_dve"], 6)
                    pe.wait_ge(S["proj_out_act"], 6)
                else:
                    pe.wait_ge(S["fox_normed"], 1)
                    pe.wait_ge(S["heads_out_dve" if g % 2 else "heads_out_act"], (g - 4) // 2 + 1)
                for i in range(2):
                    m = 2 * g + i
                    for t in range(TT):
                        if m < 4:
                            src = normed[:, t, 2 * m:2 * m + 2, :].rearrange("p a d -> p (a d)")
                        elif m < 8:
                            src = kdup[:, t, m - 4, :, :].rearrange("p a d -> p (a d)")
                        else:
                            src = normed[:, t, 2 * m - 4:2 * m - 2, :].rearrange("p a d -> p (a d)")
                        last = pe.transpose(bank[g % 4][:, i * T + t * P:i * T + (t + 1) * P], src, ident)
                last.then_inc(S["heads_turned"], 1)
            pe.wait_ge(S["heads_out_act"], 4)
            pe.wait_ge(S["heads_out_dve"], 4)
            pe.wait_ge(S["kcT_ready"], 1)
            pe.wait_ge(S["cum_ready"], 3)
            for par in range(2):
                rows = slice(par * HD, (par + 1) * HD)
                for t in range(TT):
                    for i in range(GROUP):
                        h = 2 * i + par
                        last = pe.matmul(bank[6 + par][:, (t * GROUP + i) * NC:(t * GROUP + i + 1) * NC],
                                         headT[rows, h // 2, t * P:(t + 1) * P], kcT[rows, h // GROUP, :],
                                         start=True, stop=True)
            last.then_inc(S["cmp_scored"], 1)

            def score(u):
                b, h, q, k, _ = unit(u)
                rows = slice((h % 2) * HD, (h % 2 + 1) * HD)
                if u >= 2:
                    pe.wait_ge(S["masked"], TT * (u - 1))
                for t, (c0, n) in enumerate(((0, P), (P, 2 * P))):
                    o = bank[u % 2][:, c0:c0 + n]
                    last = pe.matmul(o, headT[rows, q, t * P:(t + 1) * P], headT[rows, k, 0:n],
                                     start=True, stop=(b < 2))
                    if b == 2:
                        row = spread(h)
                        pe.matmul(o, row, cumk[:, 0:n], start=False, stop=False)
                        for m in range(n // P):
                            last = pe.matmul(bank[u % 2][:, c0 + m * P:c0 + (m + 1) * P],
                                             cumq[:, t * P:(t + 1) * P], row, start=False, stop=(m == n // P - 1))
                last.then_inc(S["scored"], 1)

            def turn(u):
                pe.wait_ge(S["probs_ready"], TT * (u + 1))
                if u >= 2:
                    pe.wait_ge(S["probsT_ready"], u - 1)
                for m in range(3):
                    last = pe.transpose(bank[2 + u % 2][:, m * P:(m + 1) * P], probs[:, u % 2, m * P:(m + 1) * P],
                                        ident)
                last.then_inc(S["probs_turned"], 1)

            def attend(u):
                b, h, _, _, v0 = unit(u)
                if h == 0 and b:
                    pe.wait_ge(S["mix_read"], b)
                pe.wait_ge(S["probsT_ready"], u + 1)
                o0 = 4 + 2 * (b % 2)
                pe.matmul(bank[o0][:, h * HD:(h + 1) * HD], probsT[:, u % 2, 0:P], proj[:, 0, v0:v0 + HD],
                          start=True, stop=True)
                for t in range(TT):
                    last = pe.matmul(bank[o0 + 1][:, h * HD:(h + 1) * HD], probsT[:, u % 2, (t + 1) * P:(t + 2) * P],
                                     proj[:, t, v0:v0 + HD], start=(t == 0), stop=(t == 1))
                last.then_inc(S["unit_out"], 1)

            for i in range(UNITS + 2):
                if i < UNITS:
                    score(i)
                if 1 <= i <= UNITS:
                    turn(i - 1)
                if i >= 2:
                    attend(i - 2)
                if i == 2:
                    pe.wait_ge(S["cmp_probs"], 1)
                    for t in range(TT):
                        for hk in range(NKV):
                            last = pe.transpose(bank[7][:, (t * 2 + hk) * P:(t * 2 + hk + 1) * P],
                                                cmp_s[:, hk, t, :, :].rearrange("p h n -> p (h n)"), ident)
                    last.then_inc(S["cmp_turned"], 1)
                if i == 5:
                    pe.wait_ge(S["cmp_pT_ready"], 1)
                    for t in range(TT):
                        for hk in range(NKV):
                            last = pe.matmul(bank[6 + t][:, hk * 256:(hk + 1) * 256],
                                             cmp_pT[:, (t * 2 + hk) * P:(t * 2 + hk + 1) * P],
                                             vblock[:, hk, :, :].rearrange("p g d -> p (g d)"), start=True, stop=True)
                    last.then_inc(S["cmp_out"], 1)
            out_product(pe, mixed, OUT0, 0)
            norm_pe(pe, 0, "ffn")
            moe_pe(pe, 0)
            if LAYERS > 1:
                norm_pe(pe, 1, "mix")
                gdn_pe(pe)
                norm_pe(pe, 1, "ffn")
                moe_pe(pe, 1)

        @block.vector
        def _(eng):
            chain = Chain(eng, S["dve_chain"])
            eng.memset(hx[:], 0.0).then_inc(S["hx_zeroed"], 1)
            eng.wait_ge(S["small_landed"], 16 * N_SMALL)
            eng.wait_ge(S["small_turned"], 1)
            eng.tensor_copy(peT[:].rearrange("p a l -> p (a l)"), bank[4][:, 64:128]).then_inc(S["peT_ready"], 1)
            eng.tensor_copy(gainT[:], bank[4][:, 0:32]).then_inc(S["gain_ready"], 1)
            eng.wait_ge(S["gain_ready"], 1)
            eng.wait_ge(S["peT_ready"], 1)
            norm_dve(eng, chain, 0, "mix")

            def project_out(c):
                c0, w = chunks0[c]
                j = 2 * c + 1
                eng.wait_ge(S["proj_done"], j + 1)
                if c0 == 1024:
                    eng.tensor_copy(proj[:, 1, FORGET0:FORGET0 + 8], bank[j % 4][:, 280:288]).then_inc(
                        S["forget_out"], 1)
                eng.tensor_copy(proj[:, 1, c0:c0 + w], bank[j % 4][:, 0:w]).then_inc(S["proj_out_dve"], 1)

            def head_scales(h0, n, w):
                view = squares[:, :, 0:n * HD].rearrange("p t (h d) -> p t h d", d=HD)
                sums_ = ss[:, 0:TT * n].rearrange("p (t h) -> p t h", t=TT)
                ins = eng.tensor_reduce(sums_, view, AX.X, ALU.add)
                chain(ins)
                inverse_root(eng, f"heads{n}", rstd[:, 0:TT * n], ss[:, 0:TT * n], 1.0 / HD)
                return rstd[:, 0:TT * n].rearrange("p (t h) -> p t h", t=TT)

            def by_heads(c0, n):
                return proj[:, :, c0:c0 + n * HD].rearrange("p t (h d) -> p t h d", d=HD)

            def wide(v, shape):
                return v.to_broadcast(shape)

            def scale_heads(r, groups):
                for c0, h0, n, g in groups:
                    o = normed[:, :, h0:h0 + n, :]
                    r0 = h0 if h0 < 12 else h0 - 12
                    chain(eng.tensor_tensor(o, by_heads(c0, n),
                                            r[:, :, r0:r0 + n].unsqueeze(3).to_broadcast([P, TT, n, HD]), ALU.mult))
                    chain(eng.tensor_tensor(o, o, head_gain[:, g, :].unsqueeze(1).unsqueeze(1).to_broadcast(
                        [P, TT, n, HD]), ALU.mult))

            for c in range(3):
                project_out(c)
                if c == 1:
                    eng.wait_ge(S["raw_turned"], 1)
                    for kv in range(2):
                        for half in range(2):
                            eng.tensor_tensor(
                                pe_in[:, kv, half, :].rearrange("p (n r) -> p n r", r=CMP_STRIDE),
                                bank[5][:, kv * T:(kv + 1) * T].rearrange("p (n r) -> p n r", r=CMP_STRIDE),
                                peT[:, kv, half * 16:half * 16 + 16].unsqueeze(1).to_broadcast([P, 16, 16]),
                                ALU.add).then_inc(S["pe_added"], 1)
            eng.wait_ge(S["squared_nsa"], 3)
            r = head_scales(0, 12, 0)
            eng.tensor_copy(rs[:, 7, 0:1], rstd[:, 0:1]).then_inc(S["summed_nsa"], 1)
            scale_heads(r, [(0, 0, 8, 0), (768, 8, 2, 2), (1024, 10, 2, 3)])
            project_out(3)
            half = HD // 2
            cos = table("cos").rearrange("p (t d) -> p t d", t=TT)
            sin = table("sin").rearrange("p (t d) -> p t d", t=TT)
            rot, _ = cut(0, TT, 12, HD)
            q = normed[:, :, 0:12, :]
            chain(eng.tensor_tensor(rot[:, :, :, 0:half], q[:, :, :, half:HD],
                                    sin[:, :, 0:half].unsqueeze(2).to_broadcast([P, TT, 12, half]), ALU.mult))
            chain(eng.tensor_tensor(rot[:, :, :, half:HD], q[:, :, :, 0:half],
                                    sin[:, :, half:HD].unsqueeze(2).to_broadcast([P, TT, 12, half]), ALU.mult))
            chain(eng.tensor_tensor(q, q, cos.unsqueeze(2).to_broadcast([P, TT, 12, HD]), ALU.mult))
            eng.tensor_tensor(normed[:, :, 0:8, :], normed[:, :, 0:8, :], rot[:, :, 0:8, :], ALU.add).then_inc(
                S["roped"], 1)
            for d in range(2):
                eng.tensor_tensor(kdup[:, :, :, d, :], normed[:, :, 8:12, :], rot[:, :, 8:12, :], ALU.add).then_inc(
                    S["roped"], 1)
            eng.wait_ge(S["roped"], 3)
            eng.tensor_copy(rs[:, 7, 0:1], rstd[:, 0:1]).then_inc(S["summed_nsa2"], 1)
            project_out(4)
            eng.wait_ge(S["hidden_done"], 2)
            eng.wait_ge(S["hx_zeroed"], 1)
            chain(eng.tensor_copy(hx[:, :, 0:NCMP],
                                  bank[6][:, 0:64].rearrange("p (a n) -> p a n", a=2)[:, :, 0:NCMP]))
            chain(eng.tensor_tensor(hu[:], hx[:], hx[:], ALU.mult))
            chain(eng.tensor_scalar(hu[:], hu[:], 0.044715, 1.0, ALU.mult, ALU.add))
            eng.tensor_tensor(hu[:], hu[:], hx[:], ALU.mult).then_inc(S["gelu_arg"], 1)
            eng.wait_ge(S["gelu_exp"], 1)
            chain(eng.tensor_scalar(hu[:], hu[:], 1.0, None, ALU.add))
            chain(eng.reciprocal(hu[:], hu[:]))
            for kv in range(2):
                eng.tensor_tensor(hg[:, kv, :, :], hx[:, kv, :].unsqueeze(1).to_broadcast([P, GROUP, NC]),
                                  hu[:, kv, :].unsqueeze(1).to_broadcast([P, GROUP, NC]), ALU.mult).then_inc(
                                      S["gelu_done"], 1)
            eng.wait_ge(S["forget_out"], 2)
            for c0, n, d0 in ((GATE0, 24, 0), (FORGET0, 8, 24)):
                chain(eng.tensor_tensor(gate[:, :, d0:d0 + n], proj[:, :, c0:c0 + n],
                                        bias_row[:, d0:d0 + n].unsqueeze(1).to_broadcast([P, TT, n]), ALU.add))
            eng.tensor_copy(gate_tmp[:, :, 0:24], gate[:, :, 0:24]).then_inc(S["gate_arg"], 1)
            eng.scalar_tensor_tensor(gate_tmp[:, :, 24:32], gate[:, :, 24:32], -1.0, gate[:, :, 24:32],
                                     ALU.mult, ALU.max).then_inc(S["gate_arg"], 1)
            project_out(5)
            eng.wait_ge(S["gate_exp"], 1)
            eng.tensor_scalar(gate_tmp[:], gate_tmp[:], 1.0, None, ALU.add).then_inc(S["gate_plus1"], 1)
            eng.wait_ge(S["gate_plus1"], 1)
            chain(eng.reciprocal(gate[:, :, 0:24], gate_tmp[:, :, 0:24]))
            eng.wait_ge(S["forget_ln"], 1)
            eng.scalar_tensor_tensor(logf[:], gate[:, :, 24:32], 0.0, logf[:], ALU.min, ALU.subtract).then_inc(
                S["logf_ready"], 1)
            eng.wait_ge(S["cmp_kv_done"], 1)
            kc = kct[:, 0, :, :]
            chain(eng.tensor_copy(kc, bank[7][0:NC, 0:P].rearrange("p (h d) -> p h d", h=2)))
            chain(eng.tensor_tensor(vblock[:], bank[7][:, P:2 * P].rearrange("p (h d) -> p h d", h=2).unsqueeze(
                2).to_broadcast([P, 2, GROUP, HD]), table("block_diag").rearrange("p (g d) -> p g d", g=GROUP)
                .unsqueeze(1).to_broadcast([P, 2, GROUP, HD]), ALU.mult))
            chain(eng.tensor_tensor(kct[:, 1, :, :], kc, kc, ALU.mult))
            s_, r_ = ss[0:NC, 60:62], rstd[0:NC, 60:62]
            chain(eng.tensor_reduce(s_, kct[:, 1, :, :], AX.X, ALU.add))
            inverse_root(eng, "kc", r_, s_, 1.0 / HD)
            chain(eng.tensor_tensor(kc, kc, r_.unsqueeze(2).to_broadcast([NC, 2, HD]), ALU.mult))
            chain(eng.tensor_tensor(kc, kc, head_gain[0:NC, 1, :].unsqueeze(1).to_broadcast([NC, 2, HD]), ALU.mult))
            ccos, csin = table("cmp_cos", NC), table("cmp_sin", NC)
            chain(eng.tensor_tensor(kct[:, 1, :, 0:half], kc[:, :, half:HD],
                                    csin[:, 0:half].unsqueeze(1).to_broadcast([NC, 2, half]), ALU.mult))
            chain(eng.tensor_tensor(kct[:, 1, :, half:HD], kc[:, :, 0:half],
                                    csin[:, half:HD].unsqueeze(1).to_broadcast([NC, 2, half]), ALU.mult))
            chain(eng.tensor_tensor(kct[:, 2, :, :], kc, ccos.unsqueeze(1).to_broadcast([NC, 2, HD]), ALU.mult))
            for d in range(2):
                last = eng.tensor_tensor(kcn[:, :, d, :], kct[:, 1, :, :], kct[:, 2, :, :], ALU.add)
                if d == 0:
                    chain(last)
            last.then_inc(S["kc_ready"], 1)
            eng.wait_ge(S["squared_fox"], 1)
            r = head_scales(12, 16, 0)
            scale_heads(r, [(FQ0, 12, 8, 4), (FQ0 + 512, 20, 8, 5)])
            eng.tensor_copy(rs[:, 7, 0:1], rstd[:, 0:1]).then_inc(S["fox_normed"], 1)
            eng.wait_ge(S["kc_turned"], 1)
            eng.tensor_copy(kcT[:].rearrange("p a n -> p (a n)"), bank[5][:, 0:2 * NC]).then_inc(S["kcT_ready"], 1)
            for g in range(1, 8, 2):
                eng.wait_ge(S["heads_turned"], g + 1)
                eng.tensor_copy(headT[:, 2 * g:2 * g + 2, :].rearrange("p a t -> p (a t)"), bank[g % 4][:]).then_inc(
                    S["heads_out_dve"], 1)
            eng.memset(work[:, normed_at + 2304:normed_at + 2304 + 2 * T], 0.0).then_inc(S["cum_ready"], 1)
            eng.wait_ge(S["cum_ready"], 1)
            eng.wait_ge(S["cum_done"], 1)
            eng.tensor_scalar(cumk[0:NH, :], bank[6][0:NH, 256:512], -8.0, None, ALU.mult).then_inc(S["cum_ready"], 1)
            eng.tensor_scalar(cumq[0:NH, :], bank[6][0:NH, 256:512], 8.0, None, ALU.mult).then_inc(S["cum_ready"], 1)
            eng.wait_ge(S["cmp_scored"], 1)
            bias = table("cmp_bias").rearrange("p (t n) -> p t n", t=TT).unsqueeze(2).to_broadcast([P, TT, GROUP, NC])
            valid = table("cmp_valid").rearrange("p (t n) -> p t n", t=TT).unsqueeze(2).to_broadcast([P, TT, GROUP, NC])
            for par in range(2):
                chain(eng.tensor_tensor(cmp_s[:, par], bank[6 + par][:, 0:256].rearrange(
                    "p (t h n) -> p t h n", t=TT, h=GROUP), bias, ALU.add))
            flat_s = work[:, 0:512].rearrange("p (m n) -> p m n", n=NC)
            flat_e = work[:, 512:1024].rearrange("p (m n) -> p m n", n=NC)
            chain(eng.tensor_reduce(cmp_m[:], flat_s, AX.X, ALU.max))
            eng.tensor_tensor(flat_s, flat_s, cmp_m[:].unsqueeze(2).to_broadcast([P, 16, NC]), ALU.subtract).then_inc(
                S["cmp_shifted"], 1)
            eng.wait_ge(S["cmp_exp"], 1)
            chain(eng.tensor_reduce(cmp_m[:], flat_e, AX.X, ALU.add))
            chain(eng.reciprocal(cmp_r[:], cmp_m[:]))
            for par in range(2):
                chain(eng.tensor_tensor(cmp_e[:, par], cmp_e[:, par], valid, ALU.mult))
            r16 = cmp_r[:].rearrange("p (a t h) -> p a t h", a=2, t=TT)
            for par in range(2):
                for hk in range(NKV):
                    last = eng.tensor_tensor(
                        cmp_s[:, hk, :, par:GROUP:2, :], cmp_e[:, par, :, 2 * hk:2 * hk + 2, :],
                        r16[:, par, :, 2 * hk:2 * hk + 2].unsqueeze(3).to_broadcast([P, TT, 2, NC]), ALU.mult)
                    if (par, hk) != (1, 1):
                        chain(last)
            last.then_inc(S["cmp_probs"], 1)

            causal = table("causal")

            def mask(u):
                eng.wait_ge(S["scored"], u + 1)
                if u >= 2:
                    eng.wait_ge(S["probs_ready"], TT * (u - 1))
                for t, (c0, c1, m0) in enumerate(((0, P, P), (P, 3 * P, 0))):
                    eng.tensor_tensor_reduce(negs[:, u % 2, c0:c1], bank[u % 2][:, c0:c1], causal[:, m0:2 * P],
                                             -SCALE, BIG, ALU.add, ALU.min,
                                             neg_max[:, u, t:t + 1]).then_inc(S["masked"], 1)

            def mix(b):
                u0 = b * NH
                eng.wait_ge(S["unit_out"], u0 + NH)
                f = factor[:, u0:u0 + NH, :]
                chain(eng.reciprocal(f, sums[:, u0:u0 + NH, :]))
                o0 = 4 + 2 * (b % 2)
                if b < 2:
                    g = gate[:, :, 0:24].rearrange("p t (h c) -> p t h c", c=3)[:, :, :, b + 1].rearrange(
                        "p t h -> p h t")
                    chain(eng.tensor_tensor(f, f, g, ALU.mult))
                for t in range(TT):
                    src = bank[o0 + t][:].rearrange("p (h d) -> p h d", d=HD)
                    fb = f[:, :, t].unsqueeze(2).to_broadcast([P, NH, HD])
                    if b < 2:
                        chain(eng.tensor_tensor(mix_tmp.rearrange("p (h d) -> p h d", d=HD), src, fb, ALU.mult))
                        if t == 1:
                            eng.tensor_copy(rs[:, 7, 0:1], rstd[:, 0:1]).then_inc(S["mix_read"], 1)
                        ins = eng.tensor_tensor(mixed[:, t, 0:512], mixed[:, t, 0:512], mix_tmp, ALU.add)
                        if b == 1:
                            ins.then_inc(S["mixed_ready"], 1)
                            eng.wait_ge(S["mixed_ready"], t + 1)
                        else:
                            chain(ins)
                    else:
                        eng.tensor_tensor(mixed[:, t, 512:1024].rearrange("p (h d) -> p h d", d=HD), src, fb,
                                          ALU.mult).then_inc(S["mixed_ready"], 1)

            for u in range(UNITS):
                mask(u)
                if u == 7:
                    eng.wait_ge(S["cmp_out"], 1)
                    for t in range(TT):
                        g = gate[:, t, 0:24].rearrange("p (h c) -> p h c", c=3)[:, :, 0]
                        chain(eng.tensor_tensor(mixed[:, t, 0:512].rearrange("p (h d) -> p h d", d=HD),
                                                bank[6 + t][:].rearrange("p (h d) -> p h d", d=HD),
                                                g.unsqueeze(2).to_broadcast([P, NH, HD]), ALU.mult))
                    eng.tensor_copy(rs[:, 7, 0:1], rstd[:, 0:1]).then_inc(S["mix_read"], 1)
                if u == 10:
                    mix(0)
                if u == 18:
                    mix(1)
            mix(2)
            turn_out_dve(eng, 0)
            add_product(eng, 0)
            norm_dve(eng, chain, 0, "ffn")
            moe_dve(eng, chain, 0)
            if LAYERS > 1:
                norm_dve(eng, chain, 1, "mix")
                gdn_dve(eng, chain)
                norm_dve(eng, chain, 1, "ffn")
                moe_dve(eng, chain, 1)


INPUTS = ["x", "norm_mix", "norm_ffn", "w_in_even", "b_nsa_gate", "b_forget", "cmp_pe", "cmp_w1", "cmp_w2",
          "nsa_qk_gain", "fox_qk_gain", "w_out_even", "w_in_odd", "conv_w", "a_log", "dt_bias", "gdn_norm_gain",
          "w_out_odd", "w_router_group", "b_router_group", "w_router_expert", "b_router_expert",
          "w_expert_in", "w_expert_out"]


def program(nc, arrays, debug=()):
    a = {n: nc.dram_tensor(f"in_{n}", v.shape, F32, kind="ExternalInput").ap() for n, v in arrays.items()}
    out = nc.dram_tensor("out", (1, T, D), F32, kind="ExternalOutput").ap()
    build(nc, a, out)


def kernel(**inputs):
    from concourse.bacc import Bacc
    from concourse.bass_utils import run_bass_kernel_spmd

    arrays = {n: np.ascontiguousarray(inputs[n]) for n in INPUTS}
    arrays["tables"] = np.concatenate(list(constant_tables().values()), 1)
    nc = Bacc("TRN2", target_bir_lowering=False, num_devices=1)
    program(nc, arrays)
    r = run_bass_kernel_spmd(nc, [{f"in_{n}": v for n, v in arrays.items()}], core_ids=[0])
    return r.results[0]["out"]
```

```python
from contextlib import ExitStack

import numpy as np

import concourse.bass as bass
from concourse import mybir

F32 = mybir.dt.float32
BF16 = mybir.dt.bfloat16
ALU = mybir.AluOpType
ACT = mybir.ActivationFunctionType
AX = mybir.AxisListType

P = 128
D = 1024
T = 256
TT = T // P
KT = D // P
HD = 64
NH = 8
NKV = 2
GROUP = NH // NKV
CMP_BLOCK, CMP_STRIDE = 32, 16
NCMP = (T - CMP_BLOCK) // CMP_STRIDE + 1
NC = 32
EVEN_IN = 2848
GATE0, FQ0, FORGET0 = 1280, 1304, 2840
GH, GD = 8, 128
CHUNK = 64
CONV = 4
NG, EPG, NE, FF = 4, 4, 16, 256
EPS = 1e-6
BIG = 1e30
SCALE = HD ** -0.5

SLOTS = 6
SLOT = 4096
MOE_STEP = 4
CAP = 64
PAIRS = NE // 2
LEVELS = [1, 2, 4, 8, 16, 32]
LAYERS = 2


def constant_tables():
    t = np.arange(P)
    tab = {}
    tab["ident"] = np.eye(P)
    tab["ones"] = np.ones((P, P))
    tab["minus_half"] = np.full((P, 1), -0.5)
    tri = np.where(t[None, :] <= t[:, None], 0.0, -BIG)
    tab["causal"] = np.concatenate([np.zeros((P, P)), tri], 1)
    end = np.arange(NC) * CMP_STRIDE + CMP_BLOCK - 1
    tok = np.arange(T).reshape(TT, P)
    ok = (end[None, None, :] <= tok[:, :, None]) & (np.arange(NC) < NCMP)[None, None, :]
    ok = ok.transpose(1, 0, 2)
    tab["cmp_bias"] = np.where(ok, 0.0, -BIG).reshape(P, -1)
    tab["cmp_valid"] = ok.astype(np.float32).reshape(P, -1)
    half = HD // 2
    freq = (np.float32(10000.0) ** (-np.arange(half, dtype=np.float32) / half)).astype(np.float32)

    def rope(pos):
        ang = pos.astype(np.float32)[..., None] * freq
        c, s = np.cos(ang), np.sin(ang)
        return np.concatenate([c, c], -1), np.concatenate([-s, s], -1)

    c, s = rope(tok.T)
    tab["cos"], tab["sin"] = c.reshape(P, -1), s.reshape(P, -1)
    c, s = rope(np.concatenate([end[:NCMP], np.zeros(P - NCMP)]))
    tab["cmp_cos"], tab["cmp_sin"] = c, s
    tab["upto"] = (t[:, None] <= t[None, :]).astype(np.float32)
    tab["block_diag"] = np.kron(np.eye(GROUP), np.ones((NC, HD)))
    tab["rank"] = np.broadcast_to(NE - np.arange(NE), (P, NE))
    same = t[:, None] // CHUNK == t[None, :] // CHUNK
    tab["slot"] = np.broadcast_to(np.arange(CAP), (P, CAP))
    tab["chunk_upto"] = (same & (t[:, None] <= t[None, :])).astype(np.float32)
    tab["chunk_bias"] = np.concatenate([np.where(same & (t[:, None] < t[None, :]), 0.0, -BIG),
                                        np.where(same & (t[:, None] <= t[None, :]), 0.0, -BIG)], 1)
    last = (t // CHUNK) * CHUNK + CHUNK - 1
    tab["chunk_last"] = (t[:, None] == last[None, :]).astype(np.float32)
    for lv in LEVELS:
        m = (t[:, None] // (2 * lv) == t[None, :] // (2 * lv)) & ((t[:, None] // lv) % 2 == 0) & ((t[None, :] // lv) % 2 == 1)
        tab[f"level{lv}"] = m.astype(np.float32)
    return {k: np.ascontiguousarray(v, np.float32) for k, v in tab.items()}


def table_columns():
    at, out = 0, {}
    for k, v in constant_tables().items():
        out[k] = (at, v.shape[1])
        at += v.shape[1]
    return out, at


class Chain:

    def __init__(self, eng, sem):
        self.eng, self.sem, self.n = eng, sem, 0

    def __call__(self, ins):
        ins.then_inc(self.sem, 1)
        self.n += 1
        self.eng.wait_ge(self.sem, self.n)


class Signals(dict):

    def __init__(self, nc, ctx):
        self.nc, self.ctx = nc, ctx

    def __missing__(self, name):
        self[name] = self.ctx.enter_context(self.nc.semaphore(name))
        return self[name]


def build(nc, a, out):
    cols, width = table_columns()
    ctx = ExitStack()
    with ctx:
        def sb(name, shape, dt=F32):
            return ctx.enter_context(nc.sbuf_tensor(name, shape, dt))

        S = Signals(nc, ctx)
        bank = [ctx.enter_context(nc.psum_tensor(f"bank{i}", [P, 512], F32)) for i in range(8)]

        ring = sb("ring", [P, SLOTS, SLOT])
        const = sb("const", [P, width])
        x = sb("x", [P, TT, D])
        hT = sb("hT", [P, KT, T])
        gain_rows = sb("gain_rows", [32, P])
        gainT = sb("gainT", [P, 32])
        ss = sb("ss", [P, 64])
        rstd = sb("rstd", [P, 64])
        WORK = 16448
        work = sb("work", [P, WORK])

        def table(name, rows=P):
            at, n = cols[name]
            return const[0:rows, at:at + n]

        ident, ones = table("ident"), table("ones")

        def spread(row):
            return ident[:, row:row + 1].to_broadcast([P, P])

        def cut(at, *shape):
            n = int(np.prod(shape))
            assert at + n <= WORK, (at, shape)
            v = work[:, at:at + n]
            if len(shape) > 1:
                names = "abcd"[:len(shape)]
                v = v.rearrange(f"p ({' '.join(names)}) -> p {' '.join(names)}", **dict(zip(names, shape)))
            return v, at + n

        xn, at = cut(0, TT, D)
        mixed, _ = cut(0, TT, D)
        proj, at = cut(at, TT, EVEN_IN)
        headT, at = cut(at, 16, T)
        pe_in, _ = cut(at - 16 * T, 2, 2, T)
        normed_at = at
        normed, at = cut(at, TT, 28, HD)
        kdup, at = cut(at, TT, 4, 2, HD)
        negs, at2 = cut(normed_at, 2, 384)
        probs, at2 = cut(at2, 2, 384)
        probsT, at2 = cut(at2, 2, 384)
        cumk, at2 = cut(at2, T)
        cumq, at2 = cut(at2, TT, NH)
        mix_tmp, at2 = cut(at2, 512)
        assert at2 <= at
        squares = mixed
        cmp_s, _ = cut(0, 2, TT, GROUP, NC)
        cmp_e, _ = cut(512, 2, TT, GROUP, NC)
        cmp_pT, _ = cut(1024, 512)
        silu_g, at = cut(TT * D, TT, FF)
        act, at = cut(at, TT, FF)
        actT, at = cut(at, TT, 2, P)
        pick, at = cut(at, 2, TT, 2 * CAP)
        weigh, at = cut(at, 2, TT, 2 * CAP)
        picked, at = cut(at, KT, 2 * CAP)
        turned_pair, at = cut(at, 2, 4, P)
        pair_out, at = cut(at, D)

        HH = GH // 2
        qT, at = cut(TT * D, GH, T)
        kT, at = cut(at, GH, T)
        vb, at = cut(at, TT, GH, GD)
        zs, at = cut(at, TT, GH * GD)
        half_at = at
        LA, at = cut(half_at, HH, TT, 2, P)
        Tm, at = cut(at, HH, TT, P)
        TmT_at = at
        TmT, at = cut(at, HH, TT, P)
        X_at = at
        Xm, at = cut(at, HH, TT, P)
        level, at = cut(at, HH, TT, P)
        kbg, _ = cut(TmT_at - HH * TT * P, TT, HH, GD)
        kdec, _ = cut(X_at, TT, HH, GD)
        nwT, _ = cut(X_at + HH * TT * P, TT, HH, P)
        conv_v, _ = cut(half_at, 2, T)
        conv_sq, _ = cut(half_at + 2 * T, 2, T)
        hT_flat = hT[:].rearrange("p k t -> p (k t)")
        decay = hT_flat[:, 0:1024].rearrange("p (b t c i) -> p b t c i", b=2, t=TT, c=2)
        state = hT_flat[:, 1024:1536].rearrange("p (h d) -> p h d", h=HH)
        v_new = hT_flat[:, 1536:2048].rearrange("p (h d) -> p h d", h=HH)
        squares1 = work[:, half_at:half_at + HH * TT * GD].rearrange("p (t h d) -> p t h d", t=TT, h=HH)
        conv_rows = sb("conv_rows", [CONV * 24, P])
        convT = sb("convT", [P, CONV * 24])
        wab = sb("wab", [P, KT, 2 * GH])
        ab_bias = sb("ab_bias", [P, 2, GH])
        gdn_gain = sb("gdn_gain", [P, GD])
        ab = sb("ab", [P, 6, TT, GH])
        gd = sb("gd", [P, 12, TT, GH])
        lnss = sb("lnss", [P, 2, TT, GH])
        rowT = sb("rowT", [GH, 2, T])
        chunk_decay = sb("chunk_decay", [P, 2, TT, GH])

        pe_rows = sb("pe_rows", [CMP_BLOCK, 2, 2, HD])
        peT = sb("peT", [P, 2, CMP_BLOCK])
        w2 = sb("w2", [P, 2, P])
        hx = sb("hx", [P, 2, NC])
        hu = sb("hu", [P, 2, NC])
        hg = sb("hg", [P, 2, GROUP, NC])
        kcn = sb("kcn", [NC, 2, 2, HD])
        kct = sb("kct", [NC, 3, 2, HD])
        kcT = sb("kcT", [P, 2, NC])
        vblock = sb("vblock", [P, 2, GROUP, HD])
        head_gain = sb("head_gain", [P, 6, HD])
        bias_row = sb("bias_row", [P, 32])
        gate = sb("gate", [P, TT, 32])
        gate_tmp = sb("gate_tmp", [P, TT, 32])
        logf = sb("logf", [P, TT, NH])
        neg_max = sb("neg_max", [P, 24, TT])
        sums = sb("sums", [P, 24, TT])
        factor = sb("factor", [P, 24, TT])
        cmp_m = sb("cmp_m", [P, 2 * TT * GROUP])
        cmp_r = sb("cmp_r", [P, 2 * TT * GROUP])
        wr = sb("wr", [P, 2, KT, NG + NE])
        router_bias = sb("router_bias", [P, 2, NG + NE])
        logits = sb("logits", [P, TT, NG + NE])
        rt = sb("rt", [P, 6, TT, NE])
        rs = sb("rs", [P, 8, TT])
        gates = sb("gates", [P, TT, NE])
        routed = sb("routed", [P, TT, NE])
        place = sb("place", [P, TT, NE])
        crowd = sb("crowd", [P, 2])
        crowded = sb("crowded", [P, 1], mybir.dt.int32)
        zeros = table("causal")[:, 0:P].bitcast(BF16)[:, 0:P]
        finite = table("upto").bitcast(BF16)

        chunks0 = [(512, 512), (0, 512), (1024, 280), (1304, 512), (1816, 512), (2328, 512)]
        CMP0 = 2
        stream = [("in0", c) for c in chunks0]
        stream[CMP0:CMP0] = [("cmp", 0), ("cmp", 1)]
        in0_load = [n for n, (kind, _) in enumerate(stream) if kind == "in0"]
        OUT0 = len(stream)
        stream += [("out0", 0), ("out0", 1)]
        MOE_USES = NE + NE // 2
        MOE = {0: len(stream)}
        IN1 = MOE[0] + MOE_USES
        stream1 = [("in1", c) for c in range(8)] + [("out1", 0), ("out1", 1)]
        OUT1 = IN1 + 8
        MOE[1] = IN1 + len(stream1)
        landed = [S[f"weights_landed{i}"] for i in range(SLOTS)]
        read = {CMP0: ("hidden_done", 1), CMP0 + 1: ("hidden_done", 2)}
        for c, n in enumerate(in0_load):
            read[n] = ("proj_done", TT * (c + 1))
        for l, n0 in ((0, OUT0), (1, OUT1)):
            for c in range(2):
                read[n0 + c] = ("mixed_product", 4 * l + TT * (c + 1))
        for l in range(2):
            for m in range(MOE_USES):
                pair, part = divmod(m, 3)
                read[MOE[l] + m] = (("gu_done1", l * NE + 2 * pair + part + 1) if part < 2
                                    else ("pair_done", l * NE // 2 + pair + 1))
        for c in range(8):
            read[IN1 + c] = ("qkv_done", 4 * (c + 1)) if c < 6 else ("z_done", TT * (c - 5))

        def by_k(s, n=512):
            return ring[:, s, :].rearrange("p (k n) -> p k n", k=KT)[:, :, 0:n]

        def by_f(s):
            return ring[:, s, :].rearrange("p (e f n) -> p e f n", e=2, f=2)

        def unit(u):
            b, h = divmod(u, NH)
            if b == 2:
                return b, h, 8 + h // 2, 12 + h // 2, 2328 + h * HD
            return b, h, h // 2, 4 + 2 * b + h // GROUP, (896 if b == 0 else 1152) + h // GROUP * HD

        UNITS = 3 * NH
        n_small = [0]

        ROOTS = ["mix0", "heads12", "heads16", "kc", "ffn0", "mix1", "o0", "o1", "ffn1"]

        def root_argument(eng, to, of, mean):
            eng.tensor_scalar(to, of, mean, EPS, ALU.mult, ALU.add).then_inc(S["root_arg"], 1)

        def inverse_root(eng, name, to, of, mean):
            root_argument(eng, to, of, mean)
            eng.wait_ge(S["root_ready"], ROOTS.index(name) + 1)

        def root_pool(pool, name, to):
            pool.wait_ge(S["root_arg"], ROOTS.index(name) + 1)
            pool.tensor_tensor(to, to, table("minus_half", to.shape[0]).to_broadcast(list(to.shape)),
                               ALU.pow).then_inc(S["root_ready"], 1)

        def skip(eng, name, n):
            if name == "act_side":
                skip(eng, "pair_silu", n)
                skip(eng, "pair_turned_out", n)
                skip(eng, "pair_out_ready", 2 * n)
            else:
                eng.nop().then_inc(S[name], n)

        def either(eng, l, routed_only, everything):
            eng.wait_ge(S["crowd_known"], l + 1)
            full = eng.value_load(crowded[0:1, 0:1], min_val=0, max_val=1)
            with eng.If(full == 0):
                routed_only()
            with eng.Else():
                everything()

        def nth(l, f):
            return 2 * l + (f == "ffn")

        def norm_act(eng, l, f):
            if (l, f) == (0, "mix"):
                eng.wait_ge(S["x_landed"], 16)
            else:
                eng.wait_ge(S["x_added"], 2 * TT * nth(l, f))
            for t in range(TT):
                if t:
                    eng.wait_ge(S["squared"], TT * nth(l, f) + t)
                eng.activation(hT[:, 4 * t:4 * t + 4, :].rearrange("p k t -> p (k t)"), x[:, t, :], ACT.Square,
                               accum_out=ss[:, t:t + 1]).then_inc(S["squared"], 1)
            g0 = (16 if f == "ffn" else 0) + l * KT
            eng.wait_ge(S["rows_turned_out"], 2)
            for k in (0, 1, 4, 5):
                eng.wait_ge(S["turned"], 4 * nth(l, f) + k // 2 + 1)
                eng.activation(hT[:, k, :], bank[k // 2][:, (k % 2) * T:(k % 2 + 1) * T], ACT.Copy,
                               scale=gainT[:, g0 + k:g0 + k + 1]).then_inc(S["hT_act"], 1)

        def turn_out_act(eng, l):
            for g in (0, 2):
                eng.wait_ge(S["mixed_turned"], 4 * l + g + 1)
                eng.activation(hT[:, 2 * g:2 * g + 2, :].rearrange("p a t -> p (a t)"), bank[g][:],
                               ACT.Copy).then_inc(S["mixedT_act"], 1)

        def moe_act(eng, l):
            eng.wait_ge(S["router_arg"], 2 * l + 1)
            eng.activation(rt[:, 0, :, 0:NG], rt[:, 0, :, 0:NG], ACT.Exp).then_inc(S["router_exp"], 1)
            eng.wait_ge(S["router_arg"], 2 * l + 2)
            eng.activation(rs[:, 1, :], rs[:, 1, :], ACT.Exp).then_inc(S["router_exp"], 1)
            def everything():
                with eng.Fori(0, NE // MOE_STEP) as i:
                    for j in range(MOE_STEP):
                        n = i * MOE_STEP + j
                        for t in range(TT):
                            eng.wait_ge(S[f"gu_done{t}"], l * NE + n + 1)
                            eng.wait_ge(S[f"act_ready{t}"], l * (NE + 1) + n + 1)
                            eng.activation(silu_g[:, t, :], bank[t][:, 0:FF], ACT.Silu).then_inc(
                                S[f"silu_ready{t}"], 1)
                            eng.wait_ge(S[f"act_turned{t}"], l * NE + n + 1)
                            eng.activation(actT[:, t, :, :].rearrange("p f t -> p (f t)"), bank[2 + t][:, 0:2 * P],
                                           ACT.Copy).then_inc(S[f"actT_ready{t}"], 1)
                skip(eng, "act_side", PAIRS)

            def routed_only():
                def pair(p, k):
                    eng.wait_ge(S["gu_done1"], l * NE + 2 * p + 2)
                    eng.activation(silu_g[:, 0, :], bank[2][:, 0:FF], ACT.Silu).then_inc(S["pair_silu"], 1)
                    eng.wait_ge(S["pair_turned"], l * PAIRS + p + 1)
                    eng.activation(turned_pair[:, k].rearrange("p m t -> p (m t)"), bank[3][:],
                                   ACT.Copy).then_inc(S["pair_turned_out"], 1)
                    for c in range(2):
                        eng.wait_ge(S["pair_product"], l * NE + 2 * p + c + 1)
                        eng.activation(pair_out[:, c * 512:(c + 1) * 512], bank[c][:], ACT.Copy).then_inc(
                            S["pair_out_ready"], 1)

                with eng.Fori(0, PAIRS // 2) as i:
                    for k in range(2):
                        pair(2 * i + k, k)
                for name in ("silu_ready0", "silu_ready1", "actT_ready0", "actT_ready1"):
                    skip(eng, name, NE)

            either(eng, l, routed_only, everything)

        WARM = {"ffn norm": 36, "mix norm": 50, "router": 26, "places": 20, "compressed keys": 8, "forgetting heads": 20,
                "delta rule": 12, "inverse": 5, "chunk": 4, "out0": 30, "out1": 80}

        def keep_warm(pe, n, b):
            for _ in range(n):
                pe.matmul(bank[b][:, 0:256], zeros, finite, start=True, stop=True)

        def turn_in(pe, name, src):
            for g in range(4):
                for i in range(2):
                    for t in range(TT):
                        k = 2 * g + i
                        last = pe.transpose(bank[g][:, i * T + t * P:i * T + (t + 1) * P],
                                            src[:, t, k * P:(k + 1) * P], ident)
                last.then_inc(S[name], 1)

        def norm_pe(pe, l, f):
            if (l, f) != (0, "mix"):
                keep_warm(pe, WARM[f"{f} norm"], 0)
            pe.wait_ge(S["scaled"], TT * (nth(l, f) + 1))
            turn_in(pe, "turned", xn)
            pe.wait_ge(S["hT_act"], 4 * (nth(l, f) + 1))
            pe.wait_ge(S["hT_dve"], 4 * (nth(l, f) + 1))

        def out_product(pe, src, n0, l):
            keep_warm(pe, WARM[f"out{l}"], 6 * l)
            pe.wait_ge(S["mixed_ready"], 2 * TT * (l + 1))
            turn_in(pe, "mixed_turned", src)
            pe.wait_ge(S["mixedT_act"], 2 * (l + 1))
            pe.wait_ge(S["mixedT_dve"], 2 * (l + 1))
            for c in range(2):
                s = (n0 + c) % SLOTS
                pe.wait_ge(landed[s], 16 * ((n0 + c) // SLOTS + 1))
                for t in range(TT):
                    for k in range(KT):
                        last = pe.matmul(bank[4 + 2 * c + t][:], hT[:, k, t * P:(t + 1) * P], by_k(s)[:, k, :],
                                         start=(k == 0), stop=(k == KT - 1))
                    last.then_inc(S["mixed_product"], 1)

        def moe_pe(pe, l):
            if l == 0:
                pe.wait_ge(S["late_landed"], 16 * N_LATE)
            for t in range(TT):
                for k in range(KT):
                    last = pe.matmul(bank[0][:, t * 32:t * 32 + NG + NE], hT[:, k, t * P:(t + 1) * P], wr[:, l, k, :],
                                     start=(k == 0), stop=(k == KT - 1))
            last.then_inc(S["routed"], 1)
            pe.wait_ge(S["x_added"], 2 * TT * (2 * l + 1))
            for b in range(4, 8):
                for c in range(2):
                    pe.matmul(bank[b][:, c * 256:(c + 1) * 256], zeros, finite, start=(c == 0), stop=False,
                              skip_group_check=True)
            pe.wait_ge(S["logits_read"], l + 1)
            keep_warm(pe, WARM["router"], 2)
            pe.wait_ge(S["routed_ready"], l + 1)
            upto = table("upto")
            pe.matmul(bank[1][:, 0:NE], upto, routed[:, 0, :], start=True, stop=True)
            pe.matmul(bank[1][:, NE:2 * NE], ones, routed[:, 0, :], start=True, stop=False)
            pe.matmul(bank[1][:, NE:2 * NE], upto, routed[:, 1, :], start=False, stop=True)
            for t in range(TT):
                last = pe.matmul(bank[1][:, 2 * NE:3 * NE], ones, routed[:, t, :], start=(t == 0), stop=(t == 1))
            last.then_inc(S["ranked"], 1)
            keep_warm(pe, WARM["places"], 2)
            n0 = MOE[l]

            def inputs(i, j, t, k0, k1):
                s, turn = (n0 + 3 * (j // 2) + j % 2) % SLOTS, (n0 + 3 * (j // 2) + j % 2) // SLOTS
                if k0 == 0:
                    if t == 0:
                        pe.wait_ge(landed[s], i * 16 + 16 * (turn + 1))
                    pe.wait_ge(S[f"act_ready{t}"], l * (NE + 1) + i * MOE_STEP + j + 1)
                for k in range(k0, k1):
                    last = pe.matmul(bank[t][:], hT[:, k, t * P:(t + 1) * P], by_k(s)[:, k, :],
                                     start=(k == 0), stop=(k == KT - 1))
                if k1 == KT:
                    last.then_inc(S[f"gu_done{t}"], 1)

            def turned(i, j, t):
                pe.wait_ge(S[f"act_ready{t}"], l * (NE + 1) + i * MOE_STEP + j + 2)
                for f in range(2):
                    last = pe.transpose(bank[2 + t][:, f * P:(f + 1) * P], act[:, t, f * P:(f + 1) * P], ident)
                last.then_inc(S[f"act_turned{t}"], 1)

            def outputs(i, j, t):
                m = n0 + 3 * (j // 2) + 2
                s, turn = m % SLOTS, m // SLOTS
                if j % 2 == 0 and t == 0:
                    pe.wait_ge(landed[s], i * 16 + 16 * (turn + 1))
                pe.wait_ge(S[f"actT_ready{t}"], l * NE + i * MOE_STEP + j + 1)
                for c in range(2):
                    for f in range(2):
                        last = pe.matmul(bank[4 + 2 * c + t][:], actT[:, t, f, :],
                                         by_f(s)[:, j % 2, f, c * 512:(c + 1) * 512], start=False, stop=False,
                                         skip_group_check=True)
                if t == 1 and j % 2:
                    last.then_inc(S["pair_done"], 1)

            def everything():
                with pe.Fori(0, NE // MOE_STEP) as i:
                    for j in range(MOE_STEP):
                        inputs(i, j, 0, 0, 4)
                        if j:
                            turned(i, j - 1, 1)
                        inputs(i, j, 0, 4, KT)
                        if j:
                            outputs(i, j - 1, 1)
                        inputs(i, j, 1, 0, 4)
                        turned(i, j, 0)
                        inputs(i, j, 1, 4, KT)
                        outputs(i, j, 0)
                    turned(i, MOE_STEP - 1, 1)
                    outputs(i, MOE_STEP - 1, 1)
                for name, n in (("gathered", NE), ("pair_turned", PAIRS), ("pair_product", NE)):
                    skip(pe, name, n)

            def gather(p, k):
                pe.wait_ge(S["picks_ready"], l * PAIRS + p + 1)
                for g in range(2):
                    for kt in range(4 * g, 4 * g + 4):
                        for t in range(TT):
                            last = pe.matmul(bank[g][:, (kt % 4) * P:(kt % 4 + 1) * P], xn[:, t, kt * P:(kt + 1) * P],
                                             pick[:, k, t, :], start=(t == 0), stop=(t == 1))
                    last.then_inc(S["gathered"], 1)

            def scatter(k):
                for c in range(2):
                    for t in range(TT):
                        last = pe.matmul(bank[4 + 2 * c + t][:], turned_pair[:, k, 2 + t, :],
                                         pair_out[:, c * 512:(c + 1) * 512], start=False, stop=False,
                                         skip_group_check=True)

            def pair(i, k, first, last_pair):
                p = 2 * i + k
                halves = (slice(0, CAP), slice(CAP, 2 * CAP))
                slots = [(n0 + 3 * k + m) % SLOTS for m in range(3)]
                arrived = [i * 16 + 16 * ((n0 + 3 * k + m) // SLOTS + 1) for m in range(3)]
                pe.wait_ge(landed[slots[0]], arrived[0])
                pe.wait_ge(landed[slots[1]], arrived[1])
                pe.wait_ge(S["picked_ready"], l * NE + 2 * p + 2)
                for kt in range(KT):
                    for e in range(2):
                        done = pe.matmul(bank[2][halves[e], :], picked[:, kt, halves[e]], by_k(slots[e])[:, kt, :],
                                         start=(kt == 0), stop=(kt == KT - 1))
                done.then_inc(S["gu_done1"], 2)
                if not last_pair:
                    if not first:
                        pe.wait_ge(S["pair_out_ready"], l * NE + 2 * p)
                    gather(p + 1, 1 - k)
                pe.wait_ge(S["pair_act_ready"], l * PAIRS + p + 1)
                for f in range(2):
                    pe.transpose(bank[3][:, f * P:(f + 1) * P], act[:, 0, f * P:(f + 1) * P], ident)
                for t in range(TT):
                    done = pe.transpose(bank[3][:, (2 + t) * P:(3 + t) * P], weigh[:, k, t, :], ident)
                done.then_inc(S["pair_turned"], 1)
                if not first:
                    pe.wait_ge(S["pair_out_ready"], l * NE + 2 * p)
                    scatter(1 - k)
                pe.wait_ge(S["pair_turned_out"], l * PAIRS + p + 1)
                if not last_pair:
                    pe.wait_ge(S["picked_ready"], l * NE + 2 * p + 4)
                pe.wait_ge(landed[slots[2]], arrived[2])
                for c in range(2):
                    for f in range(2):
                        for e in range(2):
                            done = pe.matmul(bank[c][halves[e], :],
                                             turned_pair[:, k, f, halves[e]],
                                             by_f(slots[2])[:, e, f, c * 512:(c + 1) * 512],
                                             start=(f == 0), stop=(f == 1))
                    done.then_inc(S["pair_product"], 1)
                pe.wait_ge(S["pair_product"], l * NE + 2 * p + 2)
                pe.nop().then_inc(S["pair_done"], 1)

            def routed_only():
                gather(0, 0)
                pair(0, 0, True, False)
                pair(0, 1, False, False)
                with pe.Fori(1, PAIRS // 2 - 1) as i:
                    for k in range(2):
                        pair(i, k, False, False)
                pair(PAIRS // 2 - 1, 0, False, False)
                pair(PAIRS // 2 - 1, 1, False, True)
                pe.wait_ge(S["pair_out_ready"], (l + 1) * NE)
                scatter(1)
                for name in ("gu_done0", "act_turned0", "act_turned1"):
                    skip(pe, name, NE)

            either(pe, l, routed_only, everything)
            pe.matmul(bank[7][:, 256:512], zeros, finite, start=False, stop=True,
                      skip_group_check=True).then_inc(S["experts_done"], 1)

        def norm_dve(eng, chain, l, f):
            eng.wait_ge(S["squared"], TT * (nth(l, f) + 1))
            inverse_root(eng, f"{f}{l}", rstd[:, 0:TT], ss[:, 0:TT], 1.0 / D)
            for t in range(TT):
                eng.tensor_scalar(xn[:, t, :], x[:, t, :], rstd[:, t:t + 1], None, ALU.mult).then_inc(
                    S["scaled"], 1)
            g0 = (16 if f == "ffn" else 0) + l * KT
            for k in (2, 3, 6, 7):
                eng.wait_ge(S["turned"], 4 * nth(l, f) + k // 2 + 1)
                eng.tensor_scalar(hT[:, k, :], bank[k // 2][:, (k % 2) * T:(k % 2 + 1) * T],
                                  gainT[:, g0 + k:g0 + k + 1], None, ALU.mult).then_inc(S["hT_dve"], 1)

        def turn_out_dve(eng, l):
            for g in (1, 3):
                eng.wait_ge(S["mixed_turned"], 4 * l + g + 1)
                eng.tensor_copy(hT[:, 2 * g:2 * g + 2, :].rearrange("p a t -> p (a t)"), bank[g][:]).then_inc(
                    S["mixedT_dve"], 1)

        def add_product(eng, l):
            for c in range(2):
                for t in range(TT):
                    eng.wait_ge(S["mixed_product"], 4 * l + 2 * c + t + 1)
                    eng.tensor_tensor(x[:, t, c * 512:(c + 1) * 512], x[:, t, c * 512:(c + 1) * 512],
                                      bank[4 + 2 * c + t][:], ALU.add).then_inc(S["x_added"], 1)

        def moe_dve(eng, chain, l):
            eng.wait_ge(S["routed"], l + 1)
            tt, st = eng.tensor_tensor, eng.tensor_scalar
            chain(tt(logits[:], bank[0][:, 0:64].rearrange("p (t n) -> p t n", t=TT)[:, :, 0:NG + NE],
                     router_bias[:, l, :].unsqueeze(1).to_broadcast([P, TT, NG + NE]), ALU.add))
            eng.tensor_copy(rs[:, 7, :], rstd[:, 0:TT]).then_inc(S["logits_read"], 1)
            g_log, e_log = logits[:, :, 0:NG], logits[:, :, NG:NG + NE]
            rank = table("rank")

            def wide(v, n):
                return v.unsqueeze(2).to_broadcast([P, TT, n])

            def first_max(src, top, hot, n):
                rk = rank[:, NE - n:NE].unsqueeze(1).to_broadcast([P, TT, n])
                chain(eng.tensor_reduce(top, src, AX.X, ALU.max))
                chain(tt(hot, src, wide(top, n), ALU.is_equal))
                chain(tt(hot, hot, rk, ALU.mult))
                chain(eng.tensor_reduce(rs[:, 6, :], hot, AX.X, ALU.max))
                chain(tt(hot, wide(rs[:, 6, :], n), rk, ALU.is_equal))

            g_hot = rt[:, 1, :, 0:NG]
            first_max(g_log, rs[:, 0, :], g_hot, NG)
            tt(rt[:, 0, :, 0:NG], g_log, wide(rs[:, 0, :], NG), ALU.subtract).then_inc(S["router_arg"], 1)
            masked = rt[:, 2, :, :]
            chain(st(g_hot, g_hot, 1.0, BIG, ALU.subtract, ALU.mult))
            chain(tt(masked.rearrange("p t (g e) -> p t g e", g=NG), e_log.rearrange("p t (g e) -> p t g e", g=NG),
                     g_hot.unsqueeze(3).to_broadcast([P, TT, NG, EPG]), ALU.add))
            hot1, hot2 = rt[:, 3, :, :], rt[:, 4, :, :]
            first_max(masked, rs[:, 2, :], hot1, NE)
            chain(eng.scalar_tensor_tensor(rt[:, 5, :, :], hot1, -2 * BIG, masked, ALU.mult, ALU.add))
            first_max(rt[:, 5, :, :], rs[:, 3, :], hot2, NE)
            tt(rs[:, 1, :], rs[:, 3, :], rs[:, 2, :], ALU.subtract).then_inc(S["router_arg"], 1)
            eng.wait_ge(S["router_exp"], 2 * l + 1)
            chain(eng.tensor_reduce(rs[:, 4, :], rt[:, 0, :, 0:NG], AX.X, ALU.add))
            eng.wait_ge(S["router_exp"], 2 * l + 2)
            chain(st(rs[:, 5, :], rs[:, 1, :], 1.0, None, ALU.add))
            chain(tt(rs[:, 5, :], rs[:, 5, :], rs[:, 4, :], ALU.mult))
            chain(eng.reciprocal(rs[:, 4, :], rs[:, 5, :]))
            chain(tt(rs[:, 5, :], rs[:, 4, :], rs[:, 1, :], ALU.mult))
            tt(routed[:], hot1, hot2, ALU.add).then_inc(S["routed_ready"], 1)
            chain(tt(hot1, hot1, wide(rs[:, 4, :], NE), ALU.mult))
            chain(tt(hot2, hot2, wide(rs[:, 5, :], NE), ALU.mult))
            tt(gates[:], hot1, hot2, ALU.add).then_inc(S["gates_ready"], 1)
            eng.wait_ge(S["gates_ready"], l + 1)
            eng.wait_ge(S["ranked"], l + 1)
            chain(tt(place[:], bank[1][:, 0:2 * NE].rearrange("p (t e) -> p t e", t=TT), routed[:], ALU.mult))
            chain(st(place[:], place[:], -1.0, None, ALU.add))
            chain(eng.tensor_reduce(crowd[:, 0:1], bank[1][:, 2 * NE:3 * NE], AX.X, ALU.max))
            st(crowded[:], crowd[:, 0:1], float(CAP), None, ALU.is_gt).then_inc(S["crowd_known"], 1)

            def everything():
                for t in range(TT):
                    eng.tensor_copy(rs[:, 7, t:t + 1], rstd[:, t:t + 1]).then_inc(S[f"act_ready{t}"], 1)
                with eng.Fori(0, NE // MOE_STEP) as i:
                    for j in range(MOE_STEP):
                        n = i * MOE_STEP + j
                        for t in range(TT):
                            eng.wait_ge(S[f"silu_ready{t}"], l * NE + n + 1)
                            if j:
                                eng.wait_ge(S[f"act_turned{t}"], l * NE + n)
                            eng.scalar_tensor_tensor(act[:, t, :], silu_g[:, t, :],
                                                     gates[:, t, bass.ds(n, 1)],
                                                     bank[t][:, FF:2 * FF], ALU.mult, ALU.mult).then_inc(
                                                         S[f"act_ready{t}"], 1)
                        if j == MOE_STEP - 1:
                            for t in range(TT):
                                eng.wait_ge(S[f"act_turned{t}"], l * NE + n + 1)
                skip(eng, "picks_ready", PAIRS)
                skip(eng, "picked_ready", NE)
                skip(eng, "pair_act_ready", PAIRS)

            def picks(p, k):
                slot = table("slot")
                for t in range(TT):
                    for e in range(2):
                        at_ = place[:, t, bass.ds(2 * p + e, 1)]
                        half = slice(e * CAP, (e + 1) * CAP)
                        st(pick[:, k, t, half], slot, at_, None, ALU.is_equal)
                        ins = st(weigh[:, k, t, half], slot, at_, gates[:, t, bass.ds(2 * p + e, 1)], ALU.is_equal,
                                 ALU.mult)
                ins.then_inc(S["picks_ready"], 1)

            def picked_out(p):
                for g in range(2):
                    eng.wait_ge(S["gathered"], l * NE + 2 * p + g + 1)
                    gain = gainT[:, 16 + l * KT + 4 * g:16 + l * KT + 4 * g + 4]
                    tt(picked[:, 4 * g:4 * g + 4, :], bank[g][:].rearrange("p (k n) -> p k n", k=4),
                       gain.unsqueeze(2).to_broadcast([P, 4, 2 * CAP]), ALU.mult).then_inc(S["picked_ready"], 1)

            def routed_only():
                def pair(p, k, coming, after):
                    eng.wait_ge(S["pair_silu"], l * PAIRS + p + 1)
                    tt(act[:, 0, :], silu_g[:, 0, :], bank[2][:, FF:2 * FF], ALU.mult).then_inc(
                        S["pair_act_ready"], 1)
                    if coming:
                        picked_out(p + 1)
                    if after:
                        eng.wait_ge(S["pair_turned"], l * PAIRS + p + 1)
                        picks(p + 2, k)

                picks(0, 0)
                picks(1, 1)
                picked_out(0)
                with eng.Fori(0, PAIRS // 2 - 1) as i:
                    for k in range(2):
                        pair(2 * i + k, k, True, True)
                pair(PAIRS - 2, 0, True, False)
                pair(PAIRS - 1, 1, False, False)
                skip(eng, "act_ready0", NE + 1)
                skip(eng, "act_ready1", NE + 1)

            either(eng, l, routed_only, everything)
            eng.wait_ge(S["experts_done"], l + 1)
            for c in range(2):
                for t in range(TT):
                    eng.tensor_tensor(x[:, t, c * 512:(c + 1) * 512], x[:, t, c * 512:(c + 1) * 512],
                                      bank[4 + 2 * c + t][:], ALU.add).then_inc(
                                          S["x_added"], 1)

        def gdn_loads():
            return [
                (conv_rows[:], a["conv_w"][0].rearrange("j (b p) -> (j b) p", p=P)),
                (wab[:], a["w_in_odd"][0].rearrange("(k p) n -> p k n", p=P)[:, :, 4 * GH * GD:4 * GH * GD + 2 * GH]),
                (ab_bias[:, 0, :], a["dt_bias"][0].partition_broadcast(P)),
                (ab_bias[:, 1, :], a["a_log"][0].partition_broadcast(P)),
                (gdn_gain[:], a["gdn_norm_gain"][0].partition_broadcast(P)),
            ]

        def gdn_act(eng):
            eng.wait_ge(S["ab_arg"], 2)
            eng.activation(ab[:, 2:4], ab[:, 2:4], ACT.Exp, scale=-1.0).then_inc(S["ab_exp"], 1)
            eng.activation(ab_bias[:, 1, :], ab_bias[:, 1, :], ACT.Exp).then_inc(S["ab_exp"], 1)
            eng.wait_ge(S["ab_plus1"], 1)
            eng.activation(ab[:, 2:4], ab[:, 2:4], ACT.Ln).then_inc(S["ab_exp"], 1)
            eng.wait_ge(S["lnbeta_ready"], 1)
            eng.activation(gd[:, 11], gd[:, 0], ACT.Exp).then_inc(S["beta_ready"], 1)
            eng.wait_ge(S["beta_ready"], 1)
            for b in range(24):
                which, h = divmod(b, GH)
                eng.wait_ge(S["convolved"], b + 1)
                dst = (qT[:, h, :], kT[:, h, :], conv_v[:, h % 2, :])[which]
                eng.activation(dst, dst, ACT.Silu).then_inc(S["silu_qkv"], 1)
                if which < 2:
                    eng.wait_ge(S["silu_qkv"], b + 1)
                    if b >= 2:
                        eng.wait_ge(S["norms_done"], 2 * (b - 1))
                    eng.activation(conv_sq[:, b % 2, :], dst, ACT.Square).then_inc(S["qk_squared"], 1)
                if which == 2 and h >= 1:
                    v_out(eng, h - 1)
            v_out(eng, GH - 1)
            for m in range(2 * TT):
                c, t = divmod(m, TT)
                eng.wait_ge(S["z_done"], m + 1)
                eng.activation(zs[:, t, c * 512:(c + 1) * 512], bank[m][:], ACT.Silu).then_inc(S["z_ready"], 1)
            eng.wait_ge(S["norms_plus"], 1)
            eng.activation(lnss[:], lnss[:], ACT.Ln).then_inc(S["norms_ln"], 1)
            eng.wait_ge(S["scale_args"], 4)
            eng.activation(gd[:, 6:9], gd[:, 3:6], ACT.Exp).then_inc(S["scales_ready"], 1)
            eng.activation(chunk_decay[:], chunk_decay[:], ACT.Exp).then_inc(S["scales_ready"], 1)
            for hf in range(2):
                for hh in range(HH):
                    n = hf * HH + hh
                    eng.wait_ge(S["decay_arg"], TT * (n + 1))
                    d = decay[:, n % 2].rearrange("p t c i -> p (t c i)")
                    eng.activation(d, d, ACT.Exp).then_inc(S["decay_ready"], 1)
                for g in range(2):
                    eng.wait_ge(S["inv_turned"], 2 * hf + g + 1)
                    eng.activation(Tm[:, 2 * g:2 * g + 2].rearrange("p h t i -> p (h t i)"), bank[4 + g][:],
                                   ACT.Copy).then_inc(S["inv_first_out"], 1)
                for li in range(1, len(LEVELS)):
                    for g in range(2):
                        eng.wait_ge(S["inv_x"], 10 * hf + 2 * (li - 1) + g + 1)
                        eng.activation(Xm[:, 2 * g:2 * g + 2].rearrange("p h t i -> p (h t i)"), bank[4 + g][:],
                                       ACT.Copy).then_inc(S["inv_x_out"], 1)
                for t in range(TT):
                    eng.wait_ge(S["w_done"], TT * hf + t + 1)
                    eng.activation(nwT[:, t].rearrange("p h i -> p (h i)"), bank[4 + t][:], ACT.Copy,
                                   scale=-1.0).then_inc(S["w_ready"], 1)
                for c in range(4):
                    t, s_ = divmod(c, 2)
                    rows = slice(s_ * CHUNK, (s_ + 1) * CHUNK)
                    eng.wait_ge(S["v_new_done"], 4 * hf + c + 1)
                    eng.activation(v_new[rows].rearrange("p h d -> p (h d)"), bank[6 + t][rows, :],
                                   ACT.Copy).then_inc(S["v_new_ready"], 1)
                eng.wait_ge(S["o_ready"], TT * (hf + 1))
                eng.activation(squares1, mixed.rearrange("p t (h d) -> p t h d", d=GD)[:, :, hf * HH:(hf + 1) * HH, :],
                               ACT.Square).then_inc(S["o_squared"], 1)
            turn_out_act(eng, 1)

        def v_out(eng, h):
            eng.wait_ge(S["v_turned"], h + 1)
            for t in range(TT):
                eng.activation(vb[:, t, h, :], bank[5 + h % 2][:, t * P:(t + 1) * P], ACT.Copy,
                               scale=gd[:, 11, t, h:h + 1]).then_inc(S["v_ready"], 1)

        def gdn_pe(pe):
            pe.transpose(bank[6][:, 0:CONV * 24], conv_rows[:], ident[0:CONV * 24, 0:CONV * 24]).then_inc(
                S["conv_turned"], 1)
            for t in range(TT):
                for k in range(KT):
                    last = pe.matmul(bank[7][:, t * 16:(t + 1) * 16], hT[:, k, t * P:(t + 1) * P], wab[:, k, :],
                                     start=(k == 0), stop=(k == KT - 1))
            last.then_inc(S["ab_done"], 1)

            def norms(b):
                pe.wait_ge(S["qk_squared"], b + 1)
                which, h = divmod(b, GH)
                for t in range(TT):
                    at_ = (which * TT + t) * GH + h
                    pe.matmul(bank[4][:, at_:at_ + 1], conv_sq[:, b % 2, t * P:(t + 1) * P], ones[:, 0:1],
                              start=True, stop=True).then_inc(S["norms_done"], 1)

            def turn_v(h):
                pe.wait_ge(S["silu_qkv"], 16 + h + 1)
                if h >= 2:
                    pe.wait_ge(S["v_ready"], 2 * (h - 1))
                for t in range(TT):
                    last = pe.transpose(bank[5 + h % 2][:, t * P:(t + 1) * P], conv_v[:, h % 2, t * P:(t + 1) * P],
                                        ident)
                last.then_inc(S["v_turned"], 1)

            for b in range(24 + 2):
                if b < 24:
                    c, m = divmod(b, 4)
                    s_ = (IN1 + c) % SLOTS
                    if m == 0:
                        pe.wait_ge(landed[s_], 16 * ((IN1 + c) // SLOTS + 1))
                    if b >= 4:
                        pe.wait_ge(S["convolved"], b - 3)
                    for k in range(KT):
                        last = pe.matmul(bank[b % 4][:, 0:T], by_k(s_)[:, k, m * P:(m + 1) * P], hT[:, k, :],
                                         start=(k == 0), stop=(k == KT - 1))
                    last.then_inc(S["qkv_done"], 1)
                if b == 2:
                    pe.wait_ge(S["g_ready"], 1)
                    pe.matmul(bank[7][:, 64:80], table("chunk_upto"), gd[:, 1].rearrange("p t h -> p (t h)"),
                              start=True, stop=True).then_inc(S["gc_done"], 1)
                    pe.wait_ge(S["gc_ready"], 1)
                    gc = gd[:, 2].rearrange("p t h -> p (t h)")
                    pe.matmul(bank[7][:, 80:96], table("chunk_last"), gc, start=True, stop=True)
                    for s2 in range(2):
                        last = pe.matmul(bank[7][:, 96 + 16 * s2:112 + 16 * s2],
                                         spread(s2 * CHUNK + CHUNK - 1), gc, start=True, stop=True)
                    last.then_inc(S["gc_done"], 1)
                if 2 <= b < 18:
                    norms(b - 2)
                if b >= 18:
                    turn_v(b - 18)
            for m in range(2 * TT):
                c, t = divmod(m, TT)
                n = IN1 + 6 + c
                if t == 0:
                    pe.wait_ge(landed[n % SLOTS], 16 * (n // SLOTS + 1))
                pe.wait_ge(S["convolved"], 24)
                for k in range(KT):
                    last = pe.matmul(bank[m][:], hT[:, k, t * P:(t + 1) * P], by_k(n % SLOTS)[:, k, :],
                                     start=(k == 0), stop=(k == KT - 1))
                last.then_inc(S["z_done"], 1)
            pe.wait_ge(S["scale_args"], 4)
            for r in range(2):
                for t in range(TT):
                    last = pe.transpose(bank[4][0:GH, r * T + t * P:r * T + (t + 1) * P], gd[:, 3 + r, t, :], ident)
            last.then_inc(S["rows_turned"], 1)
            keep_warm(pe, WARM["delta rule"], 5)
            pe.wait_ge(S["rows_ready"], 1)
            pe.wait_ge(S["z_ready"], 2 * TT)
            for hf in range(2):
                if hf:
                    pe.wait_ge(S["o_ready"], TT)
                for hh in range(HH):
                    h, n = hf * HH + hh, hf * HH + hh
                    if hh >= 2:
                        pe.wait_ge(S["decay_arg"], TT * (n - 1))
                        pe.wait_ge(S["LA_ready"], n - 1)
                    sel = spread(h)[0:GH]
                    for r in range(2):
                        last = pe.matmul(bank[hh % 2][:, r * T:(r + 1) * T], sel, rowT[:, r, :], start=True, stop=True)
                    last.then_inc(S["rows_spread"], 1)
                    for t in range(TT):
                        tok = slice(t * P, (t + 1) * P)
                        for c, other in enumerate((kT, qT)):
                            last = pe.matmul(bank[2 + hh % 2][:, (2 * t + c) * P:(2 * t + c + 1) * P], kT[:, h, tok],
                                             other[:, h, tok], start=True, stop=True)
                    last.then_inc(S["gram_done"], 1)
                for g in range(2):
                    pe.wait_ge(S["inv_T"], 12 * hf + g + 1)
                    for m in range(4):
                        hh, t = 2 * g + m // 2, m % 2
                        last = pe.transpose(bank[4 + g][:, m * P:(m + 1) * P], TmT[:, hh, t, :], ident)
                    last.then_inc(S["inv_turned"], 1)
                for li in range(1, len(LEVELS)):
                    final = li == len(LEVELS) - 1
                    keep_warm(pe, WARM["inverse"], 3)
                    pe.wait_ge(S["level_ready"], 6 * hf + li + 1)
                    for g in range(2):
                        if li == 1:
                            pe.wait_ge(S["inv_first_out"], 2 * hf + g + 1)
                        else:
                            pe.wait_ge(S["inv_T"], 12 * hf + 2 * (li - 1) + g + 1)
                        for m in range(4):
                            hh, t = 2 * g + m // 2, m % 2
                            last = pe.matmul(bank[4 + g][:, m * P:(m + 1) * P], level[:, hh, t, :], Tm[:, hh, t, :],
                                             start=True, stop=True)
                        last.then_inc(S["inv_x"], 1)
                    for g in range(2):
                        pe.wait_ge(S["inv_x_out"], 10 * hf + 2 * (li - 1) + g + 1)
                        for m in range(4):
                            hh, t = 2 * g + m // 2, m % 2
                            last = pe.matmul(bank[g][:, m * P:(m + 1) * P], Xm[:, hh, t, :], TmT[:, hh, t, :],
                                             start=True, stop=True)
                            if not final:
                                last = pe.matmul(bank[6 + g][:, m * P:(m + 1) * P], TmT[:, hh, t, :],
                                                 Xm[:, hh, t, :], start=True, stop=True)
                        last.then_inc(S["inv_y"], 1)
                for t in range(TT):
                    for hh in range(HH):
                        last = pe.transpose(bank[2 + t][:, hh * P:(hh + 1) * P],
                                            kT[:, hf * HH + hh, t * P:(t + 1) * P], ident)
                    last.then_inc(S["k_turned"], 1)
                for t in range(TT):
                    pe.wait_ge(S["k_scaled"], 2 * (TT * hf + t + 1))
                    if t == 0:
                        pe.wait_ge(S["inv_T"], 12 * (hf + 1))
                    for hh in range(HH):
                        last = pe.matmul(bank[4 + t][:, hh * P:(hh + 1) * P], kbg[:, t, hh, :], TmT[:, hh, t, :],
                                         start=True, stop=True)
                    last.then_inc(S["w_done"], 1)
                pe.wait_ge(S["w_ready"], TT * (hf + 1))
                for c in range(4):
                    t, s_ = divmod(c, 2)
                    rows = slice(s_ * CHUNK, (s_ + 1) * CHUNK)
                    tok = slice(t * P + s_ * CHUNK, t * P + (s_ + 1) * CHUNK)
                    pe.wait_ge(S["v_ready"], 2 * GH)
                    pe.wait_ge(S["state_ready"], 5 * hf + c + 1)
                    for hh in range(HH):
                        o = bank[6 + t][rows, hh * GD:(hh + 1) * GD]
                        pe.matmul(o, TmT[:, hh, t, rows], vb[:, t, hf * HH + hh, :], start=True, stop=False)
                        last = pe.matmul(o, nwT[:, t, hh, rows], state[:, hh, :], start=False, stop=True)
                    last.then_inc(S["v_new_done"], 1)
                    for hh in range(HH):
                        last = pe.matmul(bank[t][rows, hh * GD:(hh + 1) * GD], qT[:, hf * HH + hh, tok],
                                         state[:, hh, :], start=True, stop=True)
                    last.then_inc(S["q_state_done"], 1)
                    keep_warm(pe, WARM["chunk"], 4 + c % 2)
                    pe.wait_ge(S["v_new_ready"], 4 * hf + c + 1)
                    for hh in range(HH):
                        last = pe.matmul(bank[4 + c % 2][:, hh * GD:(hh + 1) * GD], kdec[rows, t, hh, :],
                                         v_new[rows, hh, :], start=True, stop=True)
                    last.then_inc(S["update_done"], 1)
                    for hh in range(HH):
                        last = pe.matmul(bank[2 + t][rows, hh * GD:(hh + 1) * GD], LA[rows, hh, t, 1, rows],
                                         v_new[rows, hh, :], start=True, stop=True)
                    last.then_inc(S["chunk_out"], 1)
            out_product(pe, mixed, OUT1, 1)

        def gdn_pool(pool):
            pool.wait_ge(S["z_ready"], 2 * TT)
            z4 = zs.rearrange("p t (h d) -> p (t h) d", d=GD)
            pool.tensor_tensor(z4, z4, gdn_gain[:].unsqueeze(1).to_broadcast([P, TT * GH, GD]),
                               ALU.mult).then_inc(S["z_gained"], 1)
            for hf in range(2):
                for li, lv in enumerate(LEVELS):
                    if li == 0:
                        pool.wait_ge(S["LA_ready"], HH * (hf + 1))
                        if hf:
                            pool.wait_ge(S["chunk_out"], 4)
                    elif li == 1:
                        pool.wait_ge(S["inv_T"], 12 * hf + 2)
                    else:
                        pool.wait_ge(S["inv_x"], 10 * hf + 2 * (li - 1))
                    mask = table(f"level{lv}").unsqueeze(1).unsqueeze(1).to_broadcast([P, HH, TT, P])
                    pool.tensor_tensor(level, LA[:, :, :, 0, :], mask, ALU.mult).then_inc(S["level_ready"], 1)
                root_pool(pool, f"o{hf}", rstd[:, 0:TT * HH])

        def gdn_dve(eng, chain):
            tt, st, stt = eng.tensor_tensor, eng.tensor_scalar, eng.scalar_tensor_tensor
            lnbeta, g_, gc, row1, row2, dec_arg = (gd[:, i] for i in range(6))
            col = gd[:, 9]
            eng.wait_ge(S["conv_turned"], 1)
            chain(eng.tensor_copy(convT[:], bank[6][:, 0:CONV * 24]))
            eng.wait_ge(S["ab_done"], 1)
            raw = bank[7][:, 0:32].rearrange("p (t c h) -> p c t h", t=TT, c=2)
            chain(tt(ab[:, 0], raw[:, 0], ab_bias[:, 0, :].unsqueeze(1).to_broadcast([P, TT, GH]), ALU.add))
            chain(eng.tensor_copy(ab[:, 1], raw[:, 1]))
            for i in range(2):
                stt(ab[:, 2 + i], ab[:, i], -1.0, ab[:, i], ALU.mult, ALU.max).then_inc(S["ab_arg"], 1)
            eng.wait_ge(S["ab_exp"], 2)
            st(ab[:, 2:4], ab[:, 2:4], 1.0, None, ALU.add).then_inc(S["ab_plus1"], 1)
            eng.wait_ge(S["ab_exp"], 3)
            stt(lnbeta, ab[:, 1], 0.0, ab[:, 3], ALU.min, ALU.subtract).then_inc(S["lnbeta_ready"], 1)
            chain(stt(g_, ab[:, 0], 0.0, ab[:, 2], ALU.max, ALU.add))
            stt(g_, g_, -1.0, ab_bias[:, 1, :].unsqueeze(1).to_broadcast([P, TT, GH]), ALU.mult,
                ALU.mult).then_inc(S["g_ready"], 1)
            for b in range(24):
                which, h = divmod(b, GH)
                dst = (qT[:, h, :], kT[:, h, :], conv_v[:, h % 2, :])[which]
                if b == 3:
                    eng.wait_ge(S["gc_done"], 1)
                    eng.tensor_copy(gc.rearrange("p t h -> p (t h)"), bank[7][:, 64:80]).then_inc(S["gc_ready"], 1)
                    eng.wait_ge(S["gc_done"], 2)
                    chain(tt(gd[:, 10].rearrange("p t h -> p (t h)"), bank[7][:, 80:96],
                             gc.rearrange("p t h -> p (t h)"), ALU.subtract))
                    chain(eng.tensor_copy(chunk_decay[:].rearrange("p s t h -> p (s t h)"), bank[7][:, 96:128]))
                eng.wait_ge(S["qkv_done"], b + 1)
                if which == 2 and h >= 2:
                    eng.wait_ge(S["v_turned"], h - 1)
                src = bank[b % 4]
                chain(st(dst, src[:, 0:T], convT[:, 72 + b:73 + b], None, ALU.mult))
                for back in (1, 2, 3):
                    i = 24 * (3 - back) + b
                    ins = stt(dst[:, back:T], src[:, 0:T - back], convT[:, i:i + 1], dst[:, back:T], ALU.mult, ALU.add)
                    if back < 3:
                        chain(ins)
                    else:
                        ins.then_inc(S["convolved"], 1)
            eng.wait_ge(S["norms_done"], 2 * 2 * GH)
            st(lnss[:].rearrange("p c t h -> p (c t h)"), bank[4][:, 0:32], EPS, None, ALU.add).then_inc(
                S["norms_plus"], 1)
            eng.wait_ge(S["norms_ln"], 1)
            lq, lk = lnss[:, 0], lnss[:, 1]
            chain(st(lq, lq, -0.5, float(-0.5 * np.log(GD)), ALU.mult, ALU.add))
            chain(st(lk, lk, -0.5, None, ALU.mult))
            chain(tt(row1, gc, lnbeta, ALU.add))
            tt(row1, row1, lk, ALU.add).then_inc(S["scale_args"], 1)
            tt(row2, gc, lq, ALU.add).then_inc(S["scale_args"], 1)
            tt(dec_arg, gd[:, 10], lk, ALU.add).then_inc(S["scale_args"], 1)
            tt(col, lk, gc, ALU.subtract).then_inc(S["scale_args"], 1)
            eng.wait_ge(S["scale_args"], 4)
            eng.wait_ge(S["rows_turned"], 1)
            eng.tensor_copy(rowT[:].rearrange("p r t -> p (r t)"), bank[4][0:GH, :]).then_inc(S["rows_ready"], 1)
            eng.wait_ge(S["scales_ready"], 2)
            s_kb, s_q, s_kd = gd[:, 6], gd[:, 7], gd[:, 8]
            bias = table("chunk_bias").rearrange("p (c i) -> p c i", c=2)
            eng.wait_ge(S["z_done"], 2 * TT)
            for hf in range(2):
                heads = slice(hf * HH, (hf + 1) * HH)

                def gram(n):
                    eng.wait_ge(S["decay_ready"], n + 1)
                    eng.wait_ge(S["gram_done"], n + 1)
                    tt(LA[:, n % HH].rearrange("p t c i -> p (t c i)"), bank[2 + n % 2][:],
                       decay[:, n % 2].rearrange("p t c i -> p (t c i)"), ALU.mult).then_inc(S["LA_ready"], 1)

                for hh in range(HH):
                    n = hf * HH + hh
                    eng.wait_ge(S["rows_spread"], n + 1)
                    if hh >= 2:
                        eng.wait_ge(S["LA_ready"], n - 1)
                    for t in range(TT):
                        stt(decay[:, n % 2, t], bank[hh % 2][:].rearrange("p (c t) -> p c t", c=2)[
                            :, :, t * P:(t + 1) * P], col[:, t, n:n + 1], bias, ALU.add, ALU.add).then_inc(
                                S["decay_arg"], 1)
                    if hh >= 1:
                        gram(n - 1)
                gram(hf * HH + HH - 1)
                eng.memset(state, 0.0).then_inc(S["state_ready"], 1)
                eng.wait_ge(S["level_ready"], 6 * hf + 1)
                for g in range(2):
                    tt(TmT[:, 2 * g:2 * g + 2], ident.unsqueeze(1).unsqueeze(1).to_broadcast([P, 2, TT, P]),
                       level[:, 2 * g:2 * g + 2], ALU.subtract).then_inc(S["inv_T"], 1)
                eng.wait_ge(S["inv_first_out"], 2 * (hf + 1))
                for li in range(1, len(LEVELS)):
                    for g in range(2):
                        eng.wait_ge(S["inv_y"], 10 * hf + 2 * (li - 1) + g + 1)
                        v = TmT[:, 2 * g:2 * g + 2].rearrange("p h t i -> p (h t i)")
                        ins = tt(v, v, bank[g][:], ALU.subtract)
                        if li < len(LEVELS) - 1:
                            chain(ins)
                            v = Tm[:, 2 * g:2 * g + 2].rearrange("p h t i -> p (h t i)")
                            ins = tt(v, v, bank[6 + g][:], ALU.subtract)
                        ins.then_inc(S["inv_T"], 1)
                for t in range(TT):
                    eng.wait_ge(S["k_turned"], TT * hf + t + 1)
                    src = bank[2 + t][:].rearrange("p (h d) -> p h d", d=GD)
                    for dst, f in ((kbg, s_kb), (kdec, s_kd)):
                        tt(dst[:, t], src, f[:, t, heads].unsqueeze(2).to_broadcast([P, HH, GD]), ALU.mult).then_inc(
                            S["k_scaled"], 1)
                for c in range(4):
                    t, s_ = divmod(c, 2)
                    eng.wait_ge(S["q_state_done"], 4 * hf + c + 1)
                    chain(tt(state, state, chunk_decay[:, s_, t, heads].unsqueeze(2).to_broadcast([P, HH, GD]),
                             ALU.mult))
                    eng.wait_ge(S["update_done"], 4 * hf + c + 1)
                    tt(state.rearrange("p h d -> p (h d)"), state.rearrange("p h d -> p (h d)"), bank[4 + c % 2][:],
                       ALU.add).then_inc(S["state_ready"], 1)
                    if s_ == 1:
                        eng.wait_ge(S["chunk_out"], 4 * hf + c + 1)
                        o = mixed.rearrange("p t (h d) -> p t h d", d=GD)[:, t, heads, :]
                        chain(tt(o, bank[t][:].rearrange("p (h d) -> p h d", d=GD),
                                 s_q[:, t, heads].unsqueeze(2).to_broadcast([P, HH, GD]), ALU.mult))
                        tt(o, o, bank[2 + t][:].rearrange("p (h d) -> p h d", d=GD), ALU.add).then_inc(
                            S["o_ready"], 1)
                eng.wait_ge(S["z_gained"], 1)
                for t in range(TT):
                    z = zs[:, t, :].rearrange("p (h d) -> p h d", d=GD)[:, heads, :]
                    chain(tt(z, z, mixed.rearrange("p t (h d) -> p t h d", d=GD)[:, t, heads, :], ALU.mult))
                eng.wait_ge(S["o_squared"], hf + 1)
                chain(eng.tensor_reduce(ss[:, 0:TT * HH].rearrange("p (t h) -> p t h", t=TT), squares1, AX.X, ALU.add))
                inverse_root(eng, f"o{hf}", rstd[:, 0:TT * HH], ss[:, 0:TT * HH], 1.0 / GD)
                for t in range(TT):
                    o = mixed.rearrange("p t (h d) -> p t h d", d=GD)[:, t, heads, :]
                    tt(o, zs[:, t, :].rearrange("p (h d) -> p h d", d=GD)[:, heads, :],
                       rstd[:, t * HH:(t + 1) * HH].unsqueeze(2).to_broadcast([P, HH, GD]), ALU.mult).then_inc(
                        S["mixed_ready"], 1)
            turn_out_dve(eng, 1)
            add_product(eng, 1)

        N_FIRST, N_SMALL, N_LATE = 5, 7, 8 + len(gdn_loads())

        block = ctx.enter_context(nc.Block())

        @block.sync
        def _(sp):
            def load(n, kind, c):
                s = n % SLOTS
                if n >= SLOTS:
                    name, value = read[n - SLOTS]
                    sp.wait_ge(S[name], value)
                if kind == "cmp":
                    sp.wait_ge(S["slots_zeroed"], c + 1)
                    dst = ring[:, s, :].rearrange("p (l e) -> p l e", l=CMP_BLOCK)
                    src = a["cmp_w1"][0, c].rearrange("l d e -> d l e")
                    sp.dma_start(dst[0:HD, :, 0:HD], src).then_inc(S["cmp_half_landed"], 16)
                    sp.dma_start(dst[HD:P, :, HD:P], src).then_inc(landed[s], 16)
                    return
                if kind == "in0":
                    w, (c0, n_cols) = a["w_in_even"][0], c
                    if c0 == 1024:
                        sp.dma_start(by_k(s)[:, :, 280:288], w.rearrange("(k p) n -> p k n", p=P)[
                            :, :, FORGET0:FORGET0 + 8]).then_inc(S["forget_landed"], 16)
                elif kind == "out0":
                    w, c0, n_cols = a["w_out_even"][0], 512 * c, 512
                elif kind == "in1":
                    w, c0, n_cols = a["w_in_odd"][0], 512 * c, 512
                else:
                    w, c0, n_cols = a["w_out_odd"][0], 512 * c, 512
                sp.dma_start(by_k(s, n_cols), w.rearrange("(k p) n -> p k n", p=P)[
                    :, :, c0:c0 + n_cols]).then_inc(landed[s], 16)

            def load_experts(layer):
                w_in = a["w_expert_in"][layer].rearrange("e (k p) n -> e p k n", p=P)
                w_out = a["w_expert_out"][layer].rearrange("(q e) (f p) n -> q p (e f) n", p=P, e=2)

                def load_four(i):
                    for j in range(SLOTS):
                        s = (MOE[layer] + j) % SLOTS
                        pair, part = divmod(j, 3)
                        if type(i) is int:
                            name, value = read[MOE[layer] + j - SLOTS]
                            sp.wait_ge(S[name], value)
                        elif part < 2:
                            sp.wait_ge(S["gu_done1"], layer * NE + (i - 1) * MOE_STEP + 2 * pair + part + 1)
                        else:
                            sp.wait_ge(S["pair_done"], layer * NE // 2 + (i - 1) * (MOE_STEP // 2) + pair + 1)
                        if part < 2:
                            src = w_in[bass.ds(i * MOE_STEP + 2 * pair + part, 1)]
                            dst = by_k(s)
                        else:
                            src = w_out[bass.ds(i * (MOE_STEP // 2) + pair, 1)]
                            dst = by_f(s).rearrange("p e f n -> p (e f) n")
                        sp.dma_start(dst, src.rearrange("o p k n -> (o p) k n")).then_inc(landed[s], 16)

                load_four(0)
                with sp.Fori(1, NE // MOE_STEP) as i:
                    load_four(i)

            sp.dma_start(x[:], a["x"][0].rearrange("(t p) d -> p t d", p=P)).then_inc(S["x_landed"], 16)
            first = cols["causal"][0]
            sp.dma_start(const[:, 0:first], a["tables"][:, 0:first]).then_inc(S["first_landed"], 16)
            first_rows = [
                (gain_rows[0:16, :], a["norm_mix"].rearrange("l (k p) -> (l k) p", p=P)),
                (gain_rows[16:32, :], a["norm_ffn"].rearrange("l (k p) -> (l k) p", p=P)),
                (pe_rows[:, :, 0, :], a["cmp_pe"][0].rearrange("c l d -> l c d")),
                (pe_rows[:, :, 1, :], a["cmp_pe"][0].rearrange("c l d -> l c d")),
            ]
            for dst, src in first_rows:
                sp.dma_start(dst, src).then_inc(S["first_landed"], 16)
            load(0, *stream[0])
            small = [
                (head_gain[:, 0:4, :].rearrange("p a d -> p (a d)"),
                 a["nsa_qk_gain"][0].rearrange("a d -> (a d)").partition_broadcast(P)),
                (head_gain[:, 4:6, :].rearrange("p a d -> p (a d)"),
                 a["fox_qk_gain"][0].rearrange("a d -> (a d)").partition_broadcast(P)),
                (bias_row[:, 0:24], a["b_nsa_gate"][0].partition_broadcast(P)),
                (bias_row[:, 24:32], a["b_forget"][0].partition_broadcast(P)),
            ]
            for half in range(2):
                h = slice(half * HD, (half + 1) * HD)
                small.append((w2[h, :, h], a["cmp_w2"][0].rearrange("c e f -> e c f")))
            late = []
            for l in range(2):
                late += [
                    (wr[:, l, :, 0:NG], a["w_router_group"][l].rearrange("(k p) n -> p k n", p=P)),
                    (wr[:, l, :, NG:NG + NE], a["w_router_expert"][l].rearrange("(k p) n -> p k n", p=P)),
                    (router_bias[:, l, 0:NG], a["b_router_group"][l].partition_broadcast(P)),
                    (router_bias[:, l, NG:NG + NE], a["b_router_expert"][l].partition_broadcast(P)),
                ]
            sp.wait_ge(S["w2_zeroed"], 1)
            sp.dma_start(const[:, first:], a["tables"][:, first:]).then_inc(S["small_landed"], 16)
            for dst, src in small:
                sp.dma_start(dst, src).then_inc(S["small_landed"], 16)
            for n in range(1, SLOTS):
                load(n, *stream[n])
            for dst, src in late + gdn_loads():
                sp.dma_start(dst, src).then_inc(S["late_landed"], 16)

            for n in range(SLOTS, len(stream)):
                load(n, *stream[n])
            load_experts(0)
            if LAYERS > 1:
                for n, (kind, c) in enumerate(stream1):
                    load(IN1 + n, kind, c)
                load_experts(1)
            for m in range(2 * TT):
                c, t = divmod(m, TT)
                sp.wait_ge(S["x_added"], 2 * TT * (2 * LAYERS - 1) + m + 1)
                sp.dma_start(out[0].rearrange("(t p) d -> p t d", p=P)[:, t, c * 512:(c + 1) * 512],
                             x[:, t, c * 512:(c + 1) * 512]).then_inc(S["stored"], 16)
            sp.wait_ge(S["stored"], 16 * 2 * TT)

        @block.gpsimd
        def _(pool):
            pool.memset(w2[:], 0.0).then_inc(S["w2_zeroed"], 1)
            for kv in range(2):
                pool.memset(ring[:, CMP0 + kv, :], 0.0).then_inc(S["slots_zeroed"], 1)
            root_pool(pool, "mix0", rstd[:, 0:TT])
            root_pool(pool, "heads12", rstd[:, 0:TT * 12])
            root_pool(pool, "heads16", rstd[:, 0:TT * 16])
            root_pool(pool, "kc", rstd[0:NC, 60:62])
            root_pool(pool, "ffn0", rstd[:, 0:TT])
            if LAYERS > 1:
                root_pool(pool, "mix1", rstd[:, 0:TT])
                gdn_pool(pool)
                root_pool(pool, "ffn1", rstd[:, 0:TT])

        @block.scalar
        def _(eng):
            chain = Chain(eng, S["act_chain"])
            norm_act(eng, 0, "mix")
            for j in range(0, 12, 2):
                c0, w = chunks0[j // 2]
                eng.wait_ge(S["proj_done"], j + 1)
                if c0 == 1024:
                    eng.activation(proj[:, 0, FORGET0:FORGET0 + 8], bank[j % 4][:, 280:288], ACT.Copy).then_inc(
                        S["forget_out"], 1)
                eng.activation(proj[:, 0, c0:c0 + w], bank[j % 4][:, 0:w], ACT.Copy).then_inc(S["proj_out_act"], 1)
                if j == 4:
                    eng.wait_ge(S["proj_out_dve"], 3)
                    eng.wait_ge(S["proj_out_act"], 3)
                    for s0, d0, w in ((0, 0, 512), (768, 512, 128), (1024, 640, 128)):
                        eng.activation(squares[:, :, d0:d0 + w], proj[:, :, s0:s0 + w], ACT.Square).then_inc(
                            S["squared_nsa"], 1)
                if j == 8:
                    eng.wait_ge(S["gelu_arg"], 1)
                    eng.activation(hu[:], hu[:], ACT.Exp, scale=-2.0 * 0.7978845608028654).then_inc(S["gelu_exp"], 1)
                    eng.wait_ge(S["rotated"], 1)
                    eng.wait_ge(S["proj_out_act"], 5)
                    eng.wait_ge(S["proj_out_dve"], 5)
                    eng.activation(squares[:, :, :], proj[:, :, FQ0:FQ0 + 1024], ACT.Square).then_inc(
                        S["squared_fox"], 1)
            eng.wait_ge(S["gate_arg"], 2)
            eng.activation(gate_tmp[:], gate_tmp[:], ACT.Exp, scale=-1.0).then_inc(S["gate_exp"], 1)
            eng.wait_ge(S["gate_plus1"], 1)
            eng.activation(logf[:], gate_tmp[:, :, 24:32], ACT.Ln).then_inc(S["forget_ln"], 1)
            for g in range(0, 8, 2):
                eng.wait_ge(S["heads_turned"], g + 1)
                eng.activation(headT[:, 2 * g:2 * g + 2, :].rearrange("p a t -> p (a t)"), bank[g % 4][:],
                               ACT.Copy).then_inc(S["heads_out_act"], 1)
            eng.wait_ge(S["cmp_shifted"], 1)
            eng.activation(cmp_e, cmp_s, ACT.Exp, scale=SCALE).then_inc(S["cmp_exp"], 1)

            def turned_out(u):
                eng.wait_ge(S["probs_turned"], u + 1)
                if u >= 2:
                    eng.wait_ge(S["unit_out"], u - 1)
                eng.activation(probsT[:, u % 2, :], bank[2 + u % 2][:, 0:384], ACT.Copy).then_inc(
                    S["probsT_ready"], 1)

            for u in range(UNITS):
                if u >= 2:
                    turned_out(u - 2)
                eng.wait_ge(S["masked"], TT * (u + 1))
                if u >= 2:
                    eng.wait_ge(S["probs_turned"], u - 1)
                for t, (c0, c1) in enumerate(((0, P), (P, 3 * P))):
                    eng.activation(probs[:, u % 2, c0:c1], negs[:, u % 2, c0:c1], ACT.Exp,
                                   bias=neg_max[:, u, t:t + 1], scale=-1.0,
                                   accum_out=sums[:, u, t:t + 1]).then_inc(S["probs_ready"], 1)
                if u == 3:
                    eng.wait_ge(S["cmp_turned"], 1)
                    eng.activation(cmp_pT, bank[7][:], ACT.Copy).then_inc(S["cmp_pT_ready"], 1)
            turned_out(UNITS - 2)
            turned_out(UNITS - 1)
            turn_out_act(eng, 0)
            norm_act(eng, 0, "ffn")
            moe_act(eng, 0)
            if LAYERS > 1:
                norm_act(eng, 1, "mix")
                gdn_act(eng)
                norm_act(eng, 1, "ffn")
                moe_act(eng, 1)

        @block.tensor
        def _(pe):
            pe.wait_ge(S["first_landed"], 16 * N_FIRST)
            pe.transpose(bank[4][:, 0:32], gain_rows[:, :], ident[0:32, 0:32])
            for c in range(2):
                last = pe.transpose(bank[4][:, 64 + 32 * c:96 + 32 * c],
                                    pe_rows[:, c, :, :].rearrange("l a d -> l (a d)"), ident[0:32, 0:32])
            last.then_inc(S["small_turned"], 1)
            norm_pe(pe, 0, "mix")

            def project_chunk(c):
                n = in0_load[c]
                s, w = n % SLOTS, (288 if chunks0[c][0] == 1024 else 512)
                pe.wait_ge(landed[s], 16 * (n // SLOTS + 1))
                if w == 288:
                    pe.wait_ge(S["forget_landed"], 16)
                for t in range(TT):
                    j = 2 * c + t
                    if j >= 4:
                        pe.wait_ge(S["proj_out_dve" if t else "proj_out_act"], c - 1)
                    for k in range(KT):
                        last = pe.matmul(bank[j % 4][:, 0:w], hT[:, k, t * P:(t + 1) * P], by_k(s)[:, k, 0:w],
                                         start=(k == 0), stop=(k == KT - 1))
                    last.then_inc(S["proj_done"], 1)

            for c in range(6):
                project_chunk(c)
                if c == 1:
                    pe.wait_ge(S["proj_out_act"], 1)
                    pe.wait_ge(S["proj_out_dve"], 1)
                    for kv in range(2):
                        for t in range(TT):
                            last = pe.transpose(bank[5][:, kv * T + t * P:kv * T + (t + 1) * P],
                                                proj[:, t, 512 + kv * P:640 + kv * P], ident)
                    last.then_inc(S["raw_turned"], 1)
                if c == 3:
                    pe.wait_ge(S["cmp_half_landed"], 32)
                    pe.wait_ge(S["pe_added"], 4)
                    for kv in range(2):
                        pe.wait_ge(landed[CMP0 + kv], 16)
                        for l in range(CMP_BLOCK):
                            half, r = divmod(l, CMP_STRIDE)
                            rhs = pe_in[:, kv, half, :].rearrange("p (n r) -> p n r", r=CMP_STRIDE)[
                                :, half:half + NCMP, r]
                            last = pe.matmul(bank[6][:, 32 * kv:32 * kv + NCMP], ring[:, CMP0 + kv, l * P:(l + 1) * P], rhs,
                                             start=(l == 0), stop=(l == CMP_BLOCK - 1))
                        last.then_inc(S["hidden_done"], 1)
                if c == 4:
                    pe.wait_ge(S["small_landed"], 16 * N_SMALL)
                    pe.wait_ge(S["gelu_done"], 2)
                    pe.matmul(bank[7][0:NC, 0:P], hg[:, 0, 0, :], w2[:, 0, :], start=True, stop=True)
                    pe.matmul(bank[7][:, P:2 * P], hg[:, 1, :, :].rearrange("p g n -> p (g n)"), w2[:, 1, :],
                              start=True, stop=True).then_inc(S["cmp_kv_done"], 1)
            def turn_heads(g):
                if g < 4:
                    pe.wait_ge(S["roped"], 3)
                    pe.wait_ge(S["proj_out_dve"], 6)
                    pe.wait_ge(S["proj_out_act"], 6)
                else:
                    if g == 4:
                        keep_warm(pe, WARM["forgetting heads"], 4)
                    pe.wait_ge(S["fox_normed"], 1)
                    pe.wait_ge(S["heads_out_dve" if g % 2 else "heads_out_act"], (g - 4) // 2 + 1)
                for i in range(2):
                    m = 2 * g + i
                    for t in range(TT):
                        if m < 4:
                            src = normed[:, t, 2 * m:2 * m + 2, :].rearrange("p a d -> p (a d)")
                        elif m < 8:
                            src = kdup[:, t, m - 4, :, :].rearrange("p a d -> p (a d)")
                        else:
                            src = normed[:, t, 2 * m - 4:2 * m - 2, :].rearrange("p a d -> p (a d)")
                        last = pe.transpose(bank[g % 4][:, i * T + t * P:i * T + (t + 1) * P], src, ident)
                last.then_inc(S["heads_turned"], 1)
            for g in range(4):
                turn_heads(g)
            keep_warm(pe, WARM["compressed keys"], 4)
            pe.wait_ge(S["kc_ready"], 1)
            for hk in range(NKV):
                last = pe.transpose(bank[5][:, hk * NC:(hk + 1) * NC],
                                    kcn[:, hk, :, :].rearrange("n a d -> n (a d)"), ident[0:NC, 0:NC])
            last.then_inc(S["kc_turned"], 1)
            pe.wait_ge(S["logf_ready"], 1)
            upto = table("upto")
            pe.matmul(bank[6][:, 0:NH], upto, logf[:, 0, :], start=True, stop=True)
            pe.matmul(bank[6][:, NH:2 * NH], ones, logf[:, 0, :], start=True, stop=False)
            pe.matmul(bank[6][:, NH:2 * NH], upto, logf[:, 1, :], start=False, stop=True)
            pe.matmul(bank[6][0:NH, 256:384], logf[:, 0, :], upto, start=True, stop=True)
            pe.matmul(bank[6][0:NH, 384:512], logf[:, 0, :], ones, start=True, stop=False)
            pe.matmul(bank[6][0:NH, 384:512], logf[:, 1, :], upto, start=False, stop=True).then_inc(S["cum_done"], 1)
            for g in range(4, 8):
                turn_heads(g)
            pe.wait_ge(S["heads_out_act"], 4)
            pe.wait_ge(S["heads_out_dve"], 4)
            pe.wait_ge(S["kcT_ready"], 1)
            pe.wait_ge(S["cum_ready"], 2)
            for par in range(2):
                rows = slice(par * HD, (par + 1) * HD)
                for t in range(TT):
                    for i in range(GROUP):
                        h = 2 * i + par
                        last = pe.matmul(bank[6 + par][:, (t * GROUP + i) * NC:(t * GROUP + i + 1) * NC],
                                         headT[rows, h // 2, t * P:(t + 1) * P], kcT[rows, h // GROUP, :],
                                         start=True, stop=True)
            last.then_inc(S["cmp_scored"], 1)

            def score(u):
                b, h, q, k, _ = unit(u)
                rows = slice((h % 2) * HD, (h % 2 + 1) * HD)
                if u >= 2:
                    pe.wait_ge(S["masked"], TT * (u - 1))
                    pe.wait_ge(S["cum_ready"], 2 + min(u - 1, 2 * NH))
                for t, (c0, n) in enumerate(((0, P), (P, 2 * P))):
                    last = pe.matmul(bank[u % 2][:, c0:c0 + n], headT[rows, q, t * P:(t + 1) * P],
                                     headT[rows, k, 0:n], start=True, stop=True)
                if u < 2 * NH:
                    hf, m = divmod(u, 2)
                    last = pe.matmul(bank[u % 2][:, 3 * P:], spread(hf)[0:NH], cumk[0:NH, m * P:(m + 1) * P],
                                     start=True, stop=True)
                last.then_inc(S["scored"], 1)

            def turn(u):
                if u >= 2:
                    pe.wait_ge(S["probsT_ready"], u - 1)
                keep_warm(pe, 16 if u < 4 else 2, 2 + u % 2)
                pe.wait_ge(S["probs_ready"], TT * (u + 1))
                for m in range(3):
                    last = pe.transpose(bank[2 + u % 2][:, m * P:(m + 1) * P], probs[:, u % 2, m * P:(m + 1) * P],
                                        ident)
                last.then_inc(S["probs_turned"], 1)

            def attend(u):
                b, h, _, _, v0 = unit(u)
                if h == 0 and b:
                    pe.wait_ge(S["mix_read"], b)
                pe.wait_ge(S["probsT_ready"], u + 1)
                o0 = 4 + 2 * (b % 2)
                pe.matmul(bank[o0][:, h * HD:(h + 1) * HD], probsT[:, u % 2, 0:P], proj[:, 0, v0:v0 + HD],
                          start=True, stop=True)
                for t in range(TT):
                    last = pe.matmul(bank[o0 + 1][:, h * HD:(h + 1) * HD], probsT[:, u % 2, (t + 1) * P:(t + 2) * P],
                                     proj[:, t, v0:v0 + HD], start=(t == 0), stop=(t == 1))
                last.then_inc(S["unit_out"], 1)

            keep_warm(pe, 24, 4)
            for i in range(UNITS + 3):
                if i < UNITS:
                    score(i)
                if 2 <= i <= UNITS + 1:
                    turn(i - 2)
                if i >= 3:
                    attend(i - 3)
                if i == 2:
                    pe.wait_ge(S["cmp_probs"], 1)
                    for t in range(TT):
                        for hk in range(NKV):
                            last = pe.transpose(bank[7][:, (t * 2 + hk) * P:(t * 2 + hk + 1) * P],
                                                cmp_s[:, hk, t, :, :].rearrange("p h n -> p (h n)"), ident)
                    last.then_inc(S["cmp_turned"], 1)
                if i == 6:
                    pe.wait_ge(S["cmp_pT_ready"], 1)
                    for t in range(TT):
                        for hk in range(NKV):
                            last = pe.matmul(bank[6 + t][:, hk * 256:(hk + 1) * 256],
                                             cmp_pT[:, (t * 2 + hk) * P:(t * 2 + hk + 1) * P],
                                             vblock[:, hk, :, :].rearrange("p g d -> p (g d)"), start=True, stop=True)
                    last.then_inc(S["cmp_out"], 1)
            out_product(pe, mixed, OUT0, 0)
            norm_pe(pe, 0, "ffn")
            moe_pe(pe, 0)
            if LAYERS > 1:
                norm_pe(pe, 1, "mix")
                gdn_pe(pe)
                norm_pe(pe, 1, "ffn")
                moe_pe(pe, 1)

        @block.vector
        def _(eng):
            chain = Chain(eng, S["dve_chain"])
            eng.memset(hx[:], 0.0).then_inc(S["hx_zeroed"], 1)
            eng.wait_ge(S["small_turned"], 1)
            eng.tensor_copy(peT[:].rearrange("p a l -> p (a l)"), bank[4][:, 64:128]).then_inc(S["rows_turned_out"], 1)
            eng.tensor_copy(gainT[:], bank[4][:, 0:32]).then_inc(S["rows_turned_out"], 1)
            eng.wait_ge(S["rows_turned_out"], 2)
            norm_dve(eng, chain, 0, "mix")

            def project_out(c):
                c0, w = chunks0[c]
                j = 2 * c + 1
                eng.wait_ge(S["proj_done"], j + 1)
                if c0 == 1024:
                    eng.tensor_copy(proj[:, 1, FORGET0:FORGET0 + 8], bank[j % 4][:, 280:288]).then_inc(
                        S["forget_out"], 1)
                eng.tensor_copy(proj[:, 1, c0:c0 + w], bank[j % 4][:, 0:w]).then_inc(S["proj_out_dve"], 1)

            def head_scales(n):
                view = squares[:, :, 0:n * HD].rearrange("p t (h d) -> p t h d", d=HD)
                sums_ = ss[:, 0:TT * n].rearrange("p (t h) -> p t h", t=TT)
                ins = eng.tensor_reduce(sums_, view, AX.X, ALU.add)
                chain(ins)
                root_argument(eng, rstd[:, 0:TT * n], ss[:, 0:TT * n], 1.0 / HD)
                eng.wait_ge(S["root_ready"], ROOTS.index(f"heads{n}") + 1)
                return rstd[:, 0:TT * n].rearrange("p (t h) -> p t h", t=TT)

            def by_heads(c0, n):
                return proj[:, :, c0:c0 + n * HD].rearrange("p t (h d) -> p t h d", d=HD)

            def scale_heads(r, groups):
                for c0, h0, n, g in groups:
                    o = normed[:, :, h0:h0 + n, :]
                    r0 = h0 if h0 < 12 else h0 - 12
                    chain(eng.tensor_tensor(o, by_heads(c0, n),
                                            r[:, :, r0:r0 + n].unsqueeze(3).to_broadcast([P, TT, n, HD]), ALU.mult))
                    chain(eng.tensor_tensor(o, o, head_gain[:, g, :].unsqueeze(1).unsqueeze(1).to_broadcast(
                        [P, TT, n, HD]), ALU.mult))

            for c in range(3):
                project_out(c)
                if c == 1:
                    eng.wait_ge(S["raw_turned"], 1)
                    for kv in range(2):
                        for half in range(2):
                            eng.tensor_tensor(
                                pe_in[:, kv, half, :].rearrange("p (n r) -> p n r", r=CMP_STRIDE),
                                bank[5][:, kv * T:(kv + 1) * T].rearrange("p (n r) -> p n r", r=CMP_STRIDE),
                                peT[:, kv, half * 16:half * 16 + 16].unsqueeze(1).to_broadcast([P, 16, 16]),
                                ALU.add).then_inc(S["pe_added"], 1)
            eng.wait_ge(S["small_landed"], 16 * N_SMALL)
            eng.wait_ge(S["squared_nsa"], 3)
            r = head_scales(12)
            scale_heads(r, [(0, 0, 8, 0), (768, 8, 2, 2), (1024, 10, 2, 3)])
            project_out(3)
            half = HD // 2
            cos = table("cos").rearrange("p (t d) -> p t d", t=TT)
            sin = table("sin").rearrange("p (t d) -> p t d", t=TT)
            rot, _ = cut(0, TT, 12, HD)
            q = normed[:, :, 0:12, :]
            chain(eng.tensor_tensor(rot[:, :, :, 0:half], q[:, :, :, half:HD],
                                    sin[:, :, 0:half].unsqueeze(2).to_broadcast([P, TT, 12, half]), ALU.mult))
            chain(eng.tensor_tensor(rot[:, :, :, half:HD], q[:, :, :, 0:half],
                                    sin[:, :, half:HD].unsqueeze(2).to_broadcast([P, TT, 12, half]), ALU.mult))
            chain(eng.tensor_tensor(q, q, cos.unsqueeze(2).to_broadcast([P, TT, 12, HD]), ALU.mult))
            eng.tensor_tensor(normed[:, :, 0:8, :], normed[:, :, 0:8, :], rot[:, :, 0:8, :], ALU.add).then_inc(
                S["roped"], 1)
            for d in range(2):
                eng.tensor_tensor(kdup[:, :, :, d, :], normed[:, :, 8:12, :], rot[:, :, 8:12, :], ALU.add).then_inc(
                    S["roped"], 1)
            eng.wait_ge(S["roped"], 3)
            eng.tensor_copy(rs[:, 7, 0:1], rstd[:, 0:1]).then_inc(S["rotated"], 1)
            project_out(4)
            eng.wait_ge(S["hidden_done"], 2)
            eng.wait_ge(S["hx_zeroed"], 1)
            chain(eng.tensor_copy(hx[:, :, 0:NCMP],
                                  bank[6][:, 0:64].rearrange("p (a n) -> p a n", a=2)[:, :, 0:NCMP]))
            chain(eng.tensor_tensor(hu[:], hx[:], hx[:], ALU.mult))
            chain(eng.tensor_scalar(hu[:], hu[:], 0.044715, 1.0, ALU.mult, ALU.add))
            eng.tensor_tensor(hu[:], hu[:], hx[:], ALU.mult).then_inc(S["gelu_arg"], 1)
            eng.wait_ge(S["gelu_exp"], 1)
            chain(eng.tensor_scalar(hu[:], hu[:], 1.0, None, ALU.add))
            chain(eng.reciprocal(hu[:], hu[:]))
            for kv in range(2):
                eng.tensor_tensor(hg[:, kv, :, :], hx[:, kv, :].unsqueeze(1).to_broadcast([P, GROUP, NC]),
                                  hu[:, kv, :].unsqueeze(1).to_broadcast([P, GROUP, NC]), ALU.mult).then_inc(
                                      S["gelu_done"], 1)
            eng.wait_ge(S["forget_out"], 2)
            for c0, n, d0 in ((GATE0, 24, 0), (FORGET0, 8, 24)):
                chain(eng.tensor_tensor(gate[:, :, d0:d0 + n], proj[:, :, c0:c0 + n],
                                        bias_row[:, d0:d0 + n].unsqueeze(1).to_broadcast([P, TT, n]), ALU.add))
            eng.tensor_copy(gate_tmp[:, :, 0:24], gate[:, :, 0:24]).then_inc(S["gate_arg"], 1)
            eng.scalar_tensor_tensor(gate_tmp[:, :, 24:32], gate[:, :, 24:32], -1.0, gate[:, :, 24:32],
                                     ALU.mult, ALU.max).then_inc(S["gate_arg"], 1)
            eng.wait_ge(S["squared_fox"], 1)
            r = head_scales(16)
            scale_heads(r, [(FQ0, 12, 8, 4), (FQ0 + 512, 20, 8, 5)])
            eng.tensor_copy(rs[:, 7, 0:1], rstd[:, 0:1]).then_inc(S["fox_normed"], 1)
            project_out(5)
            eng.wait_ge(S["gate_exp"], 1)
            eng.tensor_scalar(gate_tmp[:], gate_tmp[:], 1.0, None, ALU.add).then_inc(S["gate_plus1"], 1)
            eng.wait_ge(S["gate_plus1"], 1)
            chain(eng.reciprocal(gate[:, :, 0:24], gate_tmp[:, :, 0:24]))
            eng.wait_ge(S["forget_ln"], 1)
            eng.scalar_tensor_tensor(logf[:], gate[:, :, 24:32], 0.0, logf[:], ALU.min, ALU.subtract).then_inc(
                S["logf_ready"], 1)
            eng.wait_ge(S["cmp_kv_done"], 1)
            kc = kct[:, 0, :, :]
            chain(eng.tensor_copy(kc, bank[7][0:NC, 0:P].rearrange("p (h d) -> p h d", h=2)))
            chain(eng.tensor_tensor(vblock[:], bank[7][:, P:2 * P].rearrange("p (h d) -> p h d", h=2).unsqueeze(
                2).to_broadcast([P, 2, GROUP, HD]), table("block_diag").rearrange("p (g d) -> p g d", g=GROUP)
                .unsqueeze(1).to_broadcast([P, 2, GROUP, HD]), ALU.mult))
            chain(eng.tensor_tensor(kct[:, 1, :, :], kc, kc, ALU.mult))
            s_, r_ = ss[0:NC, 60:62], rstd[0:NC, 60:62]
            chain(eng.tensor_reduce(s_, kct[:, 1, :, :], AX.X, ALU.add))
            root_argument(eng, r_, s_, 1.0 / HD)
            eng.wait_ge(S["root_ready"], ROOTS.index("kc") + 1)
            chain(eng.tensor_tensor(kc, kc, r_.unsqueeze(2).to_broadcast([NC, 2, HD]), ALU.mult))
            chain(eng.tensor_tensor(kc, kc, head_gain[0:NC, 1, :].unsqueeze(1).to_broadcast([NC, 2, HD]), ALU.mult))
            ccos, csin = table("cmp_cos", NC), table("cmp_sin", NC)
            chain(eng.tensor_tensor(kct[:, 1, :, 0:half], kc[:, :, half:HD],
                                    csin[:, 0:half].unsqueeze(1).to_broadcast([NC, 2, half]), ALU.mult))
            chain(eng.tensor_tensor(kct[:, 1, :, half:HD], kc[:, :, 0:half],
                                    csin[:, half:HD].unsqueeze(1).to_broadcast([NC, 2, half]), ALU.mult))
            chain(eng.tensor_tensor(kct[:, 2, :, :], kc, ccos.unsqueeze(1).to_broadcast([NC, 2, HD]), ALU.mult))
            for d in range(2):
                last = eng.tensor_tensor(kcn[:, :, d, :], kct[:, 1, :, :], kct[:, 2, :, :], ALU.add)
                if d == 0:
                    chain(last)
            last.then_inc(S["kc_ready"], 1)
            def heads_out(g):
                eng.wait_ge(S["heads_turned"], g + 1)
                eng.tensor_copy(headT[:, 2 * g:2 * g + 2, :].rearrange("p a t -> p (a t)"), bank[g % 4][:]).then_inc(
                    S["heads_out_dve"], 1)

            for g in (1, 3):
                heads_out(g)
            eng.wait_ge(S["kc_turned"], 1)
            eng.tensor_copy(kcT[:].rearrange("p a n -> p (a n)"), bank[5][:, 0:2 * NC]).then_inc(S["kcT_ready"], 1)
            for g in (5, 7):
                heads_out(g)
            eng.wait_ge(S["cum_done"], 1)
            eng.tensor_scalar(cumk[0:NH, :], bank[6][0:NH, 256:512], -8.0, None, ALU.mult).then_inc(S["cum_ready"], 1)
            eng.tensor_scalar(cumq.rearrange("p t h -> p (t h)"), bank[6][:, 0:TT * NH], 8.0, None,
                              ALU.mult).then_inc(S["cum_ready"], 1)
            eng.wait_ge(S["cmp_scored"], 1)
            bias = table("cmp_bias").rearrange("p (t n) -> p t n", t=TT).unsqueeze(2).to_broadcast([P, TT, GROUP, NC])
            valid = table("cmp_valid").rearrange("p (t n) -> p t n", t=TT).unsqueeze(2).to_broadcast([P, TT, GROUP, NC])
            for par in range(2):
                chain(eng.tensor_tensor(cmp_s[:, par], bank[6 + par][:, 0:256].rearrange(
                    "p (t h n) -> p t h n", t=TT, h=GROUP), bias, ALU.add))
            flat_s = work[:, 0:512].rearrange("p (m n) -> p m n", n=NC)
            flat_e = work[:, 512:1024].rearrange("p (m n) -> p m n", n=NC)
            chain(eng.tensor_reduce(cmp_m[:], flat_s, AX.X, ALU.max))
            eng.tensor_tensor(flat_s, flat_s, cmp_m[:].unsqueeze(2).to_broadcast([P, 16, NC]), ALU.subtract).then_inc(
                S["cmp_shifted"], 1)
            eng.wait_ge(S["cmp_exp"], 1)
            chain(eng.tensor_reduce(cmp_m[:], flat_e, AX.X, ALU.add))
            chain(eng.reciprocal(cmp_r[:], cmp_m[:]))
            for par in range(2):
                chain(eng.tensor_tensor(cmp_e[:, par], cmp_e[:, par], valid, ALU.mult))
            r16 = cmp_r[:].rearrange("p (a t h) -> p a t h", a=2, t=TT)
            for par in range(2):
                for hk in range(NKV):
                    last = eng.tensor_tensor(
                        cmp_s[:, hk, :, par:GROUP:2, :], cmp_e[:, par, :, 2 * hk:2 * hk + 2, :],
                        r16[:, par, :, 2 * hk:2 * hk + 2].unsqueeze(3).to_broadcast([P, TT, 2, NC]), ALU.mult)
                    if (par, hk) != (1, 1):
                        chain(last)
            last.then_inc(S["cmp_probs"], 1)

            causal = table("causal")

            def mask(u):
                eng.wait_ge(S["scored"], u + 1)
                if u >= 2:
                    eng.wait_ge(S["probs_ready"], TT * (u - 1))
                for t, (c0, c1, m0) in enumerate(((0, P, P), (P, 3 * P, 0))):
                    bias = causal[:, m0:2 * P] if u < 2 * NH else forget_bias[u - 2 * NH][t]
                    eng.tensor_tensor_reduce(negs[:, u % 2, c0:c1], bank[u % 2][:, c0:c1], bias,
                                             -SCALE, BIG, ALU.add, ALU.min,
                                             neg_max[:, u, t:t + 1]).then_inc(S["masked"], 1)

            forget_bias = []
            for h in range(NH):
                wide_at = (1, FQ0 + 2 * P * h) if h < 4 else (h % 2, 2 * P * ((h - 4) // 2))
                forget_bias.append((proj[:, 0, FQ0 + P * h:FQ0 + P * (h + 1)],
                                    proj[:, wide_at[0], wide_at[1]:wide_at[1] + 2 * P]))

            def bias_part(u):
                h, m = divmod(u, 2)
                src = bank[u % 2][:, 3 * P:]
                if m == 0:
                    chain(eng.scalar_tensor_tensor(forget_bias[h][0], src, cumq[:, 0, h:h + 1], causal[:, P:2 * P],
                                                   ALU.add, ALU.add))
                eng.scalar_tensor_tensor(forget_bias[h][1][:, m * P:(m + 1) * P], src, cumq[:, 1, h:h + 1],
                                         causal[:, m * P:(m + 1) * P], ALU.add, ALU.add).then_inc(S["cum_ready"], 1)

            def mix(b):
                u0 = b * NH
                eng.wait_ge(S["unit_out"], u0 + NH)
                f = factor[:, u0:u0 + NH, :]
                chain(eng.reciprocal(f, sums[:, u0:u0 + NH, :]))
                o0 = 4 + 2 * (b % 2)
                if b < 2:
                    g = gate[:, :, 0:24].rearrange("p t (h c) -> p t h c", c=3)[:, :, :, b + 1].rearrange(
                        "p t h -> p h t")
                    chain(eng.tensor_tensor(f, f, g, ALU.mult))
                for t in range(TT):
                    src = bank[o0 + t][:].rearrange("p (h d) -> p h d", d=HD)
                    fb = f[:, :, t].unsqueeze(2).to_broadcast([P, NH, HD])
                    if b < 2:
                        chain(eng.tensor_tensor(mix_tmp.rearrange("p (h d) -> p h d", d=HD), src, fb, ALU.mult))
                        if t == 1:
                            eng.tensor_copy(rs[:, 7, 0:1], rstd[:, 0:1]).then_inc(S["mix_read"], 1)
                        ins = eng.tensor_tensor(mixed[:, t, 0:512], mixed[:, t, 0:512], mix_tmp, ALU.add)
                        if b == 1:
                            ins.then_inc(S["mixed_ready"], 1)
                            eng.wait_ge(S["mixed_ready"], t + 1)
                        else:
                            chain(ins)
                    else:
                        eng.tensor_tensor(mixed[:, t, 512:1024].rearrange("p (h d) -> p h d", d=HD), src, fb,
                                          ALU.mult).then_inc(S["mixed_ready"], 1)

            for u in range(UNITS):
                if u == 2 * NH:
                    eng.wait_ge(S["cum_ready"], 2 + 2 * NH)
                mask(u)
                if u < 2 * NH:
                    bias_part(u)
                if u == 8:
                    eng.wait_ge(S["cmp_out"], 1)
                    for t in range(TT):
                        g = gate[:, t, 0:24].rearrange("p (h c) -> p h c", c=3)[:, :, 0]
                        chain(eng.tensor_tensor(mixed[:, t, 0:512].rearrange("p (h d) -> p h d", d=HD),
                                                bank[6 + t][:].rearrange("p (h d) -> p h d", d=HD),
                                                g.unsqueeze(2).to_broadcast([P, NH, HD]), ALU.mult))
                    eng.tensor_copy(rs[:, 7, 0:1], rstd[:, 0:1]).then_inc(S["mix_read"], 1)
                if u == 11:
                    mix(0)
                if u == 19:
                    mix(1)
            mix(2)
            turn_out_dve(eng, 0)
            add_product(eng, 0)
            norm_dve(eng, chain, 0, "ffn")
            moe_dve(eng, chain, 0)
            if LAYERS > 1:
                norm_dve(eng, chain, 1, "mix")
                gdn_dve(eng, chain)
                norm_dve(eng, chain, 1, "ffn")
                moe_dve(eng, chain, 1)


INPUTS = ["x", "norm_mix", "norm_ffn", "w_in_even", "b_nsa_gate", "b_forget", "cmp_pe", "cmp_w1", "cmp_w2",
          "nsa_qk_gain", "fox_qk_gain", "w_out_even", "w_in_odd", "conv_w", "a_log", "dt_bias", "gdn_norm_gain",
          "w_out_odd", "w_router_group", "b_router_group", "w_router_expert", "b_router_expert",
          "w_expert_in", "w_expert_out"]


def program(nc, arrays, debug=()):
    a = {n: nc.dram_tensor(f"in_{n}", v.shape, F32, kind="ExternalInput").ap() for n, v in arrays.items()}
    out = nc.dram_tensor("out", (1, T, D), F32, kind="ExternalOutput").ap()
    build(nc, a, out)


def kernel(**inputs):
    from concourse.bacc import Bacc
    from concourse.bass_utils import run_bass_kernel_spmd

    arrays = {n: np.ascontiguousarray(inputs[n]) for n in INPUTS}
    arrays["tables"] = np.concatenate(list(constant_tables().values()), 1)
    nc = Bacc("TRN2", target_bir_lowering=False, num_devices=1)
    program(nc, arrays)
    r = run_bass_kernel_spmd(nc, [{f"in_{n}": v for n, v in arrays.items()}], core_ids=[0])
    return r.results[0]["out"]
```
